# Optimizing a Trainium2 kernel written in Bass

```python
import math
import jax, jax.numpy as jnp
from jax import lax
import numpy as np

D_MODEL = 1024
BATCH = 1
SEQ = 512
DEPTH = 1

D_MIX = D_MODEL
N_MIXERS = 4
GROUP_W = D_MIX // N_MIXERS
CONF_KERNEL = 31
CONF_GROUPS = 4
GN_EPS = 1e-5
SCONV_KERNEL = 3
ATT_HEADS = 4
HEAD_DIM = GROUP_W // ATT_HEADS
MOBA_BLOCK = 256
MOBA_TOP_K = 3
Q_BLOCK = 128
LRU_BLOCKS = 4
LRU_BLOCK_W = GROUP_W // LRU_BLOCKS
LRU_CONV = 4
LRU_C = 8.0
D_FF = 4 * D_MODEL
RMS_EPS = 1e-6
CONF_COLS = 2 * GROUP_W
SC_COLS = 3 * GROUP_W
ATT_COLS = 3 * GROUP_W
LRU_COLS = 2 * GROUP_W
IN_COLS = CONF_COLS + SC_COLS + ATT_COLS + LRU_COLS


def rms_norm(x, g):
    xf = x.astype(jnp.float32)
    y = xf * lax.rsqrt(jnp.mean(xf * xf, axis=-1, keepdims=True) + RMS_EPS)
    return (y * g.astype(jnp.float32)).astype(x.dtype)

def causal_depthwise_conv(x, w):
    k_w, c = w.shape
    return lax.conv_general_dilated(
        x, w[:, None, :].astype(x.dtype), window_strides=(1,), padding=[(k_w - 1, 0)],
        dimension_numbers=("NWC", "WIO", "NWC"), feature_group_count=c)

def group_norm_channels(x, g, b):
    bsz, s, c = x.shape
    xf = x.astype(jnp.float32).reshape(bsz, s, CONF_GROUPS, c // CONF_GROUPS)
    mu = jnp.mean(xf, axis=-1, keepdims=True)
    var = jnp.mean(jnp.square(xf - mu), axis=-1, keepdims=True)
    y = ((xf - mu) * lax.rsqrt(var + GN_EPS)).reshape(bsz, s, c)
    return (y * g.astype(jnp.float32) + b.astype(jnp.float32)).astype(x.dtype)

def conformer_conv_mixer(u, dw_w, dw_b, gn_g, gn_b):
    val, gate = jnp.split(u, 2, axis=-1)
    z = val * jax.nn.sigmoid(gate)
    z = causal_depthwise_conv(z, dw_w) + dw_b
    z = group_norm_channels(z, gn_g, gn_b)
    return jax.nn.silu(z)

def short_conv_mixer(u, conv_w):
    b_gate, c_gate, xs = jnp.split(u, 3, axis=-1)
    return b_gate * causal_depthwise_conv(c_gate * xs, conv_w)

def block_diag(x, w, b):
    bsz, s, c = x.shape
    xg = x.reshape(bsz, s, LRU_BLOCKS, LRU_BLOCK_W)
    return jnp.einsum("bsgi,gij->bsgj", xg, w).reshape(bsz, s, c) + b

def rglru_mixer(u, conv_w, conv_b, wa, ba, wx, bx, lam):
    xr, gate = jnp.split(u, 2, axis=-1)
    xc = causal_depthwise_conv(xr, conv_w) + conv_b
    r = jax.nn.sigmoid(block_diag(xc, wa, ba).astype(jnp.float32))
    i = jax.nn.sigmoid(block_diag(xc, wx, bx).astype(jnp.float32))
    log_a = -LRU_C * r * jax.nn.softplus(-lam.astype(jnp.float32))
    a = jnp.exp(log_a)
    mult = jnp.sqrt(-jnp.expm1(2.0 * log_a))
    bterm = mult * (i * xc.astype(jnp.float32))

    def combine(e1, e2):
        a1, b1 = e1
        a2, b2 = e2
        return a1 * a2, a2 * b1 + b2

    _, h = lax.associative_scan(combine, (a, bterm), axis=1)
    return (h * jax.nn.gelu(gate.astype(jnp.float32))).astype(u.dtype)

def moba_attention(u):
    bsz, s, _ = u.shape
    q, k, v = jnp.split(u.astype(jnp.float32), 3, axis=-1)
    q = q.reshape(bsz, s, ATT_HEADS, HEAD_DIM).transpose(0, 2, 1, 3) * (HEAD_DIM ** -0.5)
    k = k.reshape(bsz, s, ATT_HEADS, HEAD_DIM)
    v = v.reshape(bsz, s, ATT_HEADS, HEAD_DIM)
    nb = -(-s // MOBA_BLOCK)
    pad = nb * MOBA_BLOCK - s
    kp = jnp.pad(k, ((0, 0), (0, pad), (0, 0), (0, 0)))
    vp = jnp.pad(v, ((0, 0), (0, pad), (0, 0), (0, 0)))
    kb = kp.reshape(bsz, nb, MOBA_BLOCK, ATT_HEADS, HEAD_DIM).transpose(0, 3, 1, 2, 4)
    vb = vp.reshape(bsz, nb, MOBA_BLOCK, ATT_HEADS, HEAD_DIM).transpose(0, 3, 1, 2, 4)
    slopes = 2.0 ** (-8.0 * jnp.arange(1, ATT_HEADS + 1, dtype=jnp.float32) / ATT_HEADS)

    kmean = jnp.mean(kb, axis=3)
    gate = jnp.einsum("bhsd,bhnd->bhsn", q, kmean)
    q_blk = jnp.arange(s) // MOBA_BLOCK
    past = jnp.arange(nb)[None, :] < q_blk[:, None]
    gate = jnp.where(past, gate, -jnp.inf)
    topk = max(min(MOBA_TOP_K, nb - 1), 1)
    _, idx = lax.top_k(gate, topk)

    nq = s // Q_BLOCK
    q_c = q.reshape(bsz, ATT_HEADS, nq, Q_BLOCK, HEAD_DIM).transpose(0, 2, 1, 3, 4)
    q_c = q_c.reshape(bsz * nq, ATT_HEADS, Q_BLOCK, HEAD_DIM)
    i_c = idx.reshape(bsz, ATT_HEADS, nq, Q_BLOCK, topk).transpose(0, 2, 1, 3, 4)
    i_c = i_c.reshape(bsz * nq, ATT_HEADS, Q_BLOCK, topk)
    b_ids = jnp.repeat(jnp.arange(bsz), nq)
    n_ids = jnp.tile(jnp.arange(nq), bsz)
    hh = jnp.arange(ATT_HEADS)[:, None, None]
    offs = jnp.arange(MOBA_BLOCK)

    def one_block(args):
        qc, ic, b, n = args
        kbb = kb[b]
        vbb = vb[b]
        t = n * Q_BLOCK + jnp.arange(Q_BLOCK)
        own = (n * Q_BLOCK) // MOBA_BLOCK
        k_own = kbb[:, own]
        v_own = vbb[:, own]
        s_pos = own * MOBA_BLOCK + offs
        d_own = (t[:, None] - s_pos[None, :]).astype(jnp.float32)
        s_own = jnp.einsum("hqd,hkd->hqk", qc, k_own) - slopes[:, None, None] * d_own
        s_own = jnp.where(d_own >= 0, s_own, -jnp.inf)
        kg = kbb[hh, ic]
        vg = vbb[hh, ic]
        sel_pos = ic[..., None] * MOBA_BLOCK + offs
        d_sel = (t[None, :, None, None] - sel_pos).astype(jnp.float32)
        s_sel = jnp.einsum("hqd,hqjkd->hqjk", qc, kg) - slopes[:, None, None, None] * d_sel
        s_sel = jnp.where((ic < own)[..., None], s_sel, -jnp.inf)
        scores = jnp.concatenate([s_sel.reshape(ATT_HEADS, Q_BLOCK, topk * MOBA_BLOCK), s_own], axis=-1)
        p = jax.nn.softmax(scores, axis=-1)
        p_sel = p[..., : topk * MOBA_BLOCK].reshape(ATT_HEADS, Q_BLOCK, topk, MOBA_BLOCK)
        p_own = p[..., topk * MOBA_BLOCK:]
        return (jnp.einsum("hqjk,hqjkd->hqd", p_sel, vg)
                + jnp.einsum("hqk,hkd->hqd", p_own, v_own))

    out = lax.map(one_block, (q_c, i_c, b_ids, n_ids))
    out = out.reshape(bsz, nq, ATT_HEADS, Q_BLOCK, HEAD_DIM).transpose(0, 1, 3, 2, 4)
    return out.reshape(bsz, s, GROUP_W).astype(u.dtype)

def first_inputs(seed: int = 0) -> dict:
    key = jax.random.key(seed)
    ks = jax.random.split(key, 24)
    f32 = jnp.float32

    def nrm(k, shape, scale):
        return jax.random.normal(k, shape, f32) * scale

    def gain(k, shape):
        return 1.0 + 0.05 * jax.random.normal(k, shape, f32)

    u = jax.random.uniform(ks[20], (DEPTH, GROUP_W), f32, 0.9, 0.999)
    base = u ** (1.0 / LRU_C)
    lru_lam = jnp.log(base) - jnp.log1p(-base)
    return {
        "x": jax.random.normal(ks[0], (BATCH, SEQ, D_MODEL), f32),
        "pre_mix_g": gain(ks[1], (DEPTH, D_MODEL)),
        "w_in": nrm(ks[2], (DEPTH, D_MODEL, IN_COLS), D_MODEL ** -0.5),
        "conf_dw_w": nrm(ks[3], (DEPTH, CONF_KERNEL, GROUP_W), CONF_KERNEL ** -0.5),
        "conf_dw_b": nrm(ks[4], (DEPTH, GROUP_W), 0.02),
        "conf_gn_g": gain(ks[5], (DEPTH, GROUP_W)),
        "conf_gn_b": nrm(ks[6], (DEPTH, GROUP_W), 0.02),
        "sconv_w": nrm(ks[7], (DEPTH, SCONV_KERNEL, GROUP_W), SCONV_KERNEL ** -0.5),
        "lru_conv_w": nrm(ks[8], (DEPTH, LRU_CONV, GROUP_W), LRU_CONV ** -0.5),
        "lru_conv_b": nrm(ks[9], (DEPTH, GROUP_W), 0.02),
        "lru_wa": nrm(ks[10], (DEPTH, LRU_BLOCKS, LRU_BLOCK_W, LRU_BLOCK_W), LRU_BLOCK_W ** -0.5),
        "lru_ba": nrm(ks[11], (DEPTH, GROUP_W), 0.02),
        "lru_wx": nrm(ks[12], (DEPTH, LRU_BLOCKS, LRU_BLOCK_W, LRU_BLOCK_W), LRU_BLOCK_W ** -0.5),
        "lru_bx": nrm(ks[13], (DEPTH, GROUP_W), 0.02),
        "lru_lam": lru_lam,
        "w_out": nrm(ks[14], (DEPTH, D_MIX, D_MODEL), D_MIX ** -0.5),
        "post_mix_g": gain(ks[15], (DEPTH, D_MODEL)),
        "pre_mlp_g": gain(ks[16], (DEPTH, D_MODEL)),
        "mlp_w1": nrm(ks[17], (DEPTH, D_MODEL, D_FF), D_MODEL ** -0.5),
        "mlp_w2": nrm(ks[18], (DEPTH, D_FF, D_MODEL), D_FF ** -0.5),
        "post_mlp_g": gain(ks[19], (DEPTH, D_MODEL)),
    }

def first_block(x, pre_mix_g, w_in, conf_dw_w, conf_dw_b, conf_gn_g, conf_gn_b, sconv_w,
              lru_conv_w, lru_conv_b, lru_wa, lru_ba, lru_wx, lru_bx, lru_lam, w_out,
              post_mix_g, pre_mlp_g, mlp_w1, mlp_w2, post_mlp_g):
    splits = [CONF_COLS, CONF_COLS + SC_COLS, CONF_COLS + SC_COLS + ATT_COLS]
    for l in range(DEPTH):
        h = rms_norm(x, pre_mix_g[l])
        u = h @ w_in[l]
        u_conf, u_sc, u_att, u_lru = jnp.split(u, splits, axis=-1)
        y_a = conformer_conv_mixer(u_conf, conf_dw_w[l], conf_dw_b[l], conf_gn_g[l], conf_gn_b[l])
        y_b = short_conv_mixer(u_sc, sconv_w[l])
        y_c = moba_attention(u_att)
        y_d = rglru_mixer(u_lru, lru_conv_w[l], lru_conv_b[l], lru_wa[l], lru_ba[l],
                          lru_wx[l], lru_bx[l], lru_lam[l])
        y = jnp.concatenate([y_a, y_b, y_c, y_d], axis=-1) @ w_out[l]
        x = x + rms_norm(y, post_mix_g[l])
        h = rms_norm(x, pre_mlp_g[l])
        m = jnp.square(jax.nn.relu(h @ mlp_w1[l])) @ mlp_w2[l]
        x = x + rms_norm(m, post_mlp_g[l])
    return x


N_MIXERS_2 = 3
NORM_EPS = 1e-6

RW_HEAD = 64
RW_HEADS = D_MODEL // RW_HEAD
RW_WIDTH = RW_HEADS * RW_HEAD
RW_DECAY_RANK = 64
RW_AAA_RANK = 64
RW_VRES_RANK = 32
RW_GN_EPS = 64e-5

SSD_EXPAND = 2
SSD_WIDTH = SSD_EXPAND * D_MODEL
SSD_HEAD = 64
SSD_HEADS = SSD_WIDTH // SSD_HEAD
SSD_GROUPS = 8
SSD_STATE = 128
SSD_CONV = 4
SSD_CHUNK = 128
SSD_CONV_DIM = SSD_WIDTH + 2 * SSD_GROUPS * SSD_STATE

SB_HEAD = 64
SB_HEADS = D_MODEL // SB_HEAD
SB_WIDTH = SB_HEADS * SB_HEAD
SB_BLOCK = 128
SB_SCALE = 1.0 / math.sqrt(SB_HEAD)


def rms_norm_2(u, g, eps=NORM_EPS):
    u32 = u.astype(jnp.float32)
    y = u32 * lax.rsqrt(jnp.mean(u32 * u32, axis=-1, keepdims=True) + eps)
    return (y * g.astype(jnp.float32)).astype(u.dtype)

def token_shift(h):
    return jnp.pad(h, ((0, 0), (1, 0), (0, 0)))[:, :-1]

def rwkv7_mixer(h, p, v_first):
    mu, w_in, w_up, w0, a_up, a0, k_k, k_a, r_k, gn_w, gn_b, w_out = p[:12]
    Bsz, T, _ = h.shape
    W, H, N = RW_WIDTH, RW_HEADS, RW_HEAD
    dx = token_shift(h) - h
    x_r, x_w, x_k, x_v, x_a, x_g = (h + dx * mu[i] for i in range(6))
    c = np.cumsum([0, W, W, W, W, RW_DECAY_RANK, RW_AAA_RANK])
    r = x_r @ w_in[:, c[0]:c[1]]
    k = x_k @ w_in[:, c[1]:c[2]]
    v = x_v @ w_in[:, c[2]:c[3]]
    g = jax.nn.silu(x_g @ w_in[:, c[3]:c[4]])
    w_lo = jnp.tanh(x_w @ w_in[:, c[4]:c[5]])
    a_lo = x_a @ w_in[:, c[5]:c[6]]
    f32 = jnp.float32
    w_raw = (w0 + w_lo @ w_up).astype(f32)
    log_decay = -jnp.exp(-jax.nn.softplus(-w_raw) - 0.5)
    a = jax.nn.sigmoid((a0 + a_lo @ a_up).astype(f32))
    if v_first is None:
        v_first = v
    else:
        v_up, v0 = p[12:]
        v_lo = x_v @ w_in[:, c[6]:]
        v = v + (v_first - v) * jax.nn.sigmoid(v0 + v_lo @ v_up)

    def heads(t):
        return t.astype(f32).reshape(Bsz, T, H, N)

    kk = heads(k * k_k)
    kk = kk / jnp.maximum(jnp.sqrt(jnp.sum(kk * kk, axis=-1, keepdims=True)), 1e-12)
    k = k.astype(f32) * (1.0 + (a - 1.0) * k_a.astype(f32))
    r_h, k_h, v_h, a_h = heads(r), heads(k), heads(v), heads(a)
    decay_h = jnp.exp(heads(log_decay))

    def step(S, inp):
        r_t, w_t, k_t, v_t, kk_t, a_t = inp
        sa = jnp.einsum('bhvk,bhk->bhv', S, -kk_t)
        S = (S * w_t[:, :, None, :]
             + sa[..., None] * (kk_t * a_t)[:, :, None, :]
             + v_t[..., None] * k_t[:, :, None, :])
        y_t = jnp.einsum('bhvk,bhk->bhv', S, r_t)
        return S, y_t

    tm = lambda t: jnp.moveaxis(t, 1, 0)
    S0 = jnp.zeros((Bsz, H, N, N), f32)
    _, y = lax.scan(step, S0, (tm(r_h), tm(decay_h), tm(k_h), tm(v_h), tm(kk), tm(a_h)))
    y = jnp.moveaxis(y, 0, 1)
    mean = jnp.mean(y, axis=-1, keepdims=True)
    var = jnp.mean(jnp.square(y - mean), axis=-1, keepdims=True)
    y = (y - mean) * lax.rsqrt(var + RW_GN_EPS)
    y = y * gn_w.astype(f32).reshape(H, N) + gn_b.astype(f32).reshape(H, N)
    y = y + jnp.sum(r_h * k_h * r_k.astype(f32), axis=-1, keepdims=True) * v_h
    y = y.reshape(Bsz, T, W).astype(h.dtype) * g
    return y @ w_out, v_first

def causal_depthwise_conv_2(u, w, b):
    out = lax.conv_general_dilated(
        u, w[:, None, :].astype(u.dtype), window_strides=(1,),
        padding=[(w.shape[0] - 1, 0)], dimension_numbers=('NWC', 'WIO', 'NWC'),
        feature_group_count=u.shape[-1])
    return out + b

def ssd_chunked(x, a, Bm, Cm):
    Bsz, T, H, P = x.shape
    G, R, l = SSD_GROUPS, H // SSD_GROUPS, SSD_CHUNK
    nc = T // l
    x = x.reshape(Bsz, nc, l, G, R, P)
    Bm = Bm.reshape(Bsz, nc, l, G, SSD_STATE)
    Cm = Cm.reshape(Bsz, nc, l, G, SSD_STATE)
    ac = jnp.cumsum(jnp.moveaxis(a.reshape(Bsz, nc, l, G, R), 2, -1), axis=-1)
    causal = jnp.tril(jnp.ones((l, l), bool))
    seg = ac[..., :, None] - ac[..., None, :]
    decay_in = jnp.exp(jnp.where(causal, seg, -jnp.inf))
    cb = jnp.einsum('bclgn,bcsgn->bcgls', Cm, Bm)
    y_diag = jnp.einsum('bcgrls,bcsgrp->bclgrp', cb[:, :, :, None] * decay_in, x)
    decay_states = jnp.moveaxis(jnp.exp(ac[..., -1:] - ac), -1, 2)
    states = jnp.einsum('bclgn,bclgrp->bcgrpn', Bm, x * decay_states[..., None])
    chunk_decay = ac[..., -1]

    def chunk_step(h_prev, inp):
        st, dec = inp
        return h_prev * jnp.exp(dec)[..., None, None] + st, h_prev

    h0 = jnp.zeros((Bsz, G, R, P, SSD_STATE), x.dtype)
    _, h_in = lax.scan(chunk_step, h0, (jnp.moveaxis(states, 1, 0), jnp.moveaxis(chunk_decay, 1, 0)))
    h_in = jnp.moveaxis(h_in, 0, 1)
    decay_out = jnp.moveaxis(jnp.exp(ac), -1, 2)
    y_off = jnp.einsum('bclgn,bcgrpn->bclgrp', Cm, h_in) * decay_out[..., None]
    return (y_diag + y_off).reshape(Bsz, T, H, P)

def mamba2_mixer(h, p):
    w_in, conv_w, conv_b, dt_bias, a_log, d_skip, gnorm_w, w_out = p
    Bsz, T, _ = h.shape
    f32 = jnp.float32
    proj = h @ w_in
    z = proj[..., :SSD_WIDTH]
    xbc = proj[..., SSD_WIDTH:SSD_WIDTH + SSD_CONV_DIM]
    dt_raw = proj[..., SSD_WIDTH + SSD_CONV_DIM:]
    xbc = jax.nn.silu(causal_depthwise_conv_2(xbc, conv_w, conv_b)).astype(f32)
    gn = SSD_GROUPS * SSD_STATE
    xs = xbc[..., :SSD_WIDTH].reshape(Bsz, T, SSD_HEADS, SSD_HEAD)
    Bm = xbc[..., SSD_WIDTH:SSD_WIDTH + gn].reshape(Bsz, T, SSD_GROUPS, SSD_STATE)
    Cm = xbc[..., SSD_WIDTH + gn:].reshape(Bsz, T, SSD_GROUPS, SSD_STATE)
    dt = jax.nn.softplus((dt_raw + dt_bias).astype(f32))
    A = -jnp.exp(a_log.astype(f32))
    y = ssd_chunked(xs * dt[..., None], dt * A, Bm, Cm)
    y = y + xs * d_skip.astype(f32)[:, None]
    y = y.reshape(Bsz, T, SSD_WIDTH) * jax.nn.silu(z.astype(f32))
    y = y.reshape(Bsz, T, SSD_GROUPS, SSD_WIDTH // SSD_GROUPS)
    y = y * lax.rsqrt(jnp.mean(y * y, axis=-1, keepdims=True) + NORM_EPS)
    y = y.reshape(Bsz, T, SSD_WIDTH) * gnorm_w.astype(f32)
    return y.astype(h.dtype) @ w_out

def stick_breaking_mixer(h, p):
    w_in, q_norm, k_norm, w_out = p
    Bsz, T, _ = h.shape
    f32 = jnp.float32
    proj = h @ w_in
    W = SB_WIDTH
    q = rms_norm_2(proj[..., :W].reshape(Bsz, T, SB_HEADS, SB_HEAD), q_norm).astype(f32)
    k = rms_norm_2(proj[..., W:2 * W].reshape(Bsz, T, SB_HEADS, SB_HEAD), k_norm).astype(f32)
    v = proj[..., 2 * W:3 * W].reshape(Bsz, T, SB_HEADS, SB_HEAD).astype(f32)
    g = jax.nn.silu(proj[..., 3 * W:])
    outs = []
    for blk in range(T // SB_BLOCK):
        start, end = blk * SB_BLOCK, (blk + 1) * SB_BLOCK
        qb, kb, vb = q[:, start:end], k[:, :end], v[:, :end]
        z = jnp.einsum('bthd,bshd->bhts', qb, kb) * SB_SCALE
        t_idx = start + jnp.arange(SB_BLOCK)
        s_idx = jnp.arange(end)
        strict = s_idx[None, :] < t_idx[:, None]
        log_beta = jax.nn.log_sigmoid(z)
        log_1m_beta = jnp.where(strict, log_beta - z, 0.0)
        tail = lax.cumsum(log_1m_beta, axis=3, reverse=True) - log_1m_beta
        att = jnp.where(strict, jnp.exp(log_beta + tail), 0.0)
        outs.append(jnp.einsum('bhts,bshd->bthd', att, vb))
    o = jnp.concatenate(outs, axis=1).reshape(Bsz, T, W).astype(h.dtype)
    return (o * g) @ w_out

def _normal(key, shape, scale):
    return scale * jax.random.normal(key, shape, jnp.float32)

def _rwkv_params(key, prefix, value_residual):
    ks = jax.random.split(key, 16)
    W = RW_WIDTH
    n_cols = 4 * W + RW_DECAY_RANK + RW_AAA_RANK + (RW_VRES_RANK if value_residual else 0)
    p = {
        prefix + "norm": 1.0 + _normal(ks[0], (D_MODEL,), 0.05),
        prefix + "mu": jax.random.uniform(ks[1], (6, D_MODEL), jnp.float32),
        prefix + "w_in": _normal(ks[2], (D_MODEL, n_cols), D_MODEL ** -0.5),
        prefix + "w_up": _normal(ks[3], (RW_DECAY_RANK, W), 0.5 * RW_DECAY_RANK ** -0.5),
        prefix + "w0": jax.random.uniform(ks[4], (W,), jnp.float32, -6.0, 1.0),
        prefix + "a_up": _normal(ks[5], (RW_AAA_RANK, W), 0.5 * RW_AAA_RANK ** -0.5),
        prefix + "a0": _normal(ks[6], (W,), 0.5),
        prefix + "k_k": 0.85 + _normal(ks[7], (W,), 0.05),
        prefix + "k_a": 1.0 + _normal(ks[8], (W,), 0.05),
        prefix + "r_k": _normal(ks[9], (RW_HEADS, RW_HEAD), 0.1),
        prefix + "gn_w": 1.0 + _normal(ks[10], (W,), 0.05),
        prefix + "gn_b": _normal(ks[11], (W,), 0.01),
        prefix + "w_out": _normal(ks[12], (W, D_MODEL), W ** -0.5),
    }
    if value_residual:
        p[prefix + "v_up"] = _normal(ks[13], (RW_VRES_RANK, W), 0.5 * RW_VRES_RANK ** -0.5)
        p[prefix + "v0"] = _normal(ks[14], (W,), 0.5)
    return p

def _mamba2_params(key, prefix):
    ks = jax.random.split(key, 10)
    n_cols = SSD_WIDTH + SSD_CONV_DIM + SSD_HEADS
    dt = jnp.exp(jax.random.uniform(ks[4], (SSD_HEADS,), jnp.float32, math.log(1e-3), math.log(1e-1)))
    return {
        prefix + "norm": 1.0 + _normal(ks[0], (D_MODEL,), 0.05),
        prefix + "w_in": _normal(ks[1], (D_MODEL, n_cols), D_MODEL ** -0.5),
        prefix + "conv_w": _normal(ks[2], (SSD_CONV, SSD_CONV_DIM), SSD_CONV ** -0.5),
        prefix + "conv_b": _normal(ks[3], (SSD_CONV_DIM,), 0.01),
        prefix + "dt_bias": dt + jnp.log(-jnp.expm1(-dt)),
        prefix + "a_log": jnp.log(jax.random.uniform(ks[5], (SSD_HEADS,), jnp.float32, 1.0, 16.0)),
        prefix + "d_skip": 1.0 + _normal(ks[6], (SSD_HEADS,), 0.05),
        prefix + "gnorm_w": 1.0 + _normal(ks[7], (SSD_WIDTH,), 0.05),
        prefix + "w_out": _normal(ks[8], (SSD_WIDTH, D_MODEL), SSD_WIDTH ** -0.5),
    }

def _stickbreak_params(key, prefix):
    ks = jax.random.split(key, 5)
    return {
        prefix + "norm": 1.0 + _normal(ks[0], (D_MODEL,), 0.05),
        prefix + "w_in": _normal(ks[1], (D_MODEL, 4 * SB_WIDTH), D_MODEL ** -0.5),
        prefix + "q_norm": 1.0 + _normal(ks[2], (SB_HEAD,), 0.05),
        prefix + "k_norm": 1.0 + _normal(ks[3], (SB_HEAD,), 0.05),
        prefix + "w_out": _normal(ks[4], (SB_WIDTH, D_MODEL), SB_WIDTH ** -0.5),
    }

def second_inputs(seed: int = 0) -> dict:
    key = jax.random.key(seed)
    kx, k0, k1, k2, k3 = jax.random.split(key, 5)
    inputs = {"x": jax.random.normal(kx, (BATCH, SEQ, D_MODEL), jnp.float32)}
    inputs.update(_rwkv_params(k0, "l0_", value_residual=False))
    inputs.update(_mamba2_params(k1, "l1_"))
    inputs.update(_stickbreak_params(k2, "l2_"))
    inputs.update(_rwkv_params(k3, "l3_", value_residual=True))
    return inputs

def second_block(x,
              l0_norm, l0_mu, l0_w_in, l0_w_up, l0_w0, l0_a_up, l0_a0, l0_k_k, l0_k_a, l0_r_k,
              l0_gn_w, l0_gn_b, l0_w_out,
              l1_norm, l1_w_in, l1_conv_w, l1_conv_b, l1_dt_bias, l1_a_log, l1_d_skip, l1_gnorm_w,
              l1_w_out,
              l2_norm, l2_w_in, l2_q_norm, l2_k_norm, l2_w_out,
              l3_norm, l3_mu, l3_w_in, l3_w_up, l3_w0, l3_a_up, l3_a0, l3_k_k, l3_k_a, l3_r_k,
              l3_gn_w, l3_gn_b, l3_w_out, l3_v_up, l3_v0):
    layer_params = [
        (l0_norm, (l0_mu, l0_w_in, l0_w_up, l0_w0, l0_a_up, l0_a0, l0_k_k, l0_k_a, l0_r_k,
                   l0_gn_w, l0_gn_b, l0_w_out)),
        (l1_norm, (l1_w_in, l1_conv_w, l1_conv_b, l1_dt_bias, l1_a_log, l1_d_skip, l1_gnorm_w,
                   l1_w_out)),
        (l2_norm, (l2_w_in, l2_q_norm, l2_k_norm, l2_w_out)),
        (l3_norm, (l3_mu, l3_w_in, l3_w_up, l3_w0, l3_a_up, l3_a0, l3_k_k, l3_k_a, l3_r_k,
                   l3_gn_w, l3_gn_b, l3_w_out, l3_v_up, l3_v0)),
    ]
    v_first = None
    for i in range(DEPTH):
        norm_g, p = layer_params[i]
        h = rms_norm_2(x, norm_g)
        kind = i % N_MIXERS_2
        if kind == 0:
            y, v_first = rwkv7_mixer(h, p, v_first)
        elif kind == 1:
            y = mamba2_mixer(h, p)
        else:
            y = stick_breaking_mixer(h, p)
        x = x + y.astype(x.dtype)
    return x


def setup_inputs(seed=0):
    out = dict(first_inputs(seed))
    for name, value in second_inputs(seed + 1).items():
        if name != "x":
            out[name + "_2"] = value
    return out


def reference(
    x, pre_mix_g, w_in, conf_dw_w, conf_dw_b, conf_gn_g, conf_gn_b, sconv_w, lru_conv_w,
    lru_conv_b, lru_wa, lru_ba, lru_wx, lru_bx, lru_lam, w_out, post_mix_g, pre_mlp_g, mlp_w1,
    mlp_w2, post_mlp_g, l0_norm_2, l0_mu_2, l0_w_in_2, l0_w_up_2, l0_w0_2, l0_a_up_2, l0_a0_2,
    l0_k_k_2, l0_k_a_2, l0_r_k_2, l0_gn_w_2, l0_gn_b_2, l0_w_out_2, l1_norm_2, l1_w_in_2,
    l1_conv_w_2, l1_conv_b_2, l1_dt_bias_2, l1_a_log_2, l1_d_skip_2, l1_gnorm_w_2, l1_w_out_2,
    l2_norm_2, l2_w_in_2, l2_q_norm_2, l2_k_norm_2, l2_w_out_2, l3_norm_2, l3_mu_2, l3_w_in_2,
    l3_w_up_2, l3_w0_2, l3_a_up_2, l3_a0_2, l3_k_k_2, l3_k_a_2, l3_r_k_2, l3_gn_w_2, l3_gn_b_2,
    l3_w_out_2, l3_v_up_2, l3_v0_2,
):
    x = first_block(
        x, pre_mix_g, w_in, conf_dw_w, conf_dw_b, conf_gn_g, conf_gn_b, sconv_w, lru_conv_w,
        lru_conv_b, lru_wa, lru_ba, lru_wx, lru_bx, lru_lam, w_out, post_mix_g, pre_mlp_g,
        mlp_w1, mlp_w2, post_mlp_g,
    )
    return second_block(
        x, l0_norm_2, l0_mu_2, l0_w_in_2, l0_w_up_2, l0_w0_2, l0_a_up_2, l0_a0_2, l0_k_k_2,
        l0_k_a_2, l0_r_k_2, l0_gn_w_2, l0_gn_b_2, l0_w_out_2, l1_norm_2, l1_w_in_2, l1_conv_w_2,
        l1_conv_b_2, l1_dt_bias_2, l1_a_log_2, l1_d_skip_2, l1_gnorm_w_2, l1_w_out_2, l2_norm_2,
        l2_w_in_2, l2_q_norm_2, l2_k_norm_2, l2_w_out_2, l3_norm_2, l3_mu_2, l3_w_in_2,
        l3_w_up_2, l3_w0_2, l3_a_up_2, l3_a0_2, l3_k_k_2, l3_k_a_2, l3_r_k_2, l3_gn_w_2,
        l3_gn_b_2, l3_w_out_2, l3_v_up_2, l3_v0_2,
    )


_drawn_inputs = setup_inputs


def setup_inputs(seed=0):
    import zlib

    import numpy as np

    out = dict(_drawn_inputs(seed))
    spreads = {}
    factors = {'conf_dw_b': 3.194,
     'conf_gn_b': 6.225,
     'lru_ba': 29.053,
     'lru_bx': 8.0,
     'l0_w_up_2': 5.324,
     'l0_k_k_2': 3.027,
     'l0_k_a_2': 2.677,
     'l0_gn_w_2': 4.28,
     'l0_gn_b_2': 31.467}
    for name, (base, spread) in spreads.items():
        noise = np.random.default_rng([zlib.crc32(name.encode()), seed]).standard_normal(out[name].shape)
        drawn = base * np.exp(spread * noise) if base else spread * noise
        out[name] = __import__('jax').numpy.asarray(drawn.astype(out[name].dtype))
    for name, factor in factors.items():
        out[name] = (out[name] * factor).astype(out[name].dtype)
    return out
```

```python
import math
from contextlib import ExitStack

import numpy as np

import concourse.bass as bass
from concourse import mybir

F32 = mybir.dt.float32
F32R = mybir.dt.float32r
ALU = mybir.AluOpType
ACT = mybir.ActivationFunctionType
AX_X = mybir.AxisListType.X

P = 128
D = 1024
T = 512
KT = D // P
GW = 256
CONF_K, SC_K, LRU_K = 31, 3, 4
ATT_HEADS, HD = 4, 64
DFF = 4096
FG = 4
BT = T // P
RMS_EPS, GN_EPS, RW_GN_EPS = 1e-6, 1e-5, 64e-5
LEVELS = 6

(CV0, CG0, CV1, CG1, Q0, Q1, K0, K1, V0, V1, LX0, LX1, LG0, LG1, SC0, SX0, SC1, SX1, SB0, SB1) = range(20)
W_IN_ORDER = [0, 2, 1, 3, 10, 11, 12, 13, 14, 15, 16, 17, 18, 19, 6, 8, 7, 9, 4, 5]
J_IN, J_OUT = 0, 20
J_MLP = J_OUT + KT
J_RK = J_MLP + FG * 2 * KT
J_RR, J_RV, J_RG, J_RO = (J_RK + KT * n for n in range(1, 5))
JOBS = J_RO + KT
RAW = 4
SLOTS = 2

PARAMS = [("pre_mix_g", 8), ("post_mix_g", 8), ("pre_mlp_g", 8), ("post_mlp_g", 8), ("l0_norm", 8),
          ("mu", 48), ("conf_w", 62), ("conf_b", 2), ("gn_g", 2), ("gn_b", 2), ("sconv_w", 6),
          ("lru_w", 8), ("lru_b", 2), ("lru_ba", 2), ("lru_bx", 2), ("lam", 2), ("rw", 64)]
PCOL, _n = {}, 0
for _name, _w in PARAMS:
    PCOL[_name] = _n
    _n += _w
NPAR = _n
RW_W0, RW_A0, RW_KK, RW_KA, RW_RK, RW_GW, RW_GB, RW_OMK = range(8)

CONSTS = [("ident", 128), ("ones", 128), ("blk", 128), ("mean", 128), ("lower", 128), ("pair", 128),
          ("pairT", 128), ("gram", 512), ("level", 128 * LEVELS), ("reset", BT * 129), ("alibi", 896)]
CCOL, _n = {}, 0
for _name, _w in CONSTS:
    CCOL[_name] = (_n, _w)
    _n += _w
NCONST = _n
CHUNK_CONSTS = CCOL["alibi"][0]

HEADS = [(pair, qt, hh) for pair in range(2) for qt in range(BT) for hh in range(2)]
DECAY = -0.5 * math.exp(-0.5)
STEPS_V = 23


def constants():
    c = np.zeros((P, NCONST), np.float32)

    def put(name, value):
        a, w = CCOL[name]
        c[:, a:a + w] = value
    i, j = np.arange(P)[:, None], np.arange(P)[None, :]
    put("ident", i == j)
    put("ones", 1.0)
    same = (i // 64) == (j // 64)
    put("blk", same)
    put("mean", same / 64.0)
    put("lower", j < i)
    put("pair", (i // 2 == j // 2) & (j < i))
    put("pairT", (i // 2 == j // 2) & (i < j))
    strict, incl = i < j, i <= j
    put("gram", np.concatenate([strict, incl, strict, incl], 1))
    put("level", np.concatenate([((i >> (l + 1)) == (j >> (l + 1))) & ((i >> l) % 2 == 0) & ((j >> l) % 2 == 1)
                                 for l in range(1, LEVELS + 1)], 1))
    r = np.ones((BT, 129))
    r[:, 0] = 0.0
    put("reset", r.reshape(1, -1))
    m = np.arange(896)[None, :] - 384 - i
    put("alibi", np.where(m <= 0, m, -1e30))
    return c


class Steps:

    def __init__(self, engine, sem):
        self.engine, self.sem, self.n, self.shift = engine, sem, 0, 0

    def __call__(self, ins):
        ins.then_inc(self.sem, 1)
        self.n += 1
        self.engine.wait_ge(self.sem, self.n + self.shift)

    def loop(self, i, per):
        self.first, self.per, self.shift = self.n, per, i * per

    def end(self, turns):
        assert self.n == self.first + self.per, (self.n - self.first, self.per)
        self.n, self.shift = self.first + self.per * turns, 0


def build_program(nc, xT, wall, w_lora, lora_up, lru_bd, par, const_in, x_spill, out):
    with ExitStack() as ctx:
        def sem(name):
            return ctx.enter_context(nc.semaphore(name))

        def keep(name, shape, dt=F32):
            return ctx.enter_context(nc.sbuf_tensor(name, shape, dt))

        def region(*tensors):
            with ExitStack() as own:
                return [own.enter_context(nc.sbuf_tensor(n, s, d)) for n, s, d in tensors]

        cst = keep("cst", [P, CHUNK_CONSTS])
        prm = keep("prm", [P, NPAR])
        drv = keep("drv", [P, 160])
        row = keep("row", [P, T])
        expo = keep("expo", [P, 3])
        stat = keep("stat", [P, 32])
        mean_sq = keep("mean_sq", [P, T])
        raw = keep("raw", [P, RAW, KT * P])
        w_hi = keep("w_hi", [P, SLOTS, KT * P], F32R)
        w_lo = keep("w_lo", [P, SLOTS, KT * P], F32R)
        b_hi = keep("b_hi", [P, KT, T], F32R)
        b_lo = keep("b_lo", [P, KT, T], F32R)

        X_AND_A = [("x", [P, KT, T], F32), ("a_hi", [P, KT, T], F32R), ("a_lo", [P, KT, T], F32R)]
        with ExitStack() as own:
            x, a_hi, a_lo = [own.enter_context(nc.sbuf_tensor(n, s, d)) for n, s, d in X_AND_A]
            u, sc, zpad, xpad, cpad, bd = region(
                ("u", [P, 20, T], F32), ("sc", [P, 12, T], F32), ("zpad", [P, 2, CONF_K - 1 + T], F32),
                ("xpad", [P, 2, LRU_K - 1 + T], F32), ("cpad", [P, 2, SC_K - 1 + T], F32),
                ("bd", [P, 4, P], F32))
            vtok = u[:, SC0:SC1, :].rearrange("p n t -> p (n t)").rearrange("p (b f) -> p b f", b=BT)
            alibi = u[:, SC1:SB0, :].rearrange("p n t -> p (n t)")[:, 0:NCONST - CHUNK_CONSTS]
            z, m_acc, h_tmp, sq = region(
                ("z", [P, KT, T], F32), ("m_acc", [P, KT, T], F32), ("h_tmp", [P, 4, T], F32),
                ("sq", [P, KT, T], F32))
            rk_k, rk_r, rk_v, lora, dx, mix, w_lor = region(
                ("rk_k", [P, KT, T], F32), ("rk_r", [P, KT, T], F32), ("rk_v", [P, KT, T], F32),
                ("lora", [P, T], F32),
                ("dx", [P, KT, T], F32), ("mix", [P, 2, T], F32), ("w_lor", [P, KT, P], F32))
        h = x
        (g0, g1, a0, a1, tn0, tn1, qt0, qt1, ar, be, ka, vf, be_t, ka_t, v_t, kk, kmod,
         _, _, _, _, rk_g, thx, cs, ex, exi, ta, t2, cp, fade, w_up) = region(
            ("g0", [P, BT, 4, P], F32), ("g1", [P, BT, 4, P], F32), ("a0", [P, BT, P], F32),
            ("a1", [P, BT, P], F32), ("tn0", [P, BT, P], F32), ("tn1", [P, BT, P], F32),
            ("qt0", [P, BT, P], F32), ("qt1", [P, BT, P], F32), ("ar", [P, BT, 2, P], F32),
            ("be", [P, BT, P], F32), ("ka", [P, BT, P], F32), ("vf", [P, BT, P], F32),
            ("be_t", [P, BT, P], F32), ("ka_t", [P, BT, P], F32), ("v_t", [P, BT, P], F32),
            ("kk", [P, T], F32), ("kmod", [P, T], F32),
            ("rk_k_", [P, KT, T], F32), ("rk_r_", [P, KT, T], F32), ("rk_v_", [P, KT, T], F32),
            ("lora_", [P, T], F32), ("rk_g", [P, KT, T], F32),
            ("thx", [P, BT, 129], F32), ("cs", [P, BT, 129], F32), ("ex", [P, BT, 129], F32),
            ("exi", [P, BT, 129], F32), ("ta", [P, T], F32), ("t2", [P, T], F32), ("cp", [P, 8], F32),
            ("fade", [P, BT], F32), ("w_up", [P, P], F32))
        rn, t1, bonus, ys = mean_sq, row, ta, vf[:, :, :].rearrange("p b t -> p (b t)")
        s_t, r_s, u_s, s_new = (kmod[:, n * P:(n + 1) * P] for n in range(4))
        x_back, o_buf = region(("x_back", [P, KT, T], F32), ("o_buf", [P, KT, T], F32))
        bank = [ctx.enter_context(nc.psum_tensor(f"bank{n}", [P, T], F32)) for n in range(8)]
        grams, aab, tns, qts = (g0, g1), (a0, a1), (tn0, tn1), (qt0, qt1)

        def const(name, n=0):
            a, w = CCOL[name]
            return cst[:, a:a + w] if name in ("gram", "reset") else cst[:, a + n * P:a + (n + 1) * P]

        def par_col(name, n=0):
            return prm[:, PCOL[name] + n:PCOL[name] + n + 1]

        def over_blocks(mask):
            return mask.rearrange("p (b s) -> p b s", b=1).broadcast_to([P, BT, P])

        CW, LBA, LBX, SP2, TMP, RW = 0, 62, 64, 66, 68, 90

        par_landed = sem("par_landed")
        x_landed = sem("x_landed")
        lora_landed = sem("lora_landed")
        hi_ready = sem("hi_ready")
        lo_ready = sem("lo_ready")
        job_done = sem("job_done")
        job_out = sem("job_out")
        sq_ready = sem("sq_ready")
        ms_done = sem("ms_done")
        ms_out = sem("ms_out")
        row_ready = sem("row_ready")
        x_ready = sem("x_ready")
        ahi_ready, alo_ready = sem("ahi_ready"), sem("alo_ready")
        bhi_ready, blo_ready = sem("bhi_ready"), sem("blo_ready")
        v_steps, s_steps, g_steps = sem("vector_steps"), sem("scalar_steps"), sem("gpsimd_steps")
        names = """drv_in drv_exp drv_ready gate_tanh conf_mean conf_d conf_sq conf_var conf_ve conf_rs conf_n
            conf_t conf_y sc_y lru_xc lru_mm lru_tr lru_t1 lru_t lru_pow lru_x2 lru_in lru_th lru_y v_tr v_tok qk_done
            s_out s_max p_exp p_ready p_tr p_tok pv_done hq_ready xw_ready lora_k
            lora_out mix_ready g_tanh spilled up_landed cp_ready up_done th_ready cs_ready ex_ready kr_ready kn_done n2_out
            n2_pow cut_ready bk_done vf_ready tr_done tr_out gram_done gram_out a_done a_out q_done q_out
            tt_done tt_out tn_done tn_out tn_init r_done r_out u_done u_out st_done st_out y_done y_out ym_done yd_ready yq_ready yv_done
            ve_out ve_pow y_ready x_returned stored alibi_landed tile_done f_ready bonus_ready""".split()
        on = {n: sem(n) for n in names}
        w_landed = [sem(f"w_landed{n}") for n in range(RAW)]
        block = ctx.enter_context(nc.Block())

        @block.sync
        def _(e):
            for j in range(RAW):
                e.dma_start(raw[:, j, :], wall[j]).then_inc(w_landed[j], 16)
            with e.Fori(0, (JOBS - RAW) // RAW) as i:
                for s in range(RAW):
                    e.wait_ge(lo_ready, i * RAW + (s + 1))
                    e.dma_start(raw[:, s, :], wall[i * RAW + (s + RAW)]).then_inc(w_landed[s], 16)
            for k in range(KT):
                e.wait_ge(job_out, J_RO + k + 1)
                e.dma_start(out[k], o_buf[:, k, :]).then_inc(on["stored"], 16)
            e.wait_ge(on["stored"], 16 * KT)
            e.wait_ge(on["spilled"], 16 * KT)

        @block.gpsimd
        def _(e):
            g = Steps(e, g_steps)
            e.memset(expo[:, 0:1], -0.5).then_inc(g_steps, 1)
            e.memset(expo[:, 1:2], 0.5).then_inc(g_steps, 1)
            e.memset(expo[:, 2:3], -1.0).then_inc(g_steps, 1)
            e.wait_ge(g_steps, 3)

            def power(dst, src, which, done):
                e.tensor_tensor(dst, src, expo[:, which:which + 1].to_broadcast([P, T]), ALU.pow).then_inc(done, 1)

            def low(j, s):
                e.wait_ge(hi_ready, j + 1)
                e.tensor_tensor(w_lo[:, s % SLOTS, :], raw[:, s % RAW, :], w_hi[:, s % SLOTS, :].bitcast(F32),
                                ALU.subtract).then_inc(lo_ready, 1)

            def lows(a, b):
                head = (-a) % RAW
                for j in range(a, a + head):
                    low(j, j)
                turns = (b - a - head) // RAW
                with e.Fori(0, turns) as i:
                    for s in range(RAW):
                        low(i * RAW + (a + head + s), s)
                for j in range(a + head + turns * RAW, b):
                    low(j, j)

            def rms(n):
                e.wait_ge(ms_out, n)
                power(row[:, :], mean_sq[:, :], 0, row_ready)

            low(0, 0)
            low(1, 1)
            rms(1)
            lows(2, J_OUT + 2)
            for i in range(2):
                e.wait_ge(on["conf_ve"], i + 1)
                power(sc[:, 6 + i, :], sc[:, 6 + i, :], 0, on["conf_rs"])
            for i in range(2):
                e.wait_ge(on["lru_t"], i + 1)
                power(sc[:, 4 + i, :], sc[:, 4 + i, :], 2, on["lru_pow"])
                power(sc[:, 6 + i, :], sc[:, i, :], 1, on["lru_pow"])
            lows(J_OUT + 2, J_MLP + 2)
            rms(2)
            rms(3)
            lows(J_MLP + 2, J_RK + 2)
            rms(4)
            rms(5)
            lows(J_RK + 2, J_RO + 2)
            with e.Fori(0, KT) as i:
                e.wait_ge(on["n2_out"], i + 1)
                power(rn[:, :], rn[:, :], 0, on["n2_pow"])
                e.wait_ge(on["ve_out"], i + 1)
                power(t1[:, :], t1[:, :], 0, on["ve_pow"])
            lows(J_RO + 2, JOBS)

        @block.scalar
        def _(e):
            st = Steps(e, s_steps)

            def act(dst, src, func, done=None, **how):
                ins = e.activation(dst, src, func, **how)
                if done is None:
                    st(ins)
                else:
                    ins.then_inc(done, 1)

            def high(turn, s):
                e.wait_ge(w_landed[s], turn * 16 + 16)
                act(w_hi[:, s % SLOTS, :], raw[:, s, :], ACT.Copy, hi_ready)

            def next_high(turn, s):
                e.wait_ge(job_done, turn * RAW + (s + 1))
                high(turn + (s + 2) // RAW, (s + 2) % RAW)

            e.dma_start(prm[:, :], par).then_inc(par_landed, 16)
            e.dma_start(cst[:, :], const_in[:, 0:CHUNK_CONSTS]).then_inc(par_landed, 16)
            e.dma_start(bd[:, :, :], lru_bd.rearrange("n p m -> p n m")).then_inc(par_landed, 16)
            e.dma_start(x[:, :, :], xT.rearrange("k p t -> p k t")).then_inc(x_landed, 16)
            high(0, 0)
            high(0, 1)
            e.wait_ge(par_landed, 48)
            e.wait_ge(x_landed, 16)
            for k in range(KT):
                act(a_hi[:, k, :], x[:, k, :], ACT.Identity, ahi_ready, scale=par_col("pre_mix_g", k))
                act(sc[:, k, :], x[:, k, :], ACT.Square, sq_ready)
            e.wait_ge(on["drv_in"], 1)
            act(drv[:, TMP + 2:TMP + 4], drv[:, TMP:TMP + 2], ACT.Exp, on["drv_exp"])

            for n in range(J_OUT):
                next_high(n // RAW, n % RAW)
                if n in (4, 6):
                    i = (n - 4) // 2
                    e.wait_ge(job_out, 2 * i + 2)
                    act(sc[:, 10 + i, :], u[:, CG0 + 2 * i, :], ACT.Tanh, on["gate_tanh"], scale=0.5)

            def y_hi(tile, src, after, count, nth, scale=1.0):
                e.wait_ge(after, count)
                act(b_hi[:, tile, :], src, ACT.Copy, bhi_ready, scale=scale)

            for i in range(2):
                y_hi(2 + i, sc[:, i, :], on["sc_y"], i + 1, i)
            e.dma_start(alibi, const_in[:, CHUNK_CONSTS:NCONST]).then_inc(on["alibi_landed"], 16)
            for i in range(2):
                e.wait_ge(on["conf_d"], i + 1)
                act(sc[:, 4 + i, :], sc[:, 10 + i, :], ACT.Square, on["conf_sq"])
            for i in range(2):
                e.wait_ge(on["conf_n"], i + 1)
                act(sc[:, 4 + i, :], sc[:, 10 + i, :], ACT.Tanh, on["conf_t"], scale=0.5)
            for i in range(2):
                y_hi(i, sc[:, 10 + i, :], on["conf_y"], i + 1, 2 + i, scale=0.5)
            for i in range(2):
                act(u[:, CV0 + 2 * i, :], u[:, LG0 + i, :], ACT.Square, on["lru_x2"])
                e.wait_ge(on["lru_mm"], i + 1)
                act(sc[:, i, :], bank[4][:, :], ACT.Tanh, on["lru_tr"], bias=drv[:, LBA + i:LBA + i + 1], scale=0.5)
                act(sc[:, 2 + i, :], bank[5][:, :], ACT.Tanh, on["lru_tr"], bias=drv[:, LBX + i:LBX + i + 1], scale=0.5)
                e.wait_ge(on["lru_tr"], 2 * i + 1)
                act(sc[:, i, :], sc[:, i, :], ACT.Tanh, on["lru_t1"], bias=drv[:, SP2 + i:SP2 + i + 1],
                    scale=drv[:, SP2 + i:SP2 + i + 1])
            for i in range(2):
                e.wait_ge(on["lru_in"], i + 1)
                act(u[:, CV0 + 2 * i, :], u[:, CV0 + 2 * i, :], ACT.Tanh, on["lru_th"], scale=math.sqrt(2.0 / math.pi))
            for i in range(2):
                y_hi(6 + i, sc[:, 10 + i, :], on["lru_y"], i + 1, 4 + i, scale=0.5)

            for n in range(2):
                e.wait_ge(on["v_tr"], n + 1)
                act(vtok[:, :, n * P:(n + 1) * P], bank[6][:, :].rearrange("p (b f) -> p b f", b=BT), ACT.Copy,
                    on["v_tok"])
            for n, (pair, qt, hh) in enumerate(HEADS):
                keys = (qt + 1) * P
                e.wait_ge(on["s_max"], n + 1)
                if n >= 2:
                    e.wait_ge(on["p_tr"], n - 1)
                act(u[:, 2 + n % 2, 0:keys], u[:, n % 2, 0:keys], ACT.Exp, on["p_exp"], bias=stat[:, n:n + 1],
                    accum_out=stat[:, 16 + n:17 + n])
                e.wait_ge(on["p_tr"], n + 1)
                if n >= 2:
                    e.wait_ge(on["pv_done"], n - 1)
                act(u[:, V0 + n % 2, 0:keys], bank[5 + n % 2][:, 0:keys], ACT.Copy, on["p_tok"])
                if qt == BT - 1 and hh == 1:
                    e.wait_ge(on["pv_done"], n + 1)
                    act(b_hi[:, 4 + pair, :], bank[7][:, :], ACT.Copy, bhi_ready)

            for n in range(KT):
                next_high((J_OUT + n) // RAW, n % RAW)
                act(sq[:, n, :], bank[n % 2][:, :], ACT.Square, sq_ready)
                act(z[:, n, :], bank[n % 2][:, :], ACT.Copy, job_out)
            e.wait_ge(ms_done, 2)
            for k in range(KT):
                e.wait_ge(x_ready, k + 1)
                act(a_hi[:, k, :], x[:, k, :], ACT.Identity, ahi_ready, scale=par_col("pre_mlp_g", k))
                act(sq[:, k, :], x[:, k, :], ACT.Square, sq_ready)

            def mlp(grp, last):
                job = grp * (2 * KT)
                for t in range(KT):
                    next_high(grp * (2 * KT // RAW) + (J_MLP + t) // RAW, t % RAW)
                    e.wait_ge(job_out, job + (J_MLP + t + 1))
                    e.wait_ge(blo_ready, grp * KT + (KT + t - 1))
                    act(h_tmp[:, 2 + t % 2, :], h_tmp[:, t % 2, :], ACT.Square, on["hq_ready"])
                    e.wait_ge(on["hq_ready"], grp * KT + (t + 1))
                    act(b_hi[:, t, :], h_tmp[:, 2 + t % 2, :], ACT.Copy, bhi_ready)
                for t in range(KT):
                    next_high(grp * (2 * KT // RAW) + (J_MLP + KT + t) // RAW, t % RAW)
                    if last:
                        e.wait_ge(job_out, job + (J_MLP + KT + t + 1))
                        act(sq[:, t, :], m_acc[:, t, :], ACT.Square, sq_ready)

            e.wait_ge(ms_done, 3)
            with e.Fori(0, FG - 1) as grp:
                mlp(grp, False)
            mlp(FG - 1, True)

            e.dma_start(w_lor[:, :, :], w_lora).then_inc(lora_landed, 16)
            e.wait_ge(ms_done, 4)
            for k in range(KT):
                e.wait_ge(x_ready, KT + k + 1)
                act(sq[:, k, :], x[:, k, :], ACT.Square, sq_ready)
                e.dma_start(x_spill[k], x[:, k, :]).then_inc(on["spilled"], 16)

            def mix_hi(dst, n, t):
                e.wait_ge(on["mix_ready"], n * KT + t + 1)
                act(dst[:, t, :], mix[:, t % 2, :], ACT.Copy, ahi_ready if dst is a_hi else bhi_ready)

            for t in range(KT):
                mix_hi(a_hi, 0, t)
            for n, (first, store, following) in enumerate(((J_RK, rk_k, b_hi), (J_RR, rk_r, a_hi), (J_RV, rk_v, b_hi))):
                for t in range(KT):
                    next_high((first + t) // RAW, t % RAW)
                    act(store[:, t, :], bank[t % 2][:, :], ACT.Copy, job_out)
                    if n == 2 and t == 0:
                        e.wait_ge(on["lora_k"], 2 * KT)
                        act(lora[0:64, :], bank[2][0:64, :], ACT.Tanh, on["lora_out"])
                        act(lora[64:128, :], bank[3][64:128, :], ACT.Copy, on["lora_out"])
                    mix_hi(following, n + 1, t)
            for t in range(KT):
                next_high((J_RG + t) // RAW, t % RAW)
                if t >= 2:
                    e.wait_ge(job_out, J_RG + t - 1)
                else:
                    e.wait_ge(blo_ready, 56)
                act(mix[:, t % 2, :], bank[t % 2][:, :], ACT.Tanh, on["g_tanh"], scale=0.5)

            e.wait_ge(job_out, J_RO)
            with e.Fori(0, KT) as i:
                tile = bass.ds(i, 1)

                def flat(store):
                    return store[:, tile, :].rearrange("p a t -> p (a t)")
                e.wait_ge(on["tile_done"], i + 1)
                e.dma_start(w_up[:, :], lora_up[tile].rearrange("a p m -> p (a m)")).then_inc(on["up_landed"], 16)
                act(cp[:, :], drv[:, RW:RW + 64].rearrange("p (k c) -> p k c", k=KT)[:, tile, :].rearrange(
                    "p a c -> p (a c)"), ACT.Copy, on["cp_ready"])
                e.wait_ge(on["cp_ready"], i + 1)
                act(kk[:, :], flat(rk_k), ACT.Identity, on["kr_ready"], scale=cp[:, RW_KK:RW_KK + 1])
                e.wait_ge(on["kr_ready"], i * 2 + 1)
                act(t2[:, :], kk[:, :], ACT.Square, on["kr_ready"])
                act(vf[:, :, :].rearrange("p b t -> p (b t)"), flat(rk_v), ACT.Copy, on["vf_ready"])
                e.wait_ge(on["up_done"], i + 1)
                act(thx[:, :, 1:129], bank[0][:, :].rearrange("p (b t) -> p b t", b=BT), ACT.Tanh, on["th_ready"],
                    bias=cp[:, RW_W0:RW_W0 + 1], scale=0.5)
                act(ta[:, :], bank[1][:, :], ACT.Tanh, on["th_ready"], bias=cp[:, RW_A0:RW_A0 + 1], scale=0.5)
                e.wait_ge(on["cs_ready"], i + 1)
                act(ex[:, :, :], thx[:, :, :], ACT.Exp, on["ex_ready"], scale=DECAY)
                act(exi[:, :, :], thx[:, :, :], ACT.Exp, on["ex_ready"], scale=-DECAY)
                for n, dst in enumerate((v_t, be_t, ka_t)):
                    e.wait_ge(on["tr_done"], i * 3 + (n + 1))
                    act(dst[:, :, :], bank[4 + n][:, :].rearrange("p (b f) -> p b f", b=BT), ACT.Copy, on["tr_out"])
                e.wait_ge(on["y_done"], i + 1)
                act(ys, bank[7][:, :], ACT.Copy, on["y_out"])
                e.wait_ge(on["yd_ready"], i + 1)
                act(t2[:, :], ys, ACT.Square, on["yq_ready"])
                e.wait_ge(on["y_ready"], i + 1)
                act(b_hi[:, tile, :].rearrange("p a t -> p (a t)"), ys, ACT.Copy, bhi_ready)

            e.wait_ge(on["tile_done"], KT + 1)
            e.dma_start(x_back[:, :, :], x_spill.rearrange("k p t -> p k t")).then_inc(on["x_returned"], 16)
            for n in range(KT - 2):
                next_high((J_RO + n) // RAW, n % RAW)

        @block.vector
        def _(e):
            v = Steps(e, v_steps)
            tt, ts, stt = e.tensor_tensor, e.tensor_scalar, e.scalar_tensor_tensor

            v(e.memset(zpad[:, :, 0:CONF_K - 1], 0.0))
            v(e.memset(xpad[:, :, 0:LRU_K - 1], 0.0))
            v(e.memset(cpad[:, :, 0:SC_K - 1], 0.0))
            e.wait_ge(par_landed, 48)
            lam = prm[:, PCOL["lam"]:PCOL["lam"] + 2]
            nl, ml, ee, s1, s2, pp = (drv[:, TMP + 2 * n:TMP + 2 * n + 2] for n in (5, 0, 1, 2, 3, 4))
            v(ts(nl, lam, -1.0, None, ALU.mult))
            tt(ml, nl, lam, ALU.min).then_inc(on["drv_in"], 1)
            v(ts(drv[:, CW:CW + 62], prm[:, PCOL["conf_w"]:PCOL["conf_w"] + 62], 0.5, None, ALU.mult))
            v(ts(drv[:, LBA:LBA + 4], prm[:, PCOL["lru_ba"]:PCOL["lru_ba"] + 4], 0.5, None, ALU.mult))
            v(e.tensor_copy(drv[:, RW:RW + 64], prm[:, PCOL["rw"]:PCOL["rw"] + 64]))
            rw = drv[:, RW:RW + 64].rearrange("p (k c) -> p k c", k=KT)
            v(ts(rw[:, :, RW_W0:RW_A0 + 1], rw[:, :, RW_W0:RW_A0 + 1], 0.5, None, ALU.mult))
            v(ts(rw[:, :, RW_OMK:RW_OMK + 1], rw[:, :, RW_KA:RW_KA + 1], -0.5, 1.0, ALU.mult, ALU.add))
            v(ts(rw[:, :, RW_KA:RW_KA + 1], rw[:, :, RW_KA:RW_KA + 1], 0.5, None, ALU.mult))
            e.wait_ge(on["drv_exp"], 1)
            v(ts(s1, ee, 2.0, None, ALU.add))
            v(e.reciprocal(s1, s1))
            v(tt(s1, s1, ee, ALU.mult))
            v(tt(s2, s1, s1, ALU.mult))
            v(ts(pp, s2, 1.0 / 17, None, ALU.mult))
            for odd in (15, 13, 11, 9, 7, 5, 3):
                v(stt(pp, pp, 1.0 / odd, s2, ALU.add, ALU.mult))
            v(stt(pp, pp, 1.0, s1, ALU.add, ALU.mult))
            v(ts(nl, nl, 0.0, None, ALU.max))
            v(ts(nl, nl, 2.0, None, ALU.mult))
            stt(drv[:, SP2:SP2 + 2], pp, 4.0, nl, ALU.mult, ALU.add).then_inc(on["drv_ready"], 1)

            for k in range(KT):
                e.wait_ge(ahi_ready, k + 1)
                stt(a_lo[:, k, :], x[:, k, :], par_col("pre_mix_g", k), a_hi[:, k, :].bitcast(F32), ALU.mult,
                    ALU.subtract).then_inc(alo_ready, 1)

            def mean_square(n):
                e.wait_ge(ms_done, n)
                ts(mean_sq[:, :], bank[2][:, :], 1.0 / D, RMS_EPS, ALU.mult, ALU.add).then_inc(ms_out, 1)

            mean_square(1)
            e.wait_ge(row_ready, 1)

            def tap(n):
                t, i = n // 2, n % 2
                w = drv[:, CW + i * CONF_K + t:CW + i * CONF_K + t + 1]
                src, acc = zpad[:, i, t:t + T], sc[:, 8 + i, :]
                if t == 0:
                    v(ts(acc, src, w, par_col("conf_b", i), ALU.mult, ALU.add))
                else:
                    v(stt(acc, src, w, acc, ALU.mult, ALU.add))

            taps = 0
            for n in range(J_OUT):
                e.wait_ge(job_done, n + 1)
                dst = u[:, n, :]
                if n in (LX0, LX1):
                    dst = xpad[:, n - LX0, LRU_K - 1:]
                if n in (Q0, Q1):
                    stt(dst, bank[n % 2][:, :], HD ** -0.5, row[:, :], ALU.mult, ALU.mult).then_inc(job_out, 1)
                else:
                    tt(dst, bank[n % 2][:, :], row[:, :], ALU.mult).then_inc(job_out, 1)
                if n in (5, 7):
                    i = (n - 5) // 2
                    e.wait_ge(on["gate_tanh"], i + 1)
                    v(stt(zpad[:, i, CONF_K - 1:], sc[:, 10 + i, :], 1.0, u[:, CV0 + 2 * i, :], ALU.add, ALU.mult))
                if n > 7:
                    for _ in range(6 if n < J_OUT - 1 else 2 * CONF_K):
                        if taps < 2 * CONF_K:
                            tap(taps)
                            taps += 1
            e.wait_ge(job_out, J_OUT)

            for i in range(2):
                v(tt(cpad[:, i, SC_K - 1:], u[:, SC0 + 2 * i, :], u[:, SX0 + 2 * i, :], ALU.mult))
                for t in range(SC_K):
                    w = par_col("sconv_w", i * SC_K + t)
                    if t == 0:
                        v(ts(sc[:, i, :], cpad[:, i, 0:T], w, None, ALU.mult))
                    else:
                        v(stt(sc[:, i, :], cpad[:, i, t:t + T], w, sc[:, i, :], ALU.mult, ALU.add))
                tt(sc[:, i, :], sc[:, i, :], u[:, SB0 + i, :], ALU.mult).then_inc(on["sc_y"], 1)

            def y_lo(tile, src, nth, scale=None):
                e.wait_ge(bhi_ready, nth)
                hi = b_hi[:, tile, :].bitcast(F32)
                if scale is None:
                    tt(b_lo[:, tile, :], src, hi, ALU.subtract).then_inc(blo_ready, 1)
                else:
                    stt(b_lo[:, tile, :], src, scale, hi, ALU.mult, ALU.subtract).then_inc(blo_ready, 1)

            for i in range(2):
                y_lo(2 + i, sc[:, i, :], i + 1)

            for i in range(2):
                e.wait_ge(on["conf_mean"], i + 1)
                tt(sc[:, 10 + i, :], sc[:, 8 + i, :], bank[2 + i][:, :], ALU.subtract).then_inc(on["conf_d"], 1)
            for i in range(2):
                e.wait_ge(on["conf_var"], i + 1)
                ts(sc[:, 6 + i, :], bank[2 + i][:, :], GN_EPS, None, ALU.add).then_inc(on["conf_ve"], 1)
            for i in range(2):
                e.wait_ge(on["conf_rs"], i + 1)
                v(tt(sc[:, 10 + i, :], sc[:, 10 + i, :], sc[:, 6 + i, :], ALU.mult))
                ts(sc[:, 10 + i, :], sc[:, 10 + i, :], par_col("gn_g", i), par_col("gn_b", i), ALU.mult,
                   ALU.add).then_inc(on["conf_n"], 1)
            for i in range(2):
                e.wait_ge(on["conf_t"], i + 1)
                stt(sc[:, 10 + i, :], sc[:, 4 + i, :], 1.0, sc[:, 10 + i, :], ALU.add, ALU.mult).then_inc(on["conf_y"], 1)
            for i in range(2):
                y_lo(i, sc[:, 10 + i, :], 3 + i, 0.5)

            for i in range(2):
                xc = u[:, LX0 + i, :]
                for t in range(LRU_K):
                    w, src = par_col("lru_w", i * LRU_K + t), xpad[:, i, t:t + T]
                    if t == 0:
                        v(ts(xc, src, w, par_col("lru_b", i), ALU.mult, ALU.add))
                    elif t < LRU_K - 1:
                        v(stt(xc, src, w, xc, ALU.mult, ALU.add))
                    else:
                        stt(xc, src, w, xc, ALU.mult, ALU.add).then_inc(on["lru_xc"], 1)
            for i in range(2):
                e.wait_ge(on["lru_x2"], i + 1)
                w = u[:, CV0 + 2 * i, :]
                v(ts(w, w, 0.044715, 1.0, ALU.mult, ALU.add))
                tt(w, w, u[:, LG0 + i, :], ALU.mult).then_inc(on["lru_in"], 1)
            for i in range(2):
                e.wait_ge(on["lru_t1"], i + 1)
                ts(sc[:, 4 + i, :], sc[:, i, :], 1.0, None, ALU.add).then_inc(on["lru_t"], 1)
            for i in range(2):
                t, ti, dd, root, a, hh = (sc[:, n + i, :] for n in (0, 2, 4, 6, 8, 10))
                e.wait_ge(on["lru_pow"], 2 * i + 2)
                v(ts(a, t, -1.0, 1.0, ALU.mult, ALU.add))
                v(tt(a, a, dd, ALU.mult))
                v(stt(ti, ti, 1.0, u[:, LX0 + i, :], ALU.add, ALU.mult))
                v(tt(ti, ti, dd, ALU.mult))
                v(tt(ti, ti, root, ALU.mult))
                v(e.tensor_tensor_scan(hh, a, ti, 0.0, ALU.mult, ALU.add))
                e.wait_ge(on["lru_th"], i + 1)
                v(stt(root, u[:, CV0 + 2 * i, :], 1.0, u[:, LG0 + i, :], ALU.add, ALU.mult))
                tt(hh, hh, root, ALU.mult).then_inc(on["lru_y"], 1)
            for i in range(2):
                y_lo(6 + i, sc[:, 10 + i, :], 5 + i, 0.5)

            e.wait_ge(on["alibi_landed"], 16)
            for n, (pair, qt, hh) in enumerate(HEADS):
                keys = (qt + 1) * P
                s = u[:, n % 2, 0:keys]
                e.wait_ge(on["qk_done"], n + 1)
                if n >= 2:
                    e.wait_ge(on["p_exp"], n - 1)
                slope = 2.0 ** (-8.0 * (2 * pair + hh + 1) / ATT_HEADS)
                stt(s, alibi[:, 384 - qt * P:384 - qt * P + keys], slope, bank[3 + n % 2][:, 0:keys], ALU.mult,
                    ALU.add).then_inc(on["s_out"], 1)
                e.wait_ge(on["s_out"], n + 1)
                e.tensor_reduce(stat[:, n:n + 1], s, AX_X, ALU.max, negate=True).then_inc(on["s_max"], 1)
                e.wait_ge(on["p_exp"], n + 1)
                v(e.reciprocal(stat[:, 16 + n:17 + n], stat[:, 16 + n:17 + n]))
                ts(u[:, 2 + n % 2, 0:keys], u[:, 2 + n % 2, 0:keys], stat[:, 16 + n:17 + n], None,
                   ALU.mult).then_inc(on["p_ready"], 1)
                if qt == BT - 1 and hh == 1:
                    y_lo(4 + pair, bank[7][:, :], 7 + pair)

            e.wait_ge(job_done, J_OUT + 1)
            v(e.memset(m_acc[:, :, :], 0.0))

            def add_normed(src, gain, norm, first, after):
                mean_square(norm)
                e.wait_ge(row_ready, norm)
                for k in range(KT):
                    v(tt(src[:, k, :], src[:, k, :], row[:, :], ALU.mult))
                    stt(x[:, k, :], src[:, k, :], par_col(gain, k), x[:, k, :], ALU.mult, ALU.add).then_inc(x_ready, 1)
                    if k:
                        after(k - 1)
                after(KT - 1)

            def mlp_in_lo(k):
                e.wait_ge(ahi_ready, KT + k + 1)
                stt(a_lo[:, k, :], x[:, k, :], par_col("pre_mlp_g", k), a_hi[:, k, :].bitcast(F32), ALU.mult,
                    ALU.subtract).then_inc(alo_ready, 1)

            add_normed(z, "post_mix_g", 2, 0, mlp_in_lo)
            mean_square(3)
            e.wait_ge(row_ready, 3)

            def mlp_out_lo(grp, t):
                e.wait_ge(bhi_ready, grp * KT + (KT + t + 1))
                tt(b_lo[:, t, :], h_tmp[:, 2 + t % 2, :], b_hi[:, t, :].bitcast(F32), ALU.subtract)\
                    .then_inc(blo_ready, 1)

            with e.Fori(0, FG) as grp:
                for t in range(KT):
                    e.wait_ge(job_done, grp * (2 * KT) + (J_MLP + t + 1))
                    stt(h_tmp[:, t % 2, :], bank[t % 2][:, :], 0.0, row[:, :], ALU.max, ALU.mult)\
                        .then_inc(job_out, 1)
                    if t:
                        mlp_out_lo(grp, t - 1)
                mlp_out_lo(grp, KT - 1)
                for t in range(KT):
                    e.wait_ge(job_done, grp * (2 * KT) + (J_MLP + KT + t + 1))
                    tt(m_acc[:, t, :], m_acc[:, t, :], bank[t % 2][:, :], ALU.add).then_inc(job_out, 1)
            e.wait_ge(job_out, J_RK)

            add_normed(m_acc, "post_mlp_g", 4, KT, lambda k: None)
            mean_square(5)
            e.wait_ge(row_ready, 5)
            e.wait_ge(x_ready, 2 * KT)

            e.wait_ge(on["spilled"], 16 * KT)
            for k in range(KT):
                v(stt(h[:, k, :], x[:, k, :], par_col("l0_norm", k), row[:, :], ALU.mult, ALU.mult))
                v(ts(dx[:, k, 0:1], h[:, k, 0:1], -1.0, None, ALU.mult))
                v(tt(dx[:, k, 1:], h[:, k, 0:T - 1], h[:, k, 1:], ALU.subtract))

            def mix_lo(n, hi, lo, base, t):
                e.wait_ge(ahi_ready if hi is a_hi else bhi_ready, base + t + 1)
                tt(lo[:, t, :], mix[:, t % 2, :], hi[:, t, :].bitcast(F32), ALU.subtract)\
                    .then_inc(alo_ready if hi is a_hi else blo_ready, 1)

            def mixes(n, which, hi, lo, base):
                for t in range(KT):
                    if t >= 2:
                        e.wait_ge(alo_ready if hi is a_hi else blo_ready, base + t - 1)
                    stt(mix[:, t % 2, :], dx[:, t, :], par_col("mu", which * KT + t), h[:, t, :], ALU.mult,
                        ALU.add).then_inc(on["mix_ready"], 1)
                    if t:
                        mix_lo(n, hi, lo, base, t - 1)
                mix_lo(n, hi, lo, base, KT - 1)

            mixes(0, 2, a_hi, a_lo, 2 * KT)
            e.wait_ge(alo_ready, 3 * KT)
            mixes(1, 0, b_hi, b_lo, KT + FG * KT)
            e.wait_ge(blo_ready, KT + FG * KT + KT)
            e.wait_ge(job_done, J_RR)
            mixes(2, 3, a_hi, a_lo, 3 * KT)
            e.wait_ge(alo_ready, 4 * KT)
            for t in range(KT):
                for s, which in ((0, 1), (1, 4)):
                    if t:
                        e.wait_ge(on["lora_k"], 2 * t - 1 + s)
                    stt(mix[:, s, :], dx[:, t, :], par_col("mu", which * KT + t), h[:, t, :], ALU.mult,
                        ALU.add).then_inc(on["xw_ready"], 1)
            e.wait_ge(job_done, J_RV)
            e.wait_ge(on["lora_k"], 2 * KT)
            mixes(3, 5, b_hi, b_lo, KT + FG * KT + KT)
            e.wait_ge(blo_ready, 56)
            for t in range(KT):
                e.wait_ge(on["g_tanh"], t + 1)
                stt(rk_g[:, t, :], mix[:, t % 2, :], 1.0, bank[t % 2][:, :], ALU.add, ALU.mult).then_inc(job_out, 1)
            e.wait_ge(job_out, J_RO)

            e.memset(thx[:, :, 0:1], -1.0).then_inc(on["tile_done"], 1)
            e.wait_ge(on["tile_done"], 1)
            with e.Fori(0, KT) as i:
                tile = bass.ds(i, 1)

                def flat(store):
                    return store[:, tile, :].rearrange("p a t -> p (a t)")

                def blocks(a):
                    return a.rearrange("p (b t) -> p b t", b=BT)
                v.loop(i, STEPS_V)
                e.wait_ge(on["th_ready"], i * 2 + 1)
                v(ts(thx[:, :, :], thx[:, :, :], 1.0, None, ALU.add))
                v(e.tensor_tensor_scan(cs[:, :, :].rearrange("p b t -> p (b t)"), const("reset"),
                                       thx[:, :, :].rearrange("p b t -> p (b t)"), 0.0, ALU.mult, ALU.add))
                tt(thx[:, :, :], cs[:, :, :], cs[:, :, 64:65].broadcast_to([P, BT, 129]), ALU.subtract)\
                    .then_inc(on["cs_ready"], 1)
                e.wait_ge(on["kn_done"], i + 1)
                ts(rn[:, :], bank[2][:, :], 1e-24, None, ALU.max).then_inc(on["n2_out"], 1)
                e.wait_ge(on["th_ready"], i * 2 + 2)
                v(ts(t1[:, :], ta[:, :], cp[:, RW_KA:RW_KA + 1], cp[:, RW_OMK:RW_OMK + 1], ALU.mult, ALU.add))
                v(tt(kmod[:, :], t1[:, :], flat(rk_k), ALU.mult))
                v(ts(ta[:, :], ta[:, :], 0.5, 0.5, ALU.mult, ALU.add))
                stt(t1[:, :], flat(rk_r), cp[:, RW_RK:RW_RK + 1], kmod[:, :], ALU.mult, ALU.mult)\
                    .then_inc(on["cut_ready"], 1)
                e.wait_ge(on["ex_ready"], i * 2 + 2)
                v(tt(ka[:, :, :], blocks(kmod[:, :]), exi[:, :, 1:129], ALU.mult))
                v(tt(ar[:, :, 1, :], blocks(flat(rk_r)), ex[:, :, 1:129], ALU.mult))
                v(tt(fade[:, 0:BT - 1], ex[:, 0:BT - 1, 128], exi[:, 1:BT, 0], ALU.mult))
                e.wait_ge(on["n2_pow"], i + 1)
                v(tt(kk[:, :], kk[:, :], rn[:, :], ALU.mult))
                v(stt(ar[:, :, 0, :], blocks(kk[:, :]), -1.0, ex[:, :, 0:128], ALU.mult, ALU.mult))
                v(tt(kk[:, :], kk[:, :], ta[:, :], ALU.mult))
                tt(be[:, :, :], blocks(kk[:, :]), exi[:, :, 1:129], ALU.mult).then_inc(on["f_ready"], 1)
                e.wait_ge(on["bk_done"], i + 1)
                tt(bonus[:, :], flat(rk_v), bank[3][:, :], ALU.mult).then_inc(on["bonus_ready"], 1)
                for n in range(2 * BT):
                    b, hh = n // 2, n % 2
                    e.wait_ge(on["gram_done"], i * (2 * BT) + (n + 1))
                    tt(grams[hh][:, b, :, :].rearrange("p c t -> p (c t)"), bank[n % 4][:, :], const("gram"),
                       ALU.mult).then_inc(on["gram_out"], 1)
                for hh in range(2):
                    e.wait_ge(on["a_done"], i * 2 + (hh + 1))
                    tt(aab[hh][:, :, :], blocks(bank[4 + hh][:, :]), over_blocks(const("lower")), ALU.mult)\
                        .then_inc(on["a_out"], 1)
                e.wait_ge(on["gram_out"], i * (2 * BT) + 2 * BT)
                e.wait_ge(on["a_out"], i * 2 + 2)
                for hh in range(2):
                    v(tt(tns[hh][:, :, :], aab[hh][:, :, :], over_blocks(const("pair")), ALU.mult))
                    v(tt(tns[hh][:, :, :], tns[hh][:, :, :], over_blocks(const("ident")), ALU.add))
                    tta = grams[hh][:, :, 0, :]
                    v(tt(tta, tta, over_blocks(const("pairT")), ALU.mult))
                    tt(tta, tta, over_blocks(const("ident")), ALU.add).then_inc(on["tn_init"], 1)
                for lv in range(LEVELS):
                    for hh in range(2):
                        e.wait_ge(on["q_done"], i * (2 * LEVELS) + (2 * lv + hh + 1))
                        tt(qts[hh][:, :, :], blocks(bank[3 * hh][:, :]), over_blocks(const("level", lv)), ALU.mult)\
                            .then_inc(on["q_out"], 1)
                    for hh in range(2):
                        e.wait_ge(on["tt_done"], i * (2 * LEVELS) + (2 * lv + hh + 1))
                        tta = grams[hh][:, :, 0, :]
                        tt(tta, tta, blocks(bank[3 * hh + 1][:, :]), ALU.add).then_inc(on["tt_out"], 1)
                        if lv < LEVELS - 1:
                            e.wait_ge(on["tn_done"], i * (2 * LEVELS - 2) + (2 * lv + hh + 1))
                            tt(tns[hh][:, :, :], tns[hh][:, :, :], blocks(bank[3 * hh + 2][:, :]), ALU.add)\
                                .then_inc(on["tn_out"], 1)
                e.memset(s_t, 0.0).then_inc(on["st_out"], 1)
                for b in range(BT):
                    e.wait_ge(on["r_done"], i * BT + (b + 1))
                    e.tensor_copy(r_s, bank[6][:, 0:P]).then_inc(on["r_out"], 1)
                    e.wait_ge(on["u_done"], i * BT + (b + 1))
                    e.tensor_copy(u_s, bank[5][:, 0:P]).then_inc(on["u_out"], 1)
                    if b < BT - 1:
                        e.wait_ge(on["st_done"], i * (BT - 1) + (b + 1))
                        v(tt(s_new, s_t, bank[4][:, 0:P], ALU.add))
                        stt(s_t, s_new, fade[:, b:b + 1], const("blk"), ALU.mult, ALU.mult)\
                            .then_inc(on["st_out"], 1)
                e.wait_ge(on["ym_done"], i + 1)
                tt(ys, ys, bank[2][:, :], ALU.subtract).then_inc(on["yd_ready"], 1)
                e.wait_ge(on["yv_done"], i + 1)
                ts(t1[:, :], bank[3][:, :], RW_GN_EPS, None, ALU.add).then_inc(on["ve_out"], 1)
                e.wait_ge(on["ve_pow"], i + 1)
                v(tt(ys, ys, t1[:, :], ALU.mult))
                v(ts(ys, ys, cp[:, RW_GW:RW_GW + 1], cp[:, RW_GB:RW_GB + 1], ALU.mult, ALU.add))
                v(tt(ys, ys, bonus[:, :], ALU.add))
                stt(ys, ys, 0.5, flat(rk_g), ALU.mult, ALU.mult).then_inc(on["y_ready"], 1)
                e.wait_ge(bhi_ready, i + (KT + FG * KT + 2 * KT + 1))
                tt(b_lo[:, tile, :].rearrange("p a t -> p (a t)"), ys,
                   b_hi[:, tile, :].rearrange("p a t -> p (a t)").bitcast(F32), ALU.subtract).then_inc(blo_ready, 1)
                e.wait_ge(blo_ready, i + (KT + FG * KT + 2 * KT + 1))
                e.memset(thx[:, :, 0:1], -1.0).then_inc(on["tile_done"], 1)
            v.end(KT)

            e.wait_ge(on["x_returned"], 16)
            for t in range(KT):
                e.wait_ge(job_done, J_RO + t + 1)
                tt(o_buf[:, t, :], x_back[:, t, :], bank[t % 2][:, :], ALU.add).then_inc(job_out, 1)

        @block.tensor
        def _(e):
            mm = e.matmul

            def job(j, s, hi, lo, ready=None, base=0, free=True):
                e.wait_ge(lo_ready, j + 1)
                if free:
                    e.wait_ge(job_out, j - 1)
                for k in range(KT):
                    if ready is not None:
                        e.wait_ge(ready, base + (k + 1))
                    wh, wl = w_hi[:, s, k * P:(k + 1) * P], w_lo[:, s, k * P:(k + 1) * P]
                    mm(bank[s][:, :], wh, hi[:, k, :], start=(k == 0), stop=False)
                    mm(bank[s][:, :], wh, lo[:, k, :], start=False, stop=False)
                    last = mm(bank[s][:, :], wl, hi[:, k, :], start=False, stop=(k == KT - 1))
                last.then_inc(job_done, 1)

            def jobs(first, count, hi, lo):
                with e.Fori(0, count // SLOTS) as i:
                    for s in range(SLOTS):
                        job(i * SLOTS + (first + s), s, hi, lo)

            def square_sum(k, nth, src):
                e.wait_ge(sq_ready, nth * KT + k + 1)
                ins = mm(bank[2][:, :], const("ones"), src[:, k, :], start=(k == 0), stop=(k == KT - 1))
                if k == KT - 1:
                    ins.then_inc(ms_done, 1)

            e.wait_ge(par_landed, 48)
            job(0, 0, a_hi, a_lo, alo_ready, 0, free=False)
            for k in range(KT):
                square_sum(k, 0, sc)
            job(1, 1, a_hi, a_lo, free=False)
            jobs(2, J_OUT - 2, a_hi, a_lo)

            e.wait_ge(on["sc_y"], 1)
            for i in range(2):
                mm(bank[2 + i][:, :], const("mean"), sc[:, 8 + i, :], start=True, stop=True).then_inc(on["conf_mean"], 1)
            for i in range(2):
                e.wait_ge(on["conf_sq"], i + 1)
                mm(bank[2 + i][:, :], const("mean"), sc[:, 4 + i, :], start=True, stop=True).then_inc(on["conf_var"], 1)
            for i in range(2):
                e.wait_ge(on["lru_xc"], i + 1)
                if i:
                    e.wait_ge(on["lru_tr"], 2 * i)
                mm(bank[4][:, :], bd[:, i, :], u[:, LX0 + i, :], start=True, stop=True)
                mm(bank[5][:, :], bd[:, 2 + i, :], u[:, LX0 + i, :], start=True, stop=True).then_inc(on["lru_mm"], 1)
            for n in range(2):
                if n:
                    e.wait_ge(on["v_tok"], n)
                for b in range(BT):
                    ins = e.transpose(bank[6][:, b * P:(b + 1) * P], u[:, V0 + n, b * P:(b + 1) * P], const("ident"))
                ins.then_inc(on["v_tr"], 1)
            e.wait_ge(on["v_tok"], 2)
            e.wait_ge(on["conf_ve"], 2)
            e.wait_ge(on["lru_tr"], 4)

            def scores(n):
                pair, qt, hh = HEADS[n]
                rows = slice(64 * hh, 64 * hh + 64)
                if n >= 2:
                    e.wait_ge(on["s_out"], n - 1)
                mm(bank[3 + n % 2][:, 0:(qt + 1) * P], u[rows, Q0 + pair, qt * P:(qt + 1) * P],
                   u[rows, K0 + pair, 0:(qt + 1) * P], start=True, stop=True).then_inc(on["qk_done"], 1)

            scores(0)
            for n, (pair, qt, hh) in enumerate(HEADS):
                if n + 1 < len(HEADS):
                    scores(n + 1)
                e.wait_ge(on["p_ready"], n + 1)
                if n >= 2:
                    e.wait_ge(on["p_tok"], n - 1)
                for b in range(qt + 1):
                    ins = e.transpose(bank[5 + n % 2][:, b * P:(b + 1) * P], u[:, 2 + n % 2, b * P:(b + 1) * P],
                                      const("ident"))
                ins.then_inc(on["p_tr"], 1)
                e.wait_ge(on["p_tok"], n + 1)
                if pair == 1 and qt == 0:
                    e.wait_ge(blo_ready, 7)
                head = 2 * pair + hh
                for b in range(qt + 1):
                    ins = mm(bank[7][64 * hh:64 * hh + 64, qt * P:(qt + 1) * P],
                             vtok[:, b, head * HD:(head + 1) * HD], u[:, V0 + n % 2, b * P:(b + 1) * P],
                             start=(b == 0), stop=(b == qt))
                ins.then_inc(on["pv_done"], 1)

            def jobs_with_norm(first, hi, lo, nth):
                for t in range(KT):
                    job(first + t, t % SLOTS, hi, lo)
                    if t:
                        square_sum(t - 1, nth, sq)
                square_sum(KT - 1, nth, sq)

            e.wait_ge(job_out, J_OUT)
            e.wait_ge(blo_ready, KT)
            jobs_with_norm(J_OUT, b_hi, b_lo, 1)

            e.wait_ge(job_out, J_MLP)
            job(J_MLP, 0, a_hi, a_lo, alo_ready, KT)
            for k in range(KT):
                square_sum(k, 2, sq)
            job(J_MLP + 1, 1, a_hi, a_lo)
            jobs(J_MLP + 2, KT - 2, a_hi, a_lo)

            def down(grp, norm):
                first = grp * (2 * KT) + (J_MLP + KT)
                for t in range(KT):
                    if t == 0:
                        job(first + t, 0, b_hi, b_lo, blo_ready, grp * KT + KT)
                    else:
                        job(first + t, t % SLOTS, b_hi, b_lo)
                    if norm and t:
                        square_sum(t - 1, 3, sq)
                if norm:
                    square_sum(KT - 1, 3, sq)

            down(0, False)
            with e.Fori(1, FG - 1) as grp:
                for t in range(KT):
                    job(grp * (2 * KT) + (J_MLP + t), t % SLOTS, a_hi, a_lo)
                down(grp, False)
            jobs(J_MLP + (FG - 1) * 2 * KT, KT, a_hi, a_lo)
            down(FG - 1, True)

            e.wait_ge(job_out, J_RK)
            for k in range(KT):
                square_sum(k, 4, sq)
            for t in range(SLOTS):
                if t == 0:
                    job(J_RK, 0, a_hi, a_lo, alo_ready, 2 * KT)
                else:
                    job(J_RK + t, t, a_hi, a_lo)
            jobs(J_RK + 2, KT - 2, a_hi, a_lo)
            e.wait_ge(blo_ready, KT + FG * KT + KT)
            jobs(J_RR, KT, b_hi, b_lo)
            e.wait_ge(lora_landed, 16)
            for k in range(KT):
                for s in range(2):
                    e.wait_ge(on["xw_ready"], 2 * k + s + 1)
                    mm(bank[2 + s][64 * s:64 * s + 64, :], w_lor[:, k, 64 * s:64 * s + 64], mix[:, s, :], start=(k == 0),
                       stop=(k == KT - 1)).then_inc(on["lora_k"], 1)
            e.wait_ge(alo_ready, 4 * KT)
            jobs(J_RV, KT, a_hi, a_lo)
            e.wait_ge(blo_ready, KT + FG * KT + 2 * KT)
            e.wait_ge(job_out, J_RG)
            jobs(J_RG, KT, b_hi, b_lo)

            e.wait_ge(job_out, J_RO)
            e.wait_ge(on["lora_out"], 2)
            with e.Fori(0, KT) as i:
                e.wait_ge(on["tile_done"], i + 1)
                e.wait_ge(on["up_landed"], i * 16 + 16)
                mm(bank[0][:, :], w_up[0:64, :], lora[0:64, :], start=True, stop=True)
                mm(bank[1][:, :], w_up[64:128, :], lora[64:128, :], start=True, stop=True).then_inc(on["up_done"], 1)
                e.wait_ge(on["kr_ready"], i * 2 + 2)
                mm(bank[2][:, :], const("blk"), t2[:, :], start=True, stop=True).then_inc(on["kn_done"], 1)
                e.wait_ge(on["vf_ready"], i + 1)
                for b in range(BT):
                    ins = e.transpose(bank[4][:, b * P:(b + 1) * P], vf[:, b, :], const("ident"))
                ins.then_inc(on["tr_done"], 1)
                e.wait_ge(on["cut_ready"], i + 1)
                mm(bank[3][:, :], const("blk"), t1[:, :], start=True, stop=True).then_inc(on["bk_done"], 1)
                e.wait_ge(on["f_ready"], i + 1)
                for n, src in ((1, be), (2, ka)):
                    for b in range(BT):
                        ins = e.transpose(bank[4 + n][:, b * P:(b + 1) * P], src[:, b, :], const("ident"))
                    ins.then_inc(on["tr_done"], 1)
                e.wait_ge(on["th_ready"], i * 2 + 2)
                e.wait_ge(on["bonus_ready"], i + 1)
                for n in range(2 * BT):
                    b, hh = n // 2, n % 2
                    rows = slice(64 * hh, 64 * hh + 64)
                    if n >= 4:
                        e.wait_ge(on["gram_out"], i * (2 * BT) + (n - 3))
                    right = ar[rows, b, :, :].rearrange("p c t -> p (c t)")
                    mm(bank[n % 4][:, 0:2 * P], be[rows, b, :], right, start=True, stop=True)
                    mm(bank[n % 4][:, 2 * P:4 * P], ka[rows, b, :], right, start=True, stop=True)\
                        .then_inc(on["gram_done"], 1)
                e.wait_ge(on["tr_out"], i * 3 + 3)
                for hh in range(2):
                    rows = slice(64 * hh, 64 * hh + 64)
                    for b in range(BT):
                        ins = mm(bank[4 + hh][:, b * P:(b + 1) * P], ar[rows, b, 0, :], be[rows, b, :], start=True,
                                 stop=True)
                    ins.then_inc(on["a_done"], 1)
                e.wait_ge(on["gram_out"], i * (2 * BT) + 2 * BT)
                for lv in range(LEVELS):
                    for hh in range(2):
                        if lv == 0:
                            e.wait_ge(on["tn_init"], i * 2 + (hh + 1))
                        else:
                            e.wait_ge(on["tt_out"], i * (2 * LEVELS) + (2 * lv + hh - 1))
                            e.wait_ge(on["tn_out"], i * (2 * LEVELS - 2) + (2 * lv + hh - 1))
                        for b in range(BT):
                            ins = mm(bank[3 * hh][:, b * P:(b + 1) * P], aab[hh][:, b, :], grams[hh][:, b, 0, :],
                                     start=True, stop=True)
                        ins.then_inc(on["q_done"], 1)
                    for hh in range(2):
                        e.wait_ge(on["q_out"], i * (2 * LEVELS) + (2 * lv + hh + 1))
                        for b in range(BT):
                            ins = mm(bank[3 * hh + 1][:, b * P:(b + 1) * P], tns[hh][:, b, :], qts[hh][:, b, :],
                                     start=True, stop=True)
                        ins.then_inc(on["tt_done"], 1)
                        if lv < LEVELS - 1:
                            for b in range(BT):
                                ins = mm(bank[3 * hh + 2][:, b * P:(b + 1) * P], qts[hh][:, b, :], tns[hh][:, b, :],
                                         start=True, stop=True)
                            ins.then_inc(on["tn_done"], 1)
                e.wait_ge(on["tt_out"], i * (2 * LEVELS) + 2 * LEVELS)
                for b in range(BT):
                    e.wait_ge(on["st_out"], i * BT + (b + 1))
                    mm(bank[6][:, 0:P], ar[:, b, 0, :], s_t, start=True, stop=False, skip_group_check=True)
                    for hh in range(2):
                        cols = slice(64 * hh, 64 * hh + 64)
                        ins = mm(bank[6][:, cols], grams[hh][:, b, 2, :], v_t[:, b, cols], start=False, stop=(hh == 1),
                                 skip_group_check=True)
                    ins.then_inc(on["r_done"], 1)
                    e.wait_ge(on["r_out"], i * BT + (b + 1))
                    for hh in range(2):
                        cols = slice(64 * hh, 64 * hh + 64)
                        ins = mm(bank[5][:, cols], grams[hh][:, b, 0, :], r_s[:, cols], start=True, stop=True)
                    ins.then_inc(on["u_done"], 1)
                    part = slice(b * P, (b + 1) * P)
                    mm(bank[7][:, part], s_t, ar[:, b, 1, :], start=True, stop=False, skip_group_check=True)
                    for hh in range(2):
                        cols = slice(64 * hh, 64 * hh + 64)
                        mm(bank[7][cols, part], v_t[:, b, cols], grams[hh][:, b, 3, :], start=False, stop=False,
                           skip_group_check=True)
                    e.wait_ge(on["u_out"], i * BT + (b + 1))
                    for hh in range(2):
                        cols = slice(64 * hh, 64 * hh + 64)
                        ins = mm(bank[7][cols, part], u_s[:, cols], grams[hh][:, b, 1, :], start=False,
                                 stop=(hh == 1), skip_group_check=True)
                    if b < BT - 1:
                        mm(bank[4][:, 0:P], be_t[:, b, :], u_s, start=True, stop=False)
                        mm(bank[4][:, 0:P], ka_t[:, b, :], v_t[:, b, :], start=False, stop=True)\
                            .then_inc(on["st_done"], 1)
                    else:
                        ins.then_inc(on["y_done"], 1)
                e.wait_ge(on["y_out"], i + 1)
                mm(bank[2][:, :], const("mean"), ys, start=True, stop=True).then_inc(on["ym_done"], 1)
                e.wait_ge(on["yq_ready"], i + 1)
                mm(bank[3][:, :], const("mean"), t2[:, :], start=True, stop=True).then_inc(on["yv_done"], 1)

            e.wait_ge(blo_ready, KT + FG * KT + 3 * KT)
            jobs(J_RO, KT, b_hi, b_lo)


_OUT = "out_0_dram"


def kernel(**inputs):
    import concourse.bacc as bacc
    from concourse.bass_utils import run_bass_kernel_spmd

    def arr(name):
        return np.asarray(inputs[name])

    def blocks_of(w):
        k, n = w.shape
        return w.reshape(k // P, P, n // P, P).transpose(2, 1, 0, 3).reshape(n // P, P, k)

    w1, w2 = blocks_of(arr("mlp_w1")[0]), arr("mlp_w2")[0]
    rw_in = arr("l0_w_in_2")
    jobs = [blocks_of(arr("w_in")[0])[W_IN_ORDER], blocks_of(arr("w_out")[0])]
    for g in range(FG):
        jobs += [w1[g * KT:(g + 1) * KT], blocks_of(w2[g * D:(g + 1) * D])]
    for c in (1, 0, 2, 3):
        jobs.append(blocks_of(rw_in[:, c * D:(c + 1) * D]))
    jobs.append(blocks_of(arr("l0_w_out_2")))
    wall = np.concatenate(jobs)

    w_lora = rw_in[:, 4 * D:4 * D + P].reshape(KT, P, P).transpose(1, 0, 2)
    lora_up = np.concatenate([arr("l0_w_up_2"), arr("l0_a_up_2")]).reshape(P, KT, P).transpose(1, 0, 2)
    bd = np.zeros((4, P, P), np.float32)
    for n, name in enumerate(("lru_wa", "lru_wx")):
        for b in range(4):
            at = slice(64 * (b % 2), 64 * (b % 2) + 64)
            bd[2 * n + b // 2, at, at] = arr(name)[0, b]

    def cols(v):
        return v.reshape(-1, P).T

    def taps(w):
        return w.reshape(w.shape[0], 2, P).transpose(2, 1, 0).reshape(P, -1)

    rw = np.stack([cols(arr(n).reshape(-1)) for n in (
        "l0_w0_2", "l0_a0_2", "l0_k_k_2", "l0_k_a_2", "l0_r_k_2", "l0_gn_w_2", "l0_gn_b_2", "l0_k_a_2")], 2)
    parts = {
        "pre_mix_g": cols(arr("pre_mix_g")), "post_mix_g": cols(arr("post_mix_g")),
        "pre_mlp_g": cols(arr("pre_mlp_g")), "post_mlp_g": cols(arr("post_mlp_g")),
        "l0_norm": cols(arr("l0_norm_2")), "mu": cols(arr("l0_mu_2")), "conf_w": taps(arr("conf_dw_w")[0]),
        "conf_b": cols(arr("conf_dw_b")), "gn_g": cols(arr("conf_gn_g")), "gn_b": cols(arr("conf_gn_b")),
        "sconv_w": taps(arr("sconv_w")[0]), "lru_w": taps(arr("lru_conv_w")[0]), "lru_b": cols(arr("lru_conv_b")),
        "lru_ba": cols(arr("lru_ba")), "lru_bx": cols(arr("lru_bx")), "lam": cols(arr("lru_lam")),
        "rw": rw.reshape(P, 64),
    }
    arrays = {
        "xT": arr("x").reshape(T, D).T.reshape(KT, P, T), "wall": wall, "w_lora": w_lora, "lora_up": lora_up,
        "lru_bd": bd, "par": np.concatenate([parts[n] for n, _ in PARAMS], 1), "const_in": constants(),
    }
    nc = bacc.Bacc("TRN2", target_bir_lowering=False, num_devices=1)
    args, fed = {}, {}
    for name, a in arrays.items():
        a = np.ascontiguousarray(a)
        fed[f"in_{name}"] = a
        args[name] = nc.dram_tensor(f"in_{name}", a.shape, F32, kind="ExternalInput").ap()
    args["x_spill"] = nc.dram_tensor("x_spill", (KT, P, T), F32, kind="Internal").ap()
    args["out"] = nc.dram_tensor(_OUT, (KT, P, T), F32, kind="ExternalOutput").ap()
    build_program(nc, **args)
    r = run_bass_kernel_spmd(nc, [fed], core_ids=[0])
    return np.ascontiguousarray(r.results[0][_OUT].reshape(D, T).T).reshape(1, T, D)
```

```python
import math
from contextlib import ExitStack

import numpy as np

import concourse.bass as bass
from concourse import mybir

F32 = mybir.dt.float32
F32R = mybir.dt.float32r
ALU = mybir.AluOpType
ACT = mybir.ActivationFunctionType
AX_X = mybir.AxisListType.X

P = 128
D = 1024
T = 512
KT = D // P
GW = 256
CONF_K, SC_K, LRU_K = 31, 3, 4
ATT_HEADS, HD = 4, 64
DFF = 4096
FG = 4
BT = T // P
RMS_EPS, GN_EPS, RW_GN_EPS = 1e-6, 1e-5, 64e-5
LEVELS = 6

(CV0, CG0, CV1, CG1, Q0, Q1, K0, K1, V0, V1, LX0, LX1, LG0, LG1, SC0, SX0, SC1, SX1, SB0, SB1) = range(20)
W_IN_ORDER = [0, 2, 1, 3, 10, 11, 12, 13, 14, 15, 16, 17, 18, 19, 6, 8, 7, 9, 4, 5]
J_IN, J_OUT = 0, 20
J_MLP = J_OUT + KT
J_RK = J_MLP + FG * 2 * KT
J_RR, J_RV, J_RG, J_RO = (J_RK + KT * n for n in range(1, 5))
JOBS = J_RO + KT
RAW = 4
SLOTS = 2

PARAMS = [("pre_mix_g", 8), ("post_mix_g", 8), ("pre_mlp_g", 8), ("post_mlp_g", 8), ("l0_norm", 8),
          ("mu", 48), ("conf_w", 62), ("conf_b", 2), ("gn_g", 2), ("gn_b", 2), ("sconv_w", 6),
          ("lru_w", 8), ("lru_b", 2), ("lru_ba", 2), ("lru_bx", 2), ("lam", 2), ("rw", 64)]
PCOL, _n = {}, 0
for _name, _w in PARAMS:
    PCOL[_name] = _n
    _n += _w
NPAR = _n
RW_W0, RW_A0, RW_KK, RW_KA, RW_RK, RW_GW, RW_GB, RW_OMK = range(8)

CONSTS = [("ident", 128), ("ones", 128), ("blk", 128), ("mean", 128), ("lower", 128), ("pair", 128),
          ("pairT", 128), ("gram", 512), ("level", 128 * LEVELS), ("reset", BT * 129), ("alibi", 896)]
CCOL, _n = {}, 0
for _name, _w in CONSTS:
    CCOL[_name] = (_n, _w)
    _n += _w
NCONST = _n
CHUNK_CONSTS = CCOL["alibi"][0]

HEADS = [(pair, qt, hh) for pair in range(2) for qt in range(BT) for hh in range(2)]
DECAY = -0.5 * math.exp(-0.5)
STEPS_V = 20


def constants():
    c = np.zeros((P, NCONST), np.float32)

    def put(name, value):
        a, w = CCOL[name]
        c[:, a:a + w] = value
    i, j = np.arange(P)[:, None], np.arange(P)[None, :]
    put("ident", i == j)
    put("ones", 1.0)
    same = (i // 64) == (j // 64)
    put("blk", same)
    put("mean", same / 64.0)
    put("lower", j < i)
    put("pair", (i // 2 == j // 2) & (j < i))
    put("pairT", (i // 2 == j // 2) & (i < j))
    strict, incl = i < j, i <= j
    put("gram", np.concatenate([strict, incl, strict, incl], 1))
    put("level", np.concatenate([((i >> (l + 1)) == (j >> (l + 1))) & ((i >> l) % 2 == 0) & ((j >> l) % 2 == 1)
                                 for l in range(1, LEVELS + 1)], 1))
    r = np.ones((BT, 129))
    r[:, 0] = 0.0
    put("reset", r.reshape(1, -1))
    m = np.arange(896)[None, :] - 384 - i
    put("alibi", np.where(m <= 0, m, -1e30))
    return c


class Steps:

    def __init__(self, engine, sem):
        self.engine, self.sem, self.n, self.shift = engine, sem, 0, 0

    def __call__(self, ins):
        ins.then_inc(self.sem, 1)
        self.n += 1
        self.engine.wait_ge(self.sem, self.n + self.shift)

    def loop(self, i, per):
        self.first, self.per, self.shift = self.n, per, i * per

    def end(self, turns):
        assert self.n == self.first + self.per, (self.n - self.first, self.per)
        self.n, self.shift = self.first + self.per * turns, 0


def build_program(nc, xT, wall, w_lora, lora_up, lru_bd, par, const_in, x_spill, out):
    with ExitStack() as ctx:
        def sem(name):
            return ctx.enter_context(nc.semaphore(name))

        def keep(name, shape, dt=F32):
            return ctx.enter_context(nc.sbuf_tensor(name, shape, dt))

        def region(*tensors):
            with ExitStack() as own:
                return [own.enter_context(nc.sbuf_tensor(n, s, d)) for n, s, d in tensors]

        cst = keep("cst", [P, CHUNK_CONSTS])
        prm = keep("prm", [P, NPAR])
        drv = keep("drv", [P, 160])
        row = keep("row", [P, T])
        eps = keep("eps", [P, 3])
        rms_t = keep("rms_t", [P, BT])
        cn_t = keep("cn_t", [P, 2, 2 * BT])
        kn_t = keep("kn_t", [P, KT, 2 * BT])
        gn_t = keep("gn_t", [P, KT, 2 * BT])
        stat = keep("stat", [P, 32])
        wide = keep("wide", [P, T])
        raw = keep("raw", [P, RAW, KT * P])
        w_hi = keep("w_hi", [P, SLOTS, KT * P], F32R)
        w_lo = keep("w_lo", [P, SLOTS, KT * P], F32R)
        b_hi = keep("b_hi", [P, KT, T], F32R)
        b_lo = keep("b_lo", [P, KT, T], F32R)

        X_AND_A = [("x", [P, KT, T], F32), ("a_hi", [P, KT, T], F32R), ("a_lo", [P, KT, T], F32R)]
        with ExitStack() as own:
            x, a_hi, a_lo = [own.enter_context(nc.sbuf_tensor(n, s, d)) for n, s, d in X_AND_A]
            u, sc, zpad, xpad, cpad, bd = region(
                ("u", [P, 20, T], F32), ("sc", [P, 12, T], F32), ("zpad", [P, 2, CONF_K - 1 + T], F32),
                ("xpad", [P, 2, LRU_K - 1 + T], F32), ("cpad", [P, 2, SC_K - 1 + T], F32),
                ("bd", [P, 4, P], F32))
            vtok = u[:, SC0:SC1, :].rearrange("p n t -> p (n t)").rearrange("p (b f) -> p b f", b=BT)
            alibi = u[:, SC1:SB0, :].rearrange("p n t -> p (n t)")[:, 0:NCONST - CHUNK_CONSTS]
            z, m_acc, h_tmp, sq = region(
                ("z", [P, KT, T], F32), ("m_acc", [P, KT, T], F32), ("h_tmp", [P, 4, T], F32),
                ("sq", [P, KT, T], F32))
            rk_k, rk_r, rk_v, lora, dx, mix, w_lor = region(
                ("rk_k", [P, KT, T], F32), ("rk_r", [P, KT, T], F32), ("rk_v", [P, KT, T], F32),
                ("lora", [P, T], F32),
                ("dx", [P, KT, T], F32), ("mix", [P, 2, T], F32), ("w_lor", [P, KT, P], F32))
        key_sq = w_lor[:, :, :].rearrange("p k m -> p (k m)").rearrange("p (s t) -> p s t", s=2)
        h = x
        (g0, g1, a0, a1, tn0, tn1, qt0, qt1, ar, be, ka, vf, be_t, ka_t, v_t, kk, kmod,
         _, _, _, _, rk_g, thx, cs, ex, exi, ta, t2, cp, fade, w_up) = region(
            ("g0", [P, BT, 4, P], F32), ("g1", [P, BT, 4, P], F32), ("a0", [P, BT, P], F32),
            ("a1", [P, BT, P], F32), ("tn0", [P, BT, P], F32), ("tn1", [P, BT, P], F32),
            ("qt0", [P, BT, P], F32), ("qt1", [P, BT, P], F32), ("ar", [P, BT, 2, P], F32),
            ("be", [P, BT, P], F32), ("ka", [P, BT, P], F32), ("vf", [P, BT, P], F32),
            ("be_t", [P, BT, P], F32), ("ka_t", [P, BT, P], F32), ("v_t", [P, BT, P], F32),
            ("kk", [P, T], F32), ("kmod", [P, T], F32),
            ("rk_k_", [P, KT, T], F32), ("rk_r_", [P, KT, T], F32), ("rk_v_", [P, KT, T], F32),
            ("lora_", [P, T], F32), ("rk_g", [P, KT, T], F32),
            ("thx", [P, BT, 129], F32), ("cs", [P, BT, 129], F32), ("ex", [P, BT, 129], F32),
            ("exi", [P, BT, 129], F32), ("ta", [P, T], F32), ("t2", [P, T], F32), ("cp", [P, 8], F32),
            ("fade", [P, BT], F32), ("w_up", [P, P], F32))
        t1, ys = row, vf[:, :, :].rearrange("p b t -> p (b t)")
        wides = (wide, ta)
        s_t, r_s, u_s, s_new = (kmod[:, n * P:(n + 1) * P] for n in range(4))
        x_back, o_buf = region(("x_back", [P, KT, T], F32), ("o_buf", [P, KT, T], F32))
        bank = [ctx.enter_context(nc.psum_tensor(f"bank{n}", [P, T], F32)) for n in range(8)]
        grams, aab, tns, qts = (g0, g1), (a0, a1), (tn0, tn1), (qt0, qt1)

        def const(name, n=0):
            a, w = CCOL[name]
            return cst[:, a:a + w] if name in ("gram", "reset") else cst[:, a + n * P:a + (n + 1) * P]

        def par_col(name, n=0):
            return prm[:, PCOL[name] + n:PCOL[name] + n + 1]

        def over_blocks(mask):
            return mask.rearrange("p (b s) -> p b s", b=1).broadcast_to([P, BT, P])

        CW, LBA, LBX, SP2, TMP, SP4, RW = 0, 62, 64, 66, 68, 82, 90

        par_landed = sem("par_landed")
        x_landed = sem("x_landed")
        lora_landed = sem("lora_landed")
        hi_ready = sem("hi_ready")
        lo_ready = sem("lo_ready")
        job_done = sem("job_done")
        job_out = sem("job_out")
        sq_ready = sem("sq_ready")
        ms_done = sem("ms_done")
        ms_out = sem("ms_out")
        wide_ready = sem("wide_ready")
        row_done = sem("row_done")
        row_ready = sem("row_ready")
        x_ready = sem("x_ready")
        ahi_ready, alo_ready = sem("ahi_ready"), sem("alo_ready")
        bhi_ready, blo_ready = sem("bhi_ready"), sem("blo_ready")
        v_steps, s_steps = sem("vector_steps"), sem("scalar_steps")
        eps_ready = sem("eps_ready")
        names = """a_done a_out alibi_landed bk_done bonus_ready conf_d conf_mean conf_n conf_row conf_rs conf_sq
            conf_t conf_var conf_ve conf_y cp_ready cs_ready cut_ready drv_exp drv_in drv_ready ex_ready
            f_ready g_tanh gate_tanh gn_aff gn_mul gn_out gn_ready gn_root gn_row gn_wide gram_done
            gram_out hq_ready kk_ready kn_done kn_ready kn_root kn_wide kq_done kq_ready lora_k
            lora_out lru_a lru_in lru_mm lru_root lru_t1 lru_th lru_tr lru_x2 lru_xc lru_y mix_ready p_exp
            p_ready p_tok p_tr pv_done q_done q_out qk_done r_done r_out s_max s_out sc_y spilled st_done
            st_out stored th_ready tile_done tn_done tn_init tn_out tr_done tr_out tt_done tt_out u_done
            u_out up_done up_landed v_tok v_tr vf_ready vn_done vn_out x_returned xw_ready y_done y_out
            yd_kept yd_ready ym_done yq_ready """.split()
        on = {n: sem(n) for n in names}
        w_landed = [sem(f"w_landed{n}") for n in range(RAW)]
        block = ctx.enter_context(nc.Block())

        @block.sync
        def _(e):
            for j in range(RAW):
                e.dma_start(raw[:, j, :], wall[j]).then_inc(w_landed[j], 16)
            with e.Fori(0, (JOBS - RAW) // RAW) as i:
                for s in range(RAW):
                    e.wait_ge(lo_ready, i * RAW + (s + 1))
                    e.dma_start(raw[:, s, :], wall[i * RAW + (s + RAW)]).then_inc(w_landed[s], 16)
            for k in range(KT):
                e.wait_ge(job_out, J_RO + k + 1)
                e.dma_start(out[k], o_buf[:, k, :]).then_inc(on["stored"], 16)
            e.wait_ge(on["stored"], 16 * KT)
            e.wait_ge(on["spilled"], 16 * KT)

        @block.gpsimd
        def _(e):
            for n, value in enumerate((RMS_EPS, GN_EPS, RW_GN_EPS)):
                e.memset(eps[:, n:n + 1], value).then_inc(eps_ready, 1)

            def low(j, s):
                e.wait_ge(hi_ready, j + 1)
                e.tensor_tensor(w_lo[:, s % SLOTS, :], raw[:, s % RAW, :], w_hi[:, s % SLOTS, :].bitcast(F32),
                                ALU.subtract).then_inc(lo_ready, 1)

            def lows(a, b):
                head = (-a) % RAW
                for j in range(a, a + head):
                    low(j, j)
                turns = (b - a - head) // RAW
                with e.Fori(0, turns) as i:
                    for s in range(RAW):
                        low(i * RAW + (a + head + s), s)
                for j in range(a + head + turns * RAW, b):
                    low(j, j)

            low(0, 0)
            low(1, 1)
            lows(2, J_RO + 2)
            for t in range(KT):
                e.wait_ge(bhi_ready, KT + FG * KT + 2 * KT + t + 1)
                e.tensor_tensor(b_lo[:, t, :], rk_k[:, t, :], b_hi[:, t, :].bitcast(F32), ALU.subtract)\
                    .then_inc(blo_ready, 1)
            lows(J_RO + 2, JOBS)

        @block.scalar
        def _(e):
            st = Steps(e, s_steps)

            def act(dst, src, func, done=None, **how):
                ins = e.activation(dst, src, func, **how)
                if done is None:
                    st(ins)
                else:
                    ins.then_inc(done, 1)

            def high(turn, s):
                e.wait_ge(w_landed[s], turn * 16 + 16)
                act(w_hi[:, s % SLOTS, :], raw[:, s, :], ACT.Copy, hi_ready)

            def rms(n):
                e.wait_ge(ms_done, n)
                act(rms_t[:, :], bank[2][:, 0:BT], ACT.Sqrt, ms_out, scale=1.0 / D, bias=eps[:, 0:1])

            def spread(dst, src, done):
                act(dst.rearrange("p (g f) -> p g f", f=HD),
                    src.rearrange("p a g -> p g a").broadcast_to([P, 2 * BT, HD]), ACT.Copy, done)

            def next_high(turn, s):
                e.wait_ge(job_done, turn * RAW + (s + 1))
                high(turn + (s + 2) // RAW, (s + 2) % RAW)

            e.dma_start(prm[:, :], par).then_inc(par_landed, 16)
            e.dma_start(cst[:, :], const_in[:, 0:CHUNK_CONSTS]).then_inc(par_landed, 16)
            e.dma_start(bd[:, :, :], lru_bd.rearrange("n p m -> p n m")).then_inc(par_landed, 16)
            e.dma_start(x[:, :, :], xT.rearrange("k p t -> p k t")).then_inc(x_landed, 16)
            high(0, 0)
            high(0, 1)
            e.wait_ge(par_landed, 48)
            e.wait_ge(x_landed, 16)
            e.wait_ge(eps_ready, 3)
            for k in range(KT):
                act(a_hi[:, k, :], x[:, k, :], ACT.Identity, ahi_ready, scale=par_col("pre_mix_g", k))
                act(sc[:, k, :], x[:, k, :], ACT.Square, sq_ready)
            e.wait_ge(on["drv_in"], 1)
            act(drv[:, TMP + 2:TMP + 4], drv[:, TMP:TMP + 2], ACT.Exp, on["drv_exp"])
            rms(1)

            for n in range(J_OUT):
                next_high(n // RAW, n % RAW)
                if n in (4, 6):
                    i = (n - 4) // 2
                    e.wait_ge(job_out, 2 * i + 2)
                    act(sc[:, 10 + i, :], u[:, CG0 + 2 * i, :], ACT.Tanh, on["gate_tanh"], scale=0.5)

            def y_hi(tile, src, after, count, nth, scale=1.0):
                e.wait_ge(after, count)
                act(b_hi[:, tile, :], src, ACT.Copy, bhi_ready, scale=scale)

            for i in range(2):
                y_hi(2 + i, sc[:, i, :], on["sc_y"], i + 1, i)
            e.dma_start(alibi, const_in[:, CHUNK_CONSTS:NCONST]).then_inc(on["alibi_landed"], 16)
            for i in range(2):
                e.wait_ge(on["conf_d"], i + 1)
                act(sc[:, 4 + i, :], sc[:, 10 + i, :], ACT.Square, on["conf_sq"])
            e.wait_ge(on["conf_var"], 1)
            act(cn_t[:, :, :].rearrange("p i g -> p (i g)"), bank[6][:, 0:4 * BT], ACT.Sqrt, on["conf_ve"],
                scale=1.0 / 64, bias=eps[:, 1:2])
            for i in range(2):
                e.wait_ge(on["conf_n"], i + 1)
                act(sc[:, 4 + i, :], sc[:, 10 + i, :], ACT.Tanh, on["conf_t"], scale=0.5)
            for i in range(2):
                y_hi(i, sc[:, 10 + i, :], on["conf_y"], i + 1, 2 + i, scale=0.5)
            for i in range(2):
                act(u[:, CV0 + 2 * i, :], u[:, LG0 + i, :], ACT.Square, on["lru_x2"])
                e.wait_ge(on["lru_mm"], i + 1)
                act(sc[:, i, :], bank[4][:, :], ACT.Tanh, on["lru_tr"], bias=drv[:, LBA + i:LBA + i + 1], scale=0.5)
                act(sc[:, 2 + i, :], bank[5][:, :], ACT.Tanh, on["lru_tr"], bias=drv[:, LBX + i:LBX + i + 1], scale=0.5)
                e.wait_ge(on["lru_tr"], 2 * i + 1)
                act(sc[:, 8 + i, :], sc[:, i, :], ACT.Exp, on["lru_a"], bias=drv[:, SP4 + i:SP4 + i + 1],
                    scale=drv[:, SP4 + i:SP4 + i + 1])
                e.wait_ge(on["lru_a"], i + 1)
                act(sc[:, i, :], sc[:, i, :], ACT.Tanh, on["lru_t1"], bias=drv[:, SP2 + i:SP2 + i + 1],
                    scale=drv[:, SP2 + i:SP2 + i + 1])
            for i in range(2):
                e.wait_ge(on["lru_t1"], i + 1)
                act(sc[:, 6 + i, :], sc[:, i, :], ACT.Sqrt, on["lru_root"])
            for i in range(2):
                e.wait_ge(on["lru_in"], i + 1)
                act(u[:, CV0 + 2 * i, :], u[:, CV0 + 2 * i, :], ACT.Tanh, on["lru_th"], scale=math.sqrt(2.0 / math.pi))
            for i in range(2):
                y_hi(6 + i, sc[:, 10 + i, :], on["lru_y"], i + 1, 4 + i, scale=0.25)

            for n in range(2):
                e.wait_ge(on["v_tr"], n + 1)
                act(vtok[:, :, n * P:(n + 1) * P], bank[6][:, :].rearrange("p (b f) -> p b f", b=BT), ACT.Copy,
                    on["v_tok"])
            for n, (pair, qt, hh) in enumerate(HEADS):
                keys = (qt + 1) * P
                e.wait_ge(on["s_max"], n + 1)
                if n >= 2:
                    e.wait_ge(on["p_tr"], n - 1)
                act(u[:, 2 + n % 2, 0:keys], u[:, n % 2, 0:keys], ACT.Exp, on["p_exp"], bias=stat[:, n:n + 1],
                    accum_out=stat[:, 16 + n:17 + n])
                e.wait_ge(on["p_tr"], n + 1)
                if n >= 2:
                    e.wait_ge(on["pv_done"], n - 1)
                act(u[:, V0 + n % 2, 0:keys], bank[5 + n % 2][:, 0:keys], ACT.Copy, on["p_tok"])
                if qt == BT - 1 and hh == 1:
                    e.wait_ge(on["pv_done"], n + 1)
                    act(b_hi[:, 4 + pair, :], bank[7][:, :], ACT.Copy, bhi_ready)

            for n in range(KT):
                next_high((J_OUT + n) // RAW, n % RAW)
                act(sq[:, n, :], bank[n % 2][:, :], ACT.Square, sq_ready)
                act(z[:, n, :], bank[n % 2][:, :], ACT.Copy, job_out)
            rms(2)
            for k in range(KT):
                e.wait_ge(x_ready, k + 1)
                act(a_hi[:, k, :], x[:, k, :], ACT.Identity, ahi_ready, scale=par_col("pre_mlp_g", k))
                act(sq[:, k, :], x[:, k, :], ACT.Square, sq_ready)

            def mlp(grp, last):
                job = grp * (2 * KT)
                for t in range(KT):
                    next_high(grp * (2 * KT // RAW) + (J_MLP + t) // RAW, t % RAW)
                    e.wait_ge(job_out, job + (J_MLP + t + 1))
                    e.wait_ge(blo_ready, grp * KT + (KT + t - 1))
                    act(h_tmp[:, 2 + t % 2, :], h_tmp[:, t % 2, :], ACT.Square, on["hq_ready"])
                    e.wait_ge(on["hq_ready"], grp * KT + (t + 1))
                    act(b_hi[:, t, :], h_tmp[:, 2 + t % 2, :], ACT.Copy, bhi_ready)
                for t in range(KT):
                    next_high(grp * (2 * KT // RAW) + (J_MLP + KT + t) // RAW, t % RAW)
                    if last:
                        e.wait_ge(job_out, job + (J_MLP + KT + t + 1))
                        act(sq[:, t, :], m_acc[:, t, :], ACT.Square, sq_ready)

            rms(3)
            with e.Fori(0, FG - 1) as grp:
                mlp(grp, False)
            mlp(FG - 1, True)

            e.dma_start(w_lor[:, :, :], w_lora).then_inc(lora_landed, 16)
            rms(4)
            for k in range(KT):
                e.wait_ge(x_ready, KT + k + 1)
                act(sq[:, k, :], x[:, k, :], ACT.Square, sq_ready)
                e.dma_start(x_spill[k], x[:, k, :]).then_inc(on["spilled"], 16)
            rms(5)

            def mix_hi(dst, n, t):
                e.wait_ge(on["mix_ready"], n * KT + t + 1)
                act(dst[:, t, :], mix[:, t % 2, :], ACT.Copy, ahi_ready if dst is a_hi else bhi_ready)

            for t in range(KT):
                mix_hi(a_hi, 0, t)
            for n, (first, store, following) in enumerate(((J_RK, rk_k, b_hi), (J_RR, rk_r, a_hi), (J_RV, rk_v, b_hi))):
                for t in range(KT):
                    next_high((first + t) // RAW, t % RAW)
                    act(store[:, t, :], bank[t % 2][:, :], ACT.Copy, job_out)
                    if n == 2 and t == 0:
                        e.wait_ge(on["lora_k"], 2 * KT)
                        act(lora[0:64, :], bank[2][0:64, :], ACT.Tanh, on["lora_out"])
                        act(lora[64:128, :], bank[3][64:128, :], ACT.Copy, on["lora_out"])
                    mix_hi(following, n + 1, t)
            for t in range(KT):
                next_high((J_RG + t) // RAW, t % RAW)
                if t >= 2:
                    e.wait_ge(job_out, J_RG + t - 1)
                else:
                    e.wait_ge(blo_ready, 56)
                act(mix[:, t % 2, :], bank[t % 2][:, :], ACT.Tanh, on["g_tanh"], scale=0.5)
                if t >= 2:
                    e.wait_ge(on["kq_done"], t - 1)
                c = RW + t * 8 + RW_KK
                act(key_sq[:, t % 2, :], rk_k[:, t, :], ACT.Square, on["kq_ready"], scale=drv[:, c:c + 1])
            e.wait_ge(on["kq_done"], KT)
            act(kn_t[:, :, :].rearrange("p i g -> p (i g)"), bank[4][:, 0:64], ACT.Sqrt, on["kn_root"])

            e.wait_ge(on["kn_ready"], 1)
            e.wait_ge(job_out, J_RO)
            with e.Fori(0, KT) as i:
                tile = bass.ds(i, 1)

                def flat(store):
                    return store[:, tile, :].rearrange("p a t -> p (a t)")
                e.wait_ge(on["tile_done"], i + 1)
                e.dma_start(w_up[:, :], lora_up[tile].rearrange("a p m -> p (a m)")).then_inc(on["up_landed"], 16)
                act(cp[:, :], drv[:, RW:RW + 64].rearrange("p (k c) -> p k c", k=KT)[:, tile, :].rearrange(
                    "p a c -> p (a c)"), ACT.Copy, on["cp_ready"])
                e.wait_ge(on["cp_ready"], i + 1)
                act(kk[:, :], flat(rk_k), ACT.Identity, on["kk_ready"], scale=cp[:, RW_KK:RW_KK + 1])
                spread(wide[:, :], kn_t[:, tile, :], on["kn_wide"])
                act(vf[:, :, :].rearrange("p b t -> p (b t)"), flat(rk_v), ACT.Copy, on["vf_ready"])
                e.wait_ge(on["up_done"], i + 1)
                act(thx[:, :, 1:129], bank[0][:, :].rearrange("p (b t) -> p b t", b=BT), ACT.Tanh, on["th_ready"],
                    bias=cp[:, RW_W0:RW_W0 + 1], scale=0.5)
                act(ta[:, :], bank[1][:, :], ACT.Tanh, on["th_ready"], bias=cp[:, RW_A0:RW_A0 + 1], scale=0.5)
                e.wait_ge(on["cs_ready"], i + 1)
                act(ex[:, :, :], thx[:, :, :], ACT.Exp, on["ex_ready"], scale=DECAY)
                act(exi[:, :, :], thx[:, :, :], ACT.Exp, on["ex_ready"], scale=-DECAY)
                for n, dst in enumerate((v_t, be_t, ka_t)):
                    e.wait_ge(on["tr_done"], i * 3 + (n + 1))
                    act(dst[:, :, :], bank[4 + n][:, :].rearrange("p (b f) -> p b f", b=BT), ACT.Copy, on["tr_out"])
                e.wait_ge(on["y_done"], i + 1)
                act(ys, bank[7][:, :], ACT.Copy, on["y_out"])
                e.wait_ge(on["yd_ready"], i + 1)
                act(t2[:, :], ys, ACT.Square, on["yq_ready"])
                act(flat(rk_k), ys, ACT.Copy, on["yd_kept"])
                e.wait_ge(on["vn_done"], i + 1)
                act(gn_t[:, tile, :].rearrange("p a g -> p (a g)"), bank[3][:, 0:2 * BT], ACT.Copy, on["vn_out"])

            e.wait_ge(on["tile_done"], KT + 1)
            e.dma_start(x_back[:, :, :], x_spill.rearrange("k p t -> p k t")).then_inc(on["x_returned"], 16)
            flat_gn = gn_t[:, :, :].rearrange("p i g -> p (i g)")
            act(flat_gn, flat_gn, ACT.Sqrt, on["gn_root"], scale=1.0 / HD, bias=eps[:, 2:3])
            e.wait_ge(on["gn_ready"], 1)

            def gated_hi(t):
                e.wait_ge(on["gn_out"], t + 1)
                act(b_hi[:, t, :], rk_k[:, t, :], ACT.Copy, bhi_ready)

            for t in range(KT):
                if t >= 2:
                    e.wait_ge(on["gn_row"], t - 1)
                spread(wides[t % 2][:, :], gn_t[:, t:t + 1, :], on["gn_wide"])
                if t:
                    e.wait_ge(on["gn_mul"], t)
                    c = RW + (t - 1) * 8
                    act(rk_k[:, t - 1, :], rk_k[:, t - 1, :], ACT.Identity, on["gn_aff"],
                        scale=drv[:, c + RW_GW:c + RW_GW + 1], bias=drv[:, c + RW_GB:c + RW_GB + 1])
                if t >= 2:
                    gated_hi(t - 2)
            e.wait_ge(on["gn_mul"], KT)
            c = RW + (KT - 1) * 8
            act(rk_k[:, KT - 1, :], rk_k[:, KT - 1, :], ACT.Identity, on["gn_aff"],
                scale=drv[:, c + RW_GW:c + RW_GW + 1], bias=drv[:, c + RW_GB:c + RW_GB + 1])
            gated_hi(KT - 2)
            gated_hi(KT - 1)

            for n in range(KT - 2):
                next_high((J_RO + n) // RAW, n % RAW)

        @block.vector
        def _(e):
            v = Steps(e, v_steps)
            tt, ts, stt = e.tensor_tensor, e.tensor_scalar, e.scalar_tensor_tensor

            v(e.memset(zpad[:, :, 0:CONF_K - 1], 0.0))
            v(e.memset(xpad[:, :, 0:LRU_K - 1], 0.0))
            v(e.memset(cpad[:, :, 0:SC_K - 1], 0.0))
            e.wait_ge(par_landed, 48)
            lam = prm[:, PCOL["lam"]:PCOL["lam"] + 2]
            nl, ml, ee, s1, s2, pp = (drv[:, TMP + 2 * n:TMP + 2 * n + 2] for n in (5, 0, 1, 2, 3, 4))
            v(ts(nl, lam, -1.0, None, ALU.mult))
            tt(ml, nl, lam, ALU.min).then_inc(on["drv_in"], 1)
            v(ts(drv[:, CW:CW + 62], prm[:, PCOL["conf_w"]:PCOL["conf_w"] + 62], 0.5, None, ALU.mult))
            v(ts(drv[:, LBA:LBA + 4], prm[:, PCOL["lru_ba"]:PCOL["lru_ba"] + 4], 0.5, None, ALU.mult))
            v(e.tensor_copy(drv[:, RW:RW + 64], prm[:, PCOL["rw"]:PCOL["rw"] + 64]))
            rw = drv[:, RW:RW + 64].rearrange("p (k c) -> p k c", k=KT)
            v(ts(rw[:, :, RW_W0:RW_A0 + 1], rw[:, :, RW_W0:RW_A0 + 1], 0.5, None, ALU.mult))
            v(ts(rw[:, :, RW_OMK:RW_OMK + 1], rw[:, :, RW_KA:RW_KA + 1], -0.5, 1.0, ALU.mult, ALU.add))
            v(ts(rw[:, :, RW_KA:RW_KA + 1], rw[:, :, RW_KA:RW_KA + 1], 0.5, None, ALU.mult))
            e.wait_ge(on["drv_exp"], 1)
            v(ts(s1, ee, 2.0, None, ALU.add))
            v(e.reciprocal(s1, s1))
            v(tt(s1, s1, ee, ALU.mult))
            v(tt(s2, s1, s1, ALU.mult))
            v(ts(pp, s2, 1.0 / 17, None, ALU.mult))
            for odd in (15, 13, 11, 9, 7, 5, 3):
                v(stt(pp, pp, 1.0 / odd, s2, ALU.add, ALU.mult))
            v(stt(pp, pp, 1.0, s1, ALU.add, ALU.mult))
            v(ts(nl, nl, 0.0, None, ALU.max))
            v(ts(nl, nl, 2.0, None, ALU.mult))
            v(stt(drv[:, SP2:SP2 + 2], pp, 4.0, nl, ALU.mult, ALU.add))
            ts(drv[:, SP4:SP4 + 2], drv[:, SP2:SP2 + 2], -2.0, None, ALU.mult).then_inc(on["drv_ready"], 1)

            for k in range(KT):
                e.wait_ge(ahi_ready, k + 1)
                stt(a_lo[:, k, :], x[:, k, :], par_col("pre_mix_g", k), a_hi[:, k, :].bitcast(F32), ALU.mult,
                    ALU.subtract).then_inc(alo_ready, 1)

            def spread(dst, src, width, done):
                groups = T // width
                e.tensor_copy(dst.rearrange("p (g f) -> p g f", f=width),
                              src.rearrange("p (g f) -> p g f", f=1).broadcast_to([P, groups, width])).then_inc(done, 1)

            def inverse_rms(n):
                e.wait_ge(ms_out, n)
                v(e.reciprocal(rms_t[:, :], rms_t[:, :]))
                spread(wide[:, :], rms_t[:, :], P, wide_ready)
                e.wait_ge(row_done, n)
                e.tensor_copy(row[:, :], bank[2][:, :]).then_inc(row_ready, 1)
                e.wait_ge(row_ready, n)

            inverse_rms(1)

            def tap(n):
                t, i = n // 2, n % 2
                w = drv[:, CW + i * CONF_K + t:CW + i * CONF_K + t + 1]
                src, acc = zpad[:, i, t:t + T], sc[:, 8 + i, :]
                if t == 0:
                    v(ts(acc, src, w, par_col("conf_b", i), ALU.mult, ALU.add))
                else:
                    v(stt(acc, src, w, acc, ALU.mult, ALU.add))

            taps = 0
            for n in range(J_OUT):
                e.wait_ge(job_done, n + 1)
                dst = u[:, n, :]
                if n in (LX0, LX1):
                    dst = xpad[:, n - LX0, LRU_K - 1:]
                if n in (Q0, Q1):
                    stt(dst, bank[n % 2][:, :], HD ** -0.5, row[:, :], ALU.mult, ALU.mult).then_inc(job_out, 1)
                else:
                    tt(dst, bank[n % 2][:, :], row[:, :], ALU.mult).then_inc(job_out, 1)
                if n in (5, 7):
                    i = (n - 5) // 2
                    e.wait_ge(on["gate_tanh"], i + 1)
                    v(stt(zpad[:, i, CONF_K - 1:], sc[:, 10 + i, :], 1.0, u[:, CV0 + 2 * i, :], ALU.add, ALU.mult))
                if n > 7:
                    for _ in range(6 if n < J_OUT - 1 else 2 * CONF_K):
                        if taps < 2 * CONF_K:
                            tap(taps)
                            taps += 1
            e.wait_ge(job_out, J_OUT)

            for i in range(2):
                v(tt(cpad[:, i, SC_K - 1:], u[:, SC0 + 2 * i, :], u[:, SX0 + 2 * i, :], ALU.mult))
                for t in range(SC_K):
                    w = par_col("sconv_w", i * SC_K + t)
                    if t == 0:
                        v(ts(sc[:, i, :], cpad[:, i, 0:T], w, None, ALU.mult))
                    else:
                        v(stt(sc[:, i, :], cpad[:, i, t:t + T], w, sc[:, i, :], ALU.mult, ALU.add))
                tt(sc[:, i, :], sc[:, i, :], u[:, SB0 + i, :], ALU.mult).then_inc(on["sc_y"], 1)

            def y_lo(tile, src, nth, scale=None):
                e.wait_ge(bhi_ready, nth)
                hi = b_hi[:, tile, :].bitcast(F32)
                if scale is None:
                    tt(b_lo[:, tile, :], src, hi, ALU.subtract).then_inc(blo_ready, 1)
                else:
                    stt(b_lo[:, tile, :], src, scale, hi, ALU.mult, ALU.subtract).then_inc(blo_ready, 1)

            for i in range(2):
                y_lo(2 + i, sc[:, i, :], i + 1)

            for i in range(2):
                e.wait_ge(on["conf_mean"], i + 1)
                tt(sc[:, 10 + i, :], sc[:, 8 + i, :], bank[2 + i][:, :], ALU.subtract).then_inc(on["conf_d"], 1)
            e.wait_ge(on["conf_ve"], 1)
            v(e.reciprocal(cn_t[:, :, :], cn_t[:, :, :]))
            for i in range(2):
                spread(sc[:, 6 + i, :], cn_t[:, i, :], HD, on["conf_rs"])
            for i in range(2):
                e.wait_ge(on["conf_row"], i + 1)
                v(tt(sc[:, 10 + i, :], sc[:, 10 + i, :], bank[2 + i][:, :], ALU.mult))
                ts(sc[:, 10 + i, :], sc[:, 10 + i, :], par_col("gn_g", i), par_col("gn_b", i), ALU.mult,
                   ALU.add).then_inc(on["conf_n"], 1)
            for i in range(2):
                e.wait_ge(on["conf_t"], i + 1)
                stt(sc[:, 10 + i, :], sc[:, 4 + i, :], 1.0, sc[:, 10 + i, :], ALU.add, ALU.mult).then_inc(on["conf_y"], 1)
            for i in range(2):
                y_lo(i, sc[:, 10 + i, :], 3 + i, 0.5)

            for i in range(2):
                xc = u[:, LX0 + i, :]
                for t in range(LRU_K):
                    w, src = par_col("lru_w", i * LRU_K + t), xpad[:, i, t:t + T]
                    if t == 0:
                        v(ts(xc, src, w, par_col("lru_b", i), ALU.mult, ALU.add))
                    elif t < LRU_K - 1:
                        v(stt(xc, src, w, xc, ALU.mult, ALU.add))
                    else:
                        stt(xc, src, w, xc, ALU.mult, ALU.add).then_inc(on["lru_xc"], 1)
            for i in range(2):
                e.wait_ge(on["lru_x2"], i + 1)
                w = u[:, CV0 + 2 * i, :]
                v(ts(w, w, 0.044715, 1.0, ALU.mult, ALU.add))
                tt(w, w, u[:, LG0 + i, :], ALU.mult).then_inc(on["lru_in"], 1)
            for i in range(2):
                ti, root, a, hh = (sc[:, n + i, :] for n in (2, 6, 8, 10))
                e.wait_ge(on["lru_root"], i + 1)
                v(stt(ti, ti, 1.0, u[:, LX0 + i, :], ALU.add, ALU.mult))
                v(stt(root, a, 1.0, root, ALU.add, ALU.mult))
                v(tt(ti, ti, root, ALU.mult))
                v(e.tensor_tensor_scan(hh, a, ti, 0.0, ALU.mult, ALU.add))
                e.wait_ge(on["lru_th"], i + 1)
                v(stt(root, u[:, CV0 + 2 * i, :], 1.0, u[:, LG0 + i, :], ALU.add, ALU.mult))
                tt(hh, hh, root, ALU.mult).then_inc(on["lru_y"], 1)
            for i in range(2):
                y_lo(6 + i, sc[:, 10 + i, :], 5 + i, 0.25)

            e.wait_ge(on["alibi_landed"], 16)
            for n, (pair, qt, hh) in enumerate(HEADS):
                keys = (qt + 1) * P
                s = u[:, n % 2, 0:keys]
                e.wait_ge(on["qk_done"], n + 1)
                if n >= 2:
                    e.wait_ge(on["p_exp"], n - 1)
                slope = 2.0 ** (-8.0 * (2 * pair + hh + 1) / ATT_HEADS)
                stt(s, alibi[:, 384 - qt * P:384 - qt * P + keys], slope, bank[3 + n % 2][:, 0:keys], ALU.mult,
                    ALU.add).then_inc(on["s_out"], 1)
                e.wait_ge(on["s_out"], n + 1)
                e.tensor_reduce(stat[:, n:n + 1], s, AX_X, ALU.max, negate=True).then_inc(on["s_max"], 1)
                e.wait_ge(on["p_exp"], n + 1)
                v(e.reciprocal(stat[:, 16 + n:17 + n], stat[:, 16 + n:17 + n]))
                ts(u[:, 2 + n % 2, 0:keys], u[:, 2 + n % 2, 0:keys], stat[:, 16 + n:17 + n], None,
                   ALU.mult).then_inc(on["p_ready"], 1)
                if qt == BT - 1 and hh == 1:
                    y_lo(4 + pair, bank[7][:, :], 7 + pair)

            e.wait_ge(job_done, J_OUT + 1)
            v(e.memset(m_acc[:, :, :], 0.0))

            def add_normed(src, gain, norm, first, after):
                inverse_rms(norm)
                for k in range(KT):
                    v(tt(src[:, k, :], src[:, k, :], row[:, :], ALU.mult))
                    stt(x[:, k, :], src[:, k, :], par_col(gain, k), x[:, k, :], ALU.mult, ALU.add).then_inc(x_ready, 1)
                    if k:
                        after(k - 1)
                after(KT - 1)

            def mlp_in_lo(k):
                e.wait_ge(ahi_ready, KT + k + 1)
                stt(a_lo[:, k, :], x[:, k, :], par_col("pre_mlp_g", k), a_hi[:, k, :].bitcast(F32), ALU.mult,
                    ALU.subtract).then_inc(alo_ready, 1)

            add_normed(z, "post_mix_g", 2, 0, mlp_in_lo)
            inverse_rms(3)

            def mlp_out_lo(grp, t):
                e.wait_ge(bhi_ready, grp * KT + (KT + t + 1))
                tt(b_lo[:, t, :], h_tmp[:, 2 + t % 2, :], b_hi[:, t, :].bitcast(F32), ALU.subtract)\
                    .then_inc(blo_ready, 1)

            with e.Fori(0, FG) as grp:
                for t in range(KT):
                    e.wait_ge(job_done, grp * (2 * KT) + (J_MLP + t + 1))
                    stt(h_tmp[:, t % 2, :], bank[t % 2][:, :], 0.0, row[:, :], ALU.max, ALU.mult)\
                        .then_inc(job_out, 1)
                    if t:
                        mlp_out_lo(grp, t - 1)
                mlp_out_lo(grp, KT - 1)
                for t in range(KT):
                    e.wait_ge(job_done, grp * (2 * KT) + (J_MLP + KT + t + 1))
                    tt(m_acc[:, t, :], m_acc[:, t, :], bank[t % 2][:, :], ALU.add).then_inc(job_out, 1)
            e.wait_ge(job_out, J_RK)

            add_normed(m_acc, "post_mlp_g", 4, KT, lambda k: None)
            inverse_rms(5)
            e.wait_ge(x_ready, 2 * KT)

            e.wait_ge(on["spilled"], 16 * KT)
            for k in range(KT):
                v(stt(h[:, k, :], x[:, k, :], par_col("l0_norm", k), row[:, :], ALU.mult, ALU.mult))
                v(ts(dx[:, k, 0:1], h[:, k, 0:1], -1.0, None, ALU.mult))
                v(tt(dx[:, k, 1:], h[:, k, 0:T - 1], h[:, k, 1:], ALU.subtract))

            def mix_lo(n, hi, lo, base, t):
                e.wait_ge(ahi_ready if hi is a_hi else bhi_ready, base + t + 1)
                tt(lo[:, t, :], mix[:, t % 2, :], hi[:, t, :].bitcast(F32), ALU.subtract)\
                    .then_inc(alo_ready if hi is a_hi else blo_ready, 1)

            def mixes(n, which, hi, lo, base):
                for t in range(KT):
                    if t >= 2:
                        e.wait_ge(alo_ready if hi is a_hi else blo_ready, base + t - 1)
                    stt(mix[:, t % 2, :], dx[:, t, :], par_col("mu", which * KT + t), h[:, t, :], ALU.mult,
                        ALU.add).then_inc(on["mix_ready"], 1)
                    if t:
                        mix_lo(n, hi, lo, base, t - 1)
                mix_lo(n, hi, lo, base, KT - 1)

            mixes(0, 2, a_hi, a_lo, 2 * KT)
            e.wait_ge(alo_ready, 3 * KT)
            mixes(1, 0, b_hi, b_lo, KT + FG * KT)
            e.wait_ge(blo_ready, KT + FG * KT + KT)
            e.wait_ge(job_done, J_RR)
            mixes(2, 3, a_hi, a_lo, 3 * KT)
            e.wait_ge(alo_ready, 4 * KT)
            for t in range(KT):
                for s, which in ((0, 1), (1, 4)):
                    if t:
                        e.wait_ge(on["lora_k"], 2 * t - 1 + s)
                    stt(mix[:, s, :], dx[:, t, :], par_col("mu", which * KT + t), h[:, t, :], ALU.mult,
                        ALU.add).then_inc(on["xw_ready"], 1)
            e.wait_ge(job_done, J_RV)
            e.wait_ge(on["lora_k"], 2 * KT)
            mixes(3, 5, b_hi, b_lo, KT + FG * KT + KT)
            e.wait_ge(blo_ready, 56)
            for t in range(KT):
                e.wait_ge(on["g_tanh"], t + 1)
                stt(rk_g[:, t, :], mix[:, t % 2, :], 1.0, bank[t % 2][:, :], ALU.add, ALU.mult).then_inc(job_out, 1)
            e.wait_ge(job_out, J_RO)
            e.wait_ge(on["kn_root"], 1)
            flat_kn = kn_t[:, :, :].rearrange("p i g -> p (i g)")
            v(ts(flat_kn, flat_kn, 1e-12, None, ALU.max))
            e.reciprocal(flat_kn, flat_kn).then_inc(on["kn_ready"], 1)

            e.memset(thx[:, :, 0:1], -1.0).then_inc(on["tile_done"], 1)
            e.wait_ge(on["tile_done"], 1)
            with e.Fori(0, KT) as i:
                tile = bass.ds(i, 1)

                def flat(store):
                    return store[:, tile, :].rearrange("p a t -> p (a t)")

                def blocks(a):
                    return a.rearrange("p (b t) -> p b t", b=BT)
                v.loop(i, STEPS_V)
                e.wait_ge(on["th_ready"], i * 2 + 1)
                v(ts(thx[:, :, :], thx[:, :, :], 1.0, None, ALU.add))
                v(e.tensor_tensor_scan(cs[:, :, :].rearrange("p b t -> p (b t)"), const("reset"),
                                       thx[:, :, :].rearrange("p b t -> p (b t)"), 0.0, ALU.mult, ALU.add))
                tt(thx[:, :, :], cs[:, :, :], cs[:, :, 64:65].broadcast_to([P, BT, 129]), ALU.subtract)\
                    .then_inc(on["cs_ready"], 1)
                e.wait_ge(on["th_ready"], i * 2 + 2)
                v(ts(t1[:, :], ta[:, :], cp[:, RW_KA:RW_KA + 1], cp[:, RW_OMK:RW_OMK + 1], ALU.mult, ALU.add))
                v(tt(kmod[:, :], t1[:, :], flat(rk_k), ALU.mult))
                v(ts(ta[:, :], ta[:, :], 0.5, 0.5, ALU.mult, ALU.add))
                stt(t1[:, :], flat(rk_r), cp[:, RW_RK:RW_RK + 1], kmod[:, :], ALU.mult, ALU.mult)\
                    .then_inc(on["cut_ready"], 1)
                e.wait_ge(on["ex_ready"], i * 2 + 2)
                v(tt(ka[:, :, :], blocks(kmod[:, :]), exi[:, :, 1:129], ALU.mult))
                v(tt(ar[:, :, 1, :], blocks(flat(rk_r)), ex[:, :, 1:129], ALU.mult))
                v(tt(fade[:, 0:BT - 1], ex[:, 0:BT - 1, 128], exi[:, 1:BT, 0], ALU.mult))
                e.wait_ge(on["kn_done"], i + 1)
                v(tt(kk[:, :], kk[:, :], bank[2][:, :], ALU.mult))
                v(stt(ar[:, :, 0, :], blocks(kk[:, :]), -1.0, ex[:, :, 0:128], ALU.mult, ALU.mult))
                v(tt(kk[:, :], kk[:, :], ta[:, :], ALU.mult))
                tt(be[:, :, :], blocks(kk[:, :]), exi[:, :, 1:129], ALU.mult).then_inc(on["f_ready"], 1)
                e.wait_ge(on["bk_done"], i + 1)
                tt(flat(rk_v), flat(rk_v), bank[3][:, :], ALU.mult).then_inc(on["bonus_ready"], 1)
                for n in range(2 * BT):
                    b, hh = n // 2, n % 2
                    e.wait_ge(on["gram_done"], i * (2 * BT) + (n + 1))
                    tt(grams[hh][:, b, :, :].rearrange("p c t -> p (c t)"), bank[n % 4][:, :], const("gram"),
                       ALU.mult).then_inc(on["gram_out"], 1)
                for hh in range(2):
                    e.wait_ge(on["a_done"], i * 2 + (hh + 1))
                    tt(aab[hh][:, :, :], blocks(bank[4 + hh][:, :]), over_blocks(const("lower")), ALU.mult)\
                        .then_inc(on["a_out"], 1)
                e.wait_ge(on["gram_out"], i * (2 * BT) + 2 * BT)
                e.wait_ge(on["a_out"], i * 2 + 2)
                for hh in range(2):
                    v(tt(tns[hh][:, :, :], aab[hh][:, :, :], over_blocks(const("pair")), ALU.mult))
                    v(tt(tns[hh][:, :, :], tns[hh][:, :, :], over_blocks(const("ident")), ALU.add))
                    tta = grams[hh][:, :, 0, :]
                    v(tt(tta, tta, over_blocks(const("pairT")), ALU.mult))
                    tt(tta, tta, over_blocks(const("ident")), ALU.add).then_inc(on["tn_init"], 1)
                for lv in range(LEVELS):
                    for hh in range(2):
                        e.wait_ge(on["q_done"], i * (2 * LEVELS) + (2 * lv + hh + 1))
                        tt(qts[hh][:, :, :], blocks(bank[3 * hh][:, :]), over_blocks(const("level", lv)), ALU.mult)\
                            .then_inc(on["q_out"], 1)
                    for hh in range(2):
                        e.wait_ge(on["tt_done"], i * (2 * LEVELS) + (2 * lv + hh + 1))
                        tta = grams[hh][:, :, 0, :]
                        tt(tta, tta, blocks(bank[3 * hh + 1][:, :]), ALU.add).then_inc(on["tt_out"], 1)
                        if lv < LEVELS - 1:
                            e.wait_ge(on["tn_done"], i * (2 * LEVELS - 2) + (2 * lv + hh + 1))
                            tt(tns[hh][:, :, :], tns[hh][:, :, :], blocks(bank[3 * hh + 2][:, :]), ALU.add)\
                                .then_inc(on["tn_out"], 1)
                e.memset(s_t, 0.0).then_inc(on["st_out"], 1)
                for b in range(BT):
                    e.wait_ge(on["r_done"], i * BT + (b + 1))
                    e.tensor_copy(r_s, bank[6][:, 0:P]).then_inc(on["r_out"], 1)
                    e.wait_ge(on["u_done"], i * BT + (b + 1))
                    e.tensor_copy(u_s, bank[5][:, 0:P]).then_inc(on["u_out"], 1)
                    if b < BT - 1:
                        e.wait_ge(on["st_done"], i * (BT - 1) + (b + 1))
                        v(tt(s_new, s_t, bank[4][:, 0:P], ALU.add))
                        stt(s_t, s_new, fade[:, b:b + 1], const("blk"), ALU.mult, ALU.mult)\
                            .then_inc(on["st_out"], 1)
                e.wait_ge(on["ym_done"], i + 1)
                tt(ys, ys, bank[2][:, :], ALU.subtract).then_inc(on["yd_ready"], 1)
                e.wait_ge(on["vn_out"], i + 1)
                e.memset(thx[:, :, 0:1], -1.0).then_inc(on["tile_done"], 1)
            v.end(KT)

            e.wait_ge(on["gn_root"], 1)
            e.reciprocal(gn_t[:, :, :], gn_t[:, :, :]).then_inc(on["gn_ready"], 1)

            def gated(t):
                e.wait_ge(on["gn_aff"], t + 1)
                v(tt(rk_k[:, t, :], rk_k[:, t, :], rk_v[:, t, :], ALU.add))
                stt(rk_k[:, t, :], rk_k[:, t, :], 0.5, rk_g[:, t, :], ALU.mult, ALU.mult).then_inc(on["gn_out"], 1)

            for t in range(KT):
                e.wait_ge(on["gn_row"], t + 1)
                tt(rk_k[:, t, :], rk_k[:, t, :], bank[2 + t % 2][:, :], ALU.mult).then_inc(on["gn_mul"], 1)
                if t:
                    gated(t - 1)
            gated(KT - 1)

            e.wait_ge(on["x_returned"], 16)
            for t in range(KT):
                e.wait_ge(job_done, J_RO + t + 1)
                tt(o_buf[:, t, :], x_back[:, t, :], bank[t % 2][:, :], ALU.add).then_inc(job_out, 1)

        @block.tensor
        def _(e):
            mm = e.matmul

            def job(j, s, hi, lo, ready=None, base=0, free=True):
                e.wait_ge(lo_ready, j + 1)
                if free:
                    e.wait_ge(job_out, j - 1)
                for k in range(KT):
                    if ready is not None:
                        e.wait_ge(ready, base + (k + 1))
                    wh, wl = w_hi[:, s, k * P:(k + 1) * P], w_lo[:, s, k * P:(k + 1) * P]
                    mm(bank[s][:, :], wh, hi[:, k, :], start=(k == 0), stop=False)
                    mm(bank[s][:, :], wh, lo[:, k, :], start=False, stop=False)
                    last = mm(bank[s][:, :], wl, hi[:, k, :], start=False, stop=(k == KT - 1))
                last.then_inc(job_done, 1)

            def jobs(first, count, hi, lo):
                with e.Fori(0, count // SLOTS) as i:
                    for s in range(SLOTS):
                        job(i * SLOTS + (first + s), s, hi, lo)

            def turned(n, src, done):
                for b in range(BT):
                    ins = e.transpose(bank[n][:, b * P:(b + 1) * P], src[:, b * P:(b + 1) * P], const("ident"))
                ins.then_inc(done, 1)

            def head_sums(n, col, src, done):
                for b in range(BT):
                    ins = mm(bank[n][:, col + 2 * b:col + 2 * b + 2], src[:, b * P:(b + 1) * P],
                             const("blk").rearrange("p (h f) -> p h f", h=2)[:, :, 0], start=True, stop=True,
                             skip_group_check=True)
                if done is not None:
                    ins.then_inc(done, 1)

            def square_sum(k, nth, src):
                e.wait_ge(sq_ready, nth * KT + k + 1)
                for b in range(BT):
                    ins = mm(bank[2][:, b:b + 1], src[:, k, b * P:(b + 1) * P], const("ones")[:, 0:1],
                             start=(k == 0 and b == 0), stop=(k == KT - 1), skip_group_check=True)
                if k == KT - 1:
                    ins.then_inc(ms_done, 1)
                    e.wait_ge(wide_ready, nth + 1)
                    turned(2, wide[:, :], row_done)

            e.wait_ge(par_landed, 48)
            job(0, 0, a_hi, a_lo, alo_ready, 0, free=False)
            for k in range(KT):
                square_sum(k, 0, sc)
            job(1, 1, a_hi, a_lo, free=False)
            jobs(2, J_OUT - 2, a_hi, a_lo)

            e.wait_ge(on["sc_y"], 1)
            for i in range(2):
                mm(bank[2 + i][:, :], const("mean"), sc[:, 8 + i, :], start=True, stop=True).then_inc(on["conf_mean"], 1)
            for i in range(2):
                e.wait_ge(on["conf_sq"], i + 1)
                head_sums(6, 2 * BT * i, sc[:, 4 + i, :], on["conf_var"] if i else None)
            for i in range(2):
                e.wait_ge(on["conf_rs"], i + 1)
                turned(2 + i, sc[:, 6 + i, :], on["conf_row"])
            for i in range(2):
                e.wait_ge(on["lru_xc"], i + 1)
                if i:
                    e.wait_ge(on["lru_tr"], 2 * i)
                mm(bank[4][:, :], bd[:, i, :], u[:, LX0 + i, :], start=True, stop=True)
                mm(bank[5][:, :], bd[:, 2 + i, :], u[:, LX0 + i, :], start=True, stop=True).then_inc(on["lru_mm"], 1)
            for n in range(2):
                if n:
                    e.wait_ge(on["v_tok"], n)
                for b in range(BT):
                    ins = e.transpose(bank[6][:, b * P:(b + 1) * P], u[:, V0 + n, b * P:(b + 1) * P], const("ident"))
                ins.then_inc(on["v_tr"], 1)
            e.wait_ge(on["v_tok"], 2)
            e.wait_ge(on["conf_n"], 2)
            e.wait_ge(on["lru_tr"], 4)

            def scores(n):
                pair, qt, hh = HEADS[n]
                rows = slice(64 * hh, 64 * hh + 64)
                if n >= 2:
                    e.wait_ge(on["s_out"], n - 1)
                mm(bank[3 + n % 2][:, 0:(qt + 1) * P], u[rows, Q0 + pair, qt * P:(qt + 1) * P],
                   u[rows, K0 + pair, 0:(qt + 1) * P], start=True, stop=True).then_inc(on["qk_done"], 1)

            scores(0)
            for n, (pair, qt, hh) in enumerate(HEADS):
                if n + 1 < len(HEADS):
                    scores(n + 1)
                e.wait_ge(on["p_ready"], n + 1)
                if n >= 2:
                    e.wait_ge(on["p_tok"], n - 1)
                for b in range(qt + 1):
                    ins = e.transpose(bank[5 + n % 2][:, b * P:(b + 1) * P], u[:, 2 + n % 2, b * P:(b + 1) * P],
                                      const("ident"))
                ins.then_inc(on["p_tr"], 1)
                e.wait_ge(on["p_tok"], n + 1)
                if pair == 1 and qt == 0:
                    e.wait_ge(blo_ready, 7)
                head = 2 * pair + hh
                for b in range(qt + 1):
                    ins = mm(bank[7][64 * hh:64 * hh + 64, qt * P:(qt + 1) * P],
                             vtok[:, b, head * HD:(head + 1) * HD], u[:, V0 + n % 2, b * P:(b + 1) * P],
                             start=(b == 0), stop=(b == qt))
                ins.then_inc(on["pv_done"], 1)

            def jobs_with_norm(first, hi, lo, nth):
                for t in range(KT):
                    job(first + t, t % SLOTS, hi, lo)
                    if t:
                        square_sum(t - 1, nth, sq)
                square_sum(KT - 1, nth, sq)

            e.wait_ge(job_out, J_OUT)
            e.wait_ge(blo_ready, KT)
            jobs_with_norm(J_OUT, b_hi, b_lo, 1)

            e.wait_ge(job_out, J_MLP)
            job(J_MLP, 0, a_hi, a_lo, alo_ready, KT)
            for k in range(KT):
                square_sum(k, 2, sq)
            job(J_MLP + 1, 1, a_hi, a_lo)
            jobs(J_MLP + 2, KT - 2, a_hi, a_lo)

            def down(grp, norm):
                first = grp * (2 * KT) + (J_MLP + KT)
                for t in range(KT):
                    if t == 0:
                        job(first + t, 0, b_hi, b_lo, blo_ready, grp * KT + KT)
                    else:
                        job(first + t, t % SLOTS, b_hi, b_lo)
                    if norm and t:
                        square_sum(t - 1, 3, sq)
                if norm:
                    square_sum(KT - 1, 3, sq)

            down(0, False)
            with e.Fori(1, FG - 1) as grp:
                for t in range(KT):
                    job(grp * (2 * KT) + (J_MLP + t), t % SLOTS, a_hi, a_lo)
                down(grp, False)
            jobs(J_MLP + (FG - 1) * 2 * KT, KT, a_hi, a_lo)
            down(FG - 1, True)

            e.wait_ge(job_out, J_RK)
            for k in range(KT):
                square_sum(k, 4, sq)
            for t in range(SLOTS):
                if t == 0:
                    job(J_RK, 0, a_hi, a_lo, alo_ready, 2 * KT)
                else:
                    job(J_RK + t, t, a_hi, a_lo)
            jobs(J_RK + 2, KT - 2, a_hi, a_lo)
            e.wait_ge(blo_ready, KT + FG * KT + KT)
            jobs(J_RR, KT, b_hi, b_lo)
            e.wait_ge(lora_landed, 16)
            for k in range(KT):
                for s in range(2):
                    e.wait_ge(on["xw_ready"], 2 * k + s + 1)
                    mm(bank[2 + s][64 * s:64 * s + 64, :], w_lor[:, k, 64 * s:64 * s + 64], mix[:, s, :], start=(k == 0),
                       stop=(k == KT - 1)).then_inc(on["lora_k"], 1)
            e.wait_ge(alo_ready, 4 * KT)
            jobs(J_RV, KT, a_hi, a_lo)
            e.wait_ge(blo_ready, KT + FG * KT + 2 * KT)
            e.wait_ge(job_out, J_RG)
            for t in range(KT):
                job(J_RG + t, t % SLOTS, b_hi, b_lo)
                if t:
                    e.wait_ge(on["kq_ready"], t)
                    head_sums(4, 2 * BT * (t - 1), key_sq[:, (t - 1) % 2, :], on["kq_done"])
            e.wait_ge(on["kq_ready"], KT)
            head_sums(4, 2 * BT * (KT - 1), key_sq[:, (KT - 1) % 2, :], on["kq_done"])

            e.wait_ge(job_out, J_RO)
            e.wait_ge(on["lora_out"], 2)
            with e.Fori(0, KT) as i:
                e.wait_ge(on["tile_done"], i + 1)
                e.wait_ge(on["up_landed"], i * 16 + 16)
                mm(bank[0][:, :], w_up[0:64, :], lora[0:64, :], start=True, stop=True)
                mm(bank[1][:, :], w_up[64:128, :], lora[64:128, :], start=True, stop=True).then_inc(on["up_done"], 1)
                e.wait_ge(on["kn_wide"], i + 1)
                turned(2, wide[:, :], on["kn_done"])
                e.wait_ge(on["vf_ready"], i + 1)
                for b in range(BT):
                    ins = e.transpose(bank[4][:, b * P:(b + 1) * P], vf[:, b, :], const("ident"))
                ins.then_inc(on["tr_done"], 1)
                e.wait_ge(on["cut_ready"], i + 1)
                mm(bank[3][:, :], const("blk"), t1[:, :], start=True, stop=True).then_inc(on["bk_done"], 1)
                e.wait_ge(on["f_ready"], i + 1)
                for n, src in ((1, be), (2, ka)):
                    for b in range(BT):
                        ins = e.transpose(bank[4 + n][:, b * P:(b + 1) * P], src[:, b, :], const("ident"))
                    ins.then_inc(on["tr_done"], 1)
                e.wait_ge(on["th_ready"], i * 2 + 2)
                e.wait_ge(on["bonus_ready"], i + 1)
                for n in range(2 * BT):
                    b, hh = n // 2, n % 2
                    rows = slice(64 * hh, 64 * hh + 64)
                    if n >= 4:
                        e.wait_ge(on["gram_out"], i * (2 * BT) + (n - 3))
                    right = ar[rows, b, :, :].rearrange("p c t -> p (c t)")
                    mm(bank[n % 4][:, 0:2 * P], be[rows, b, :], right, start=True, stop=True)
                    mm(bank[n % 4][:, 2 * P:4 * P], ka[rows, b, :], right, start=True, stop=True)\
                        .then_inc(on["gram_done"], 1)
                e.wait_ge(on["tr_out"], i * 3 + 3)
                for hh in range(2):
                    rows = slice(64 * hh, 64 * hh + 64)
                    for b in range(BT):
                        ins = mm(bank[4 + hh][:, b * P:(b + 1) * P], ar[rows, b, 0, :], be[rows, b, :], start=True,
                                 stop=True)
                    ins.then_inc(on["a_done"], 1)
                e.wait_ge(on["gram_out"], i * (2 * BT) + 2 * BT)
                for lv in range(LEVELS):
                    for hh in range(2):
                        if lv == 0:
                            e.wait_ge(on["tn_init"], i * 2 + (hh + 1))
                        else:
                            e.wait_ge(on["tt_out"], i * (2 * LEVELS) + (2 * lv + hh - 1))
                            e.wait_ge(on["tn_out"], i * (2 * LEVELS - 2) + (2 * lv + hh - 1))
                        for b in range(BT):
                            ins = mm(bank[3 * hh][:, b * P:(b + 1) * P], aab[hh][:, b, :], grams[hh][:, b, 0, :],
                                     start=True, stop=True)
                        ins.then_inc(on["q_done"], 1)
                    for hh in range(2):
                        e.wait_ge(on["q_out"], i * (2 * LEVELS) + (2 * lv + hh + 1))
                        for b in range(BT):
                            ins = mm(bank[3 * hh + 1][:, b * P:(b + 1) * P], tns[hh][:, b, :], qts[hh][:, b, :],
                                     start=True, stop=True)
                        ins.then_inc(on["tt_done"], 1)
                        if lv < LEVELS - 1:
                            for b in range(BT):
                                ins = mm(bank[3 * hh + 2][:, b * P:(b + 1) * P], qts[hh][:, b, :], tns[hh][:, b, :],
                                         start=True, stop=True)
                            ins.then_inc(on["tn_done"], 1)
                e.wait_ge(on["tt_out"], i * (2 * LEVELS) + 2 * LEVELS)
                for b in range(BT):
                    e.wait_ge(on["st_out"], i * BT + (b + 1))
                    mm(bank[6][:, 0:P], ar[:, b, 0, :], s_t, start=True, stop=False, skip_group_check=True)
                    for hh in range(2):
                        cols = slice(64 * hh, 64 * hh + 64)
                        ins = mm(bank[6][:, cols], grams[hh][:, b, 2, :], v_t[:, b, cols], start=False, stop=(hh == 1),
                                 skip_group_check=True)
                    ins.then_inc(on["r_done"], 1)
                    e.wait_ge(on["r_out"], i * BT + (b + 1))
                    for hh in range(2):
                        cols = slice(64 * hh, 64 * hh + 64)
                        ins = mm(bank[5][:, cols], grams[hh][:, b, 0, :], r_s[:, cols], start=True, stop=True)
                    ins.then_inc(on["u_done"], 1)
                    part = slice(b * P, (b + 1) * P)
                    mm(bank[7][:, part], s_t, ar[:, b, 1, :], start=True, stop=False, skip_group_check=True)
                    for hh in range(2):
                        cols = slice(64 * hh, 64 * hh + 64)
                        mm(bank[7][cols, part], v_t[:, b, cols], grams[hh][:, b, 3, :], start=False, stop=False,
                           skip_group_check=True)
                    e.wait_ge(on["u_out"], i * BT + (b + 1))
                    for hh in range(2):
                        cols = slice(64 * hh, 64 * hh + 64)
                        ins = mm(bank[7][cols, part], u_s[:, cols], grams[hh][:, b, 1, :], start=False,
                                 stop=(hh == 1), skip_group_check=True)
                    if b < BT - 1:
                        mm(bank[4][:, 0:P], be_t[:, b, :], u_s, start=True, stop=False)
                        mm(bank[4][:, 0:P], ka_t[:, b, :], v_t[:, b, :], start=False, stop=True)\
                            .then_inc(on["st_done"], 1)
                    else:
                        ins.then_inc(on["y_done"], 1)
                e.wait_ge(on["y_out"], i + 1)
                mm(bank[2][:, :], const("mean"), ys, start=True, stop=True).then_inc(on["ym_done"], 1)
                e.wait_ge(on["yq_ready"], i + 1)
                head_sums(3, 0, t2[:, :], on["vn_done"])

            for t in range(KT):
                e.wait_ge(on["gn_wide"], t + 1)
                if t >= 2:
                    e.wait_ge(on["gn_mul"], t - 1)
                turned(2 + t % 2, wides[t % 2][:, :], on["gn_row"])
            job(J_RO, 0, b_hi, b_lo, blo_ready, KT + FG * KT + 2 * KT)
            job(J_RO + 1, 1, b_hi, b_lo)
            jobs(J_RO + 2, KT - 2, b_hi, b_lo)


_OUT = "out_0_dram"


def kernel(**inputs):
    import concourse.bacc as bacc
    from concourse.bass_utils import run_bass_kernel_spmd

    def arr(name):
        return np.asarray(inputs[name])

    def blocks_of(w):
        k, n = w.shape
        return w.reshape(k // P, P, n // P, P).transpose(2, 1, 0, 3).reshape(n // P, P, k)

    w1, w2 = blocks_of(arr("mlp_w1")[0]), arr("mlp_w2")[0]
    rw_in = arr("l0_w_in_2")
    jobs = [blocks_of(arr("w_in")[0])[W_IN_ORDER], blocks_of(arr("w_out")[0])]
    for g in range(FG):
        jobs += [w1[g * KT:(g + 1) * KT], blocks_of(w2[g * D:(g + 1) * D])]
    for c in (1, 0, 2, 3):
        jobs.append(blocks_of(rw_in[:, c * D:(c + 1) * D]))
    jobs.append(blocks_of(arr("l0_w_out_2")))
    wall = np.concatenate(jobs)

    w_lora = rw_in[:, 4 * D:4 * D + P].reshape(KT, P, P).transpose(1, 0, 2)
    lora_up = np.concatenate([arr("l0_w_up_2"), arr("l0_a_up_2")]).reshape(P, KT, P).transpose(1, 0, 2)
    bd = np.zeros((4, P, P), np.float32)
    for n, name in enumerate(("lru_wa", "lru_wx")):
        for b in range(4):
            at = slice(64 * (b % 2), 64 * (b % 2) + 64)
            bd[2 * n + b // 2, at, at] = arr(name)[0, b]

    def cols(v):
        return v.reshape(-1, P).T

    def taps(w):
        return w.reshape(w.shape[0], 2, P).transpose(2, 1, 0).reshape(P, -1)

    rw = np.stack([cols(arr(n).reshape(-1)) for n in (
        "l0_w0_2", "l0_a0_2", "l0_k_k_2", "l0_k_a_2", "l0_r_k_2", "l0_gn_w_2", "l0_gn_b_2", "l0_k_a_2")], 2)
    parts = {
        "pre_mix_g": cols(arr("pre_mix_g")), "post_mix_g": cols(arr("post_mix_g")),
        "pre_mlp_g": cols(arr("pre_mlp_g")), "post_mlp_g": cols(arr("post_mlp_g")),
        "l0_norm": cols(arr("l0_norm_2")), "mu": cols(arr("l0_mu_2")), "conf_w": taps(arr("conf_dw_w")[0]),
        "conf_b": cols(arr("conf_dw_b")), "gn_g": cols(arr("conf_gn_g")), "gn_b": cols(arr("conf_gn_b")),
        "sconv_w": taps(arr("sconv_w")[0]), "lru_w": taps(arr("lru_conv_w")[0]), "lru_b": cols(arr("lru_conv_b")),
        "lru_ba": cols(arr("lru_ba")), "lru_bx": cols(arr("lru_bx")), "lam": cols(arr("lru_lam")),
        "rw": rw.reshape(P, 64),
    }
    arrays = {
        "xT": arr("x").reshape(T, D).T.reshape(KT, P, T), "wall": wall, "w_lora": w_lora, "lora_up": lora_up,
        "lru_bd": bd, "par": np.concatenate([parts[n] for n, _ in PARAMS], 1), "const_in": constants(),
    }
    nc = bacc.Bacc("TRN2", target_bir_lowering=False, num_devices=1)
    args, fed = {}, {}
    for name, a in arrays.items():
        a = np.ascontiguousarray(a)
        fed[f"in_{name}"] = a
        args[name] = nc.dram_tensor(f"in_{name}", a.shape, F32, kind="ExternalInput").ap()
    args["x_spill"] = nc.dram_tensor("x_spill", (KT, P, T), F32, kind="Internal").ap()
    args["out"] = nc.dram_tensor(_OUT, (KT, P, T), F32, kind="ExternalOutput").ap()
    build_program(nc, **args)
    r = run_bass_kernel_spmd(nc, [fed], core_ids=[0])
    return np.ascontiguousarray(r.results[0][_OUT].reshape(D, T).T).reshape(1, T, D)
```

```python
import math
from contextlib import ExitStack

import numpy as np

import concourse.bass as bass
from concourse import mybir

F32 = mybir.dt.float32
F32R = mybir.dt.float32r
ALU = mybir.AluOpType
ACT = mybir.ActivationFunctionType
AX_X = mybir.AxisListType.X

P = 128
D = 1024
T = 512
KT = D // P
GW = 256
CONF_K, SC_K, LRU_K = 31, 3, 4
ATT_HEADS, HD = 4, 64
DFF = 4096
FG = 4
BT = T // P
RMS_EPS, GN_EPS, RW_GN_EPS = 1e-6, 1e-5, 64e-5
LEVELS = 6
NG = 2 * BT

(CV0, CG0, CV1, CG1, Q0, Q1, K0, K1, V0, V1, LX0, LX1, LG0, LG1, SC0, SX0, SC1, SX1, SB0, SB1) = range(20)
W_IN_ORDER = [0, 2, 1, 3, 10, 11, 12, 13, 14, 15, 16, 17, 18, 19, 6, 8, 7, 9, 4, 5]
J_IN, J_OUT = 0, 20
J_MLP = J_OUT + KT
J_RK = J_MLP + FG * 2 * KT
J_RR, J_RV, J_RG, J_RO = (J_RK + KT * n for n in range(1, 5))
JOBS = J_RO + KT
RAW = 4
SLOTS = 2

PARAMS = [("pre_mix_g", 8), ("post_mix_g", 8), ("pre_mlp_g", 8), ("post_mlp_g", 8), ("l0_norm", 8),
          ("mu", 48), ("conf_w", 62), ("conf_b", 2), ("gn_g", 2), ("gn_b", 2), ("sconv_w", 6),
          ("lru_w", 8), ("lru_b", 2), ("lru_ba", 2), ("lru_bx", 2), ("lam", 2), ("rw", 64)]
PCOL, _n = {}, 0
for _name, _w in PARAMS:
    PCOL[_name] = _n
    _n += _w
NPAR = _n
RW_W0, RW_A0, RW_KK, RW_KA, RW_RK, RW_GW, RW_GB, RW_OMK = range(8)

CONSTS = [("ident", 128), ("ones", 1), ("blk", 128), ("mean", 128), ("lower", 128), ("pair", 128), ("pairT", 128),
          ("gram", 256), ("level", 128 * (LEVELS - 1)), ("reset", BT * 129), ("alibi", 896)]
CCOL, _n = {}, 0
for _name, _w in CONSTS:
    CCOL[_name] = (_n, _w)
    _n += _w
NCONST = _n
CHUNK_CONSTS = CCOL["alibi"][0]

HEADS = [(pair, qt, hh) for pair in range(2) for qt in range(BT) for hh in range(2)]
DECAY = -0.5 * math.exp(-0.5)
STEPS_V = 14
BANKS_AT = ((3, 4, 5, 6), (5, 3, 6, 4), (6, 5, 4, 3), (4, 6, 3, 5), (3, 4, 5, 6), (5, 3, 6, 4))
LOW, HIGH = slice(0, 64), slice(64, 128)
GRAMS_AT = (2, 5, 8, NG + 2, NG + 2)


def constants():
    c = np.zeros((P, NCONST), np.float32)

    def put(name, value):
        a, w = CCOL[name]
        c[:, a:a + w] = value
    i, j = np.arange(P)[:, None], np.arange(P)[None, :]
    put("ident", i == j)
    put("ones", 1.0)
    same = (i // 64) == (j // 64)
    put("blk", same)
    put("mean", same / 64.0)
    put("lower", j < i)
    strict, incl = i < j, i <= j
    put("gram", np.concatenate([strict, incl], 1))
    put("pair", (i // 2 == j // 2) & (j < i))
    put("pairT", (i // 2 == j // 2) & (i < j))
    put("level", np.concatenate([((i >> (l + 1)) == (j >> (l + 1))) & ((i >> l) % 2 == 0) & ((j >> l) % 2 == 1)
                                 for l in range(1, LEVELS)], 1))
    r = np.ones((BT, 129))
    r[:, 0] = 0.0
    put("reset", r.reshape(1, -1))
    m = np.arange(896)[None, :] - 384 - i
    put("alibi", np.where(m <= 0, m, -1e30))
    return c


class Steps:

    def __init__(self, engine, sem):
        self.engine, self.sem, self.n, self.shift = engine, sem, 0, 0

    def __call__(self, ins):
        ins.then_inc(self.sem, 1)
        self.n += 1
        self.engine.wait_ge(self.sem, self.n + self.shift)

    def loop(self, i, per):
        self.first, self.per, self.shift = self.n, per, i * per

    def end(self, turns):
        assert self.n == self.first + self.per, (self.n - self.first, self.per)
        self.n, self.shift = self.first + self.per * turns, 0


def build_program(nc, xT, wall, w_lora, lora_up, lru_bd, par, const_in, x_spill, out):
    with ExitStack() as ctx:
        def sem(name):
            return ctx.enter_context(nc.semaphore(name))

        def keep(name, shape, dt=F32):
            return ctx.enter_context(nc.sbuf_tensor(name, shape, dt))

        def region(*tensors):
            with ExitStack() as own:
                return [own.enter_context(nc.sbuf_tensor(n, s, d)) for n, s, d in tensors]

        cst = keep("cst", [P, CHUNK_CONSTS])
        prm = keep("prm", [P, NPAR])
        drv = keep("drv", [P, 160])
        row = keep("row", [P, T])
        eps = keep("eps", [P, 3])
        rms_t = keep("rms_t", [P, BT])
        cn_t = keep("cn_t", [P, 2, 2 * BT])
        kn_t = keep("kn_t", [P, KT, 2 * BT])
        gn_t = keep("gn_t", [P, 2 * BT])
        cp_end = keep("cp_end", [P, 8])
        stat = keep("stat", [P, 32])
        wide = keep("wide", [P, T])
        raw = keep("raw", [P, RAW, KT * P])
        w_hi = keep("w_hi", [P, SLOTS, KT * P], F32R)
        w_lo = keep("w_lo", [P, SLOTS, KT * P], F32R)
        b_hi, b_lo = region(("b_hi", [P, KT, T], F32R), ("b_lo", [P, KT, T], F32R))

        def chunk_set(name):
            return [(name + n, shape, F32) for n, shape in (
                ("gram", [P, NG, 4, P]), ("a", [P, NG, P]), ("ar", [P, BT, 2, P]), ("be_t", [P, BT, P]),
                ("ka_t", [P, BT, P]), ("v_t", [P, BT, P]))]
        odd = [keep(*t) for t in chunk_set("odd_")]
        s_t, r_s, u_s, s_new = (keep(n, [P, P]) for n in ("s_t", "r_s", "u_s", "s_new"))

        X_AND_A = [("x", [P, KT, T], F32), ("a_hi", [P, KT, T], F32R), ("a_lo", [P, KT, T], F32R)]
        with ExitStack() as own:
            x, a_hi, a_lo = [own.enter_context(nc.sbuf_tensor(n, s, d)) for n, s, d in X_AND_A]
            u, sc, zpad, xpad, cpad, bd = region(
                ("u", [P, 20, T], F32), ("sc", [P, 12, T], F32), ("zpad", [P, 2, CONF_K - 1 + T], F32),
                ("xpad", [P, 2, LRU_K - 1 + T], F32), ("cpad", [P, 2, SC_K - 1 + T], F32),
                ("bd", [P, 4, P], F32))
            vtok = u[:, SC0:SC1, :].rearrange("p n t -> p (n t)").rearrange("p (b f) -> p b f", b=BT)
            gelu = [u[:, SB0 + i, :] for i in range(2)]
            alibi = u[:, SC1:SB0, :].rearrange("p n t -> p (n t)")[:, 0:NCONST - CHUNK_CONSTS]
            z, m_acc, h_tmp, sq = region(
                ("z", [P, KT, T], F32), ("m_acc", [P, KT, T], F32), ("h_tmp", [P, 4, T], F32),
                ("sq", [P, KT, T], F32))
            rk_k, rk_r, rk_v, lora, dx, mix, w_lor = region(
                ("rk_k", [P, KT, T], F32), ("rk_r", [P, KT, T], F32), ("rk_v", [P, KT, T], F32),
                ("lora", [P, T], F32),
                ("dx", [P, KT, T], F32), ("mix", [P, 2, T], F32), ("w_lor", [P, KT, P], F32))
        key_sq = w_lor[:, :, :].rearrange("p k m -> p (k m)").rearrange("p (s t) -> p s t", s=2)
        h = x
        chunk = region(
            *chunk_set("even_"), ("be", [P, BT, P], F32), ("ka", [P, BT, P], F32), ("ta", [P, T], F32),
            ("q_full", [P, NG, P], F32), ("be_h", [P, 2, BT, P], F32), ("ka_h", [P, 2, BT, P], F32),
            ("rk_k_", [P, KT, T], F32), ("rk_r_", [P, KT, T], F32), ("rk_v_", [P, KT, T], F32),
            ("lora_", [P, T], F32), ("rk_g", [P, KT, T], F32),
            ("ex", [P, BT, 129], F32), ("exi", [P, BT, 129], F32), ("cp", [P, 8], F32), ("fade", [P, 2, BT], F32),
            ("w_up", [P, P], F32), ("t_full", [P, NG, P], F32),
            ("ys", [P, T], F32), ("t2", [P, T], F32))
        even, (be, ka, ta, q_full, be_h, ka_h), rk_g = chunk[0:6], chunk[6:12], chunk[16]
        ex, exi, cp, fade, w_up, t_full, ys, t2 = chunk[17:]
        grams, a_full, ars, be_ts, ka_ts, v_ts = ((even[n], odd[n]) for n in range(6))
        kk, kmod = (a[:, :, :].rearrange("p b t -> p (b t)") for a in (be, ka))
        t1, thx, cs = row, ex, exi
        x_back, o_buf = region(("x_back", [P, KT, T], F32), ("o_buf", [P, KT, T], F32))
        bank = [ctx.enter_context(nc.psum_tensor(f"bank{n}", [P, T], F32)) for n in range(8)]

        def const(name, n=0):
            a, w = CCOL[name]
            return cst[:, a + n * P:a + (n + 1) * P] if w % P == 0 and name != "gram" else cst[:, a:a + w]

        def par_col(name, n=0):
            return prm[:, PCOL[name] + n:PCOL[name] + n + 1]

        def over_blocks(mask):
            return mask.rearrange("p (b s) -> p b s", b=1).broadcast_to([P, BT, mask.shape[-1]])

        def over_problems(mask):
            return mask.rearrange("p (b s) -> p b s", b=1).broadcast_to([P, NG, P])

        def index(t):
            return t[0] * 2 + t[1]

        def count(t, per, more):
            return t[0] * (2 * per) + (t[1] * per + more)

        CW, LBA, LBX, SP2, TMP, SP4, RW = 0, 62, 64, 66, 68, 82, 90

        par_landed = sem("par_landed")
        const_landed = sem("const_landed")
        bd_landed = sem("bd_landed")
        spilled = [sem(f"spilled{k}") for k in range(KT)]
        x_landed = [sem(f"x_landed{k}") for k in range(KT)]
        lora_landed = sem("lora_landed")
        hi_ready = sem("hi_ready")
        lo_ready = sem("lo_ready")
        job_done = sem("job_done")
        job_out = sem("job_out")
        sq_ready = sem("sq_ready")
        ms_done = sem("ms_done")
        ms_out = sem("ms_out")
        wide_ready = sem("wide_ready")
        row_done = sem("row_done")
        row_ready = sem("row_ready")
        x_ready = sem("x_ready")
        ahi_ready, alo_ready = sem("ahi_ready"), sem("alo_ready")
        bhi_ready, blo_ready = sem("bhi_ready"), sem("blo_ready")
        v_steps, s_steps = sem("vector_steps"), sem("scalar_steps")
        eps_ready = sem("eps_ready")
        names = """alibi_landed alpha_ready bk_done bonus_ready conf_d conf_mean conf_n conf_row conf_rs conf_sq
            conf_t conf_var conf_ve conf_y cp_ready cs_ready cut_ready drv_exp drv_in drv_ready dx_ready
            end_ready ex_ready f_part f_ready g_tanh gate_tanh gated gn_aff gn_mul gn_row gn_wide gram_done
            gram_out h_ready halves_ready hq_ready kk_ready kn_done kn_ready kn_root kn_wide kq_done
            kq_ready lora_k lora_out lru_a lru_in lru_mm lru_root lru_t1 lru_th lru_tr lru_x2 lru_xc lru_y
            mix_ready mul_ready p_exp p_ready p_tok p_tr pv_done q_done q_out qk_done r_done r_out s_max
            s_out sc_y st_done st_out stored th_ready tn_done tn_init tn_out tn_part tr_done tr_out tt_done
            tt_init tt_out tt_part u_done u_out up_done up_landed v_tok v_tr vf_ready vn_done vn_out
            x_returned xw_ready y_out y_part yd_ready ym_done yq_ready""".split()
        on = {n: sem(n) for n in names}
        w_landed = [sem(f"w_landed{n}") for n in range(RAW)]
        block = ctx.enter_context(nc.Block())

        @block.sync
        def _(e):
            e.dma_start(raw[:, 0, :], wall[0]).then_inc(w_landed[0], 16)
            for k in range(KT):
                e.dma_start(x[:, k, :], xT[k]).then_inc(x_landed[k], 16)
            e.dma_start(raw[:, 1, :], wall[1]).then_inc(w_landed[1], 16)
            e.dma_start(cst[:, :], const_in[:, 0:CHUNK_CONSTS]).then_inc(const_landed, 16)
            e.dma_start(raw[:, 2, :], wall[2]).then_inc(w_landed[2], 16)
            e.dma_start(raw[:, 3, :], wall[3]).then_inc(w_landed[3], 16)
            e.dma_start(bd[:, :, :], lru_bd.rearrange("n p m -> p n m")).then_inc(bd_landed, 16)
            with e.Fori(0, (JOBS - RAW) // RAW) as i:
                for s in range(RAW):
                    e.wait_ge(lo_ready, i * RAW + (s + 1))
                    e.dma_start(raw[:, s, :], wall[i * RAW + (s + RAW)]).then_inc(w_landed[s], 16)
            for k in range(KT):
                e.wait_ge(job_out, J_RO + k + 1)
                e.dma_start(out[k], o_buf[:, k, :]).then_inc(on["stored"], 16)
            e.wait_ge(on["stored"], 16 * KT)
            for k in range(KT):
                e.wait_ge(spilled[k], 16)

        @block.gpsimd
        def _(e):
            for n, value in enumerate((RMS_EPS, GN_EPS, RW_GN_EPS)):
                e.memset(eps[:, n:n + 1], value).then_inc(eps_ready, 1)

            def low(j, s):
                e.wait_ge(hi_ready, j + 1)
                e.tensor_tensor(w_lo[:, s % SLOTS, :], raw[:, s % RAW, :], w_hi[:, s % SLOTS, :].bitcast(F32),
                                ALU.subtract).then_inc(lo_ready, 1)

            def lows(a, b):
                head = (-a) % RAW
                for j in range(a, a + head):
                    low(j, j)
                turns = (b - a - head) // RAW
                with e.Fori(0, turns) as i:
                    for s in range(RAW):
                        low(i * RAW + (a + head + s), s)
                for j in range(a + head + turns * RAW, b):
                    low(j, j)

            low(0, 0)
            low(1, 1)
            def multiply(src, norm):
                e.wait_ge(row_ready, norm)
                for k in range(1, KT, 2):
                    e.tensor_tensor(src[:, k, :], src[:, k, :], row[:, :], ALU.mult).then_inc(on["mul_ready"], 1)

            lows(2, J_MLP + 2)
            multiply(z, 2)
            lows(J_MLP + 2, J_RK + 2)
            multiply(m_acc, 4)
            for k in range(KT):
                e.wait_ge(on["h_ready"], k + 1)
                e.tensor_tensor(dx[:, k, 1:], h[:, k, 0:T - 1], h[:, k, 1:], ALU.subtract).then_inc(on["dx_ready"], 1)
            lows(J_RK + 2, J_RO + 2)
            with e.Fori(0, KT // 2) as i:
                for s in range(2):
                    e.wait_ge(on["cut_ready"], count((i, s), 1, 1))
                    e.wait_ge(on["ex_ready"], count((i, s), 2, 2))
                    e.tensor_tensor(ka[:, :, :], ka[:, :, :], exi[:, :, 1:129], ALU.mult).then_inc(on["f_part"], 1)
                    e.wait_ge(on["alpha_ready"], count((i, s), 1, 1))
                    e.tensor_tensor(kk, kk, ta[:, :], ALU.mult).then_inc(on["f_part"], 1)
                    e.wait_ge(on["f_part"], count((i, s), 2, 2))
                    e.tensor_tensor(be[:, :, :], be[:, :, :], exi[:, :, 1:129], ALU.mult).then_inc(on["f_ready"], 1)
                    e.wait_ge(on["gram_out"], count((i, s), NG + 2, NG + 2))
                    e.tensor_tensor(t_full[:, :, :], a_full[s][:, :, :], over_problems(const("pair")), ALU.mult)\
                        .then_inc(on["tn_part"], 1)
                    e.wait_ge(on["tn_part"], count((i, s), 1, 1))
                    e.tensor_tensor(t_full[:, :, :], t_full[:, :, :], over_problems(const("ident")), ALU.add)\
                        .then_inc(on["tn_init"], 1)
            lows(J_RO + 2, JOBS)

        @block.scalar
        def _(e):
            st = Steps(e, s_steps)

            def act(dst, src, func, done=None, **how):
                ins = e.activation(dst, src, func, **how)
                if done is None:
                    st(ins)
                else:
                    ins.then_inc(done, 1)

            def high(turn, s):
                e.wait_ge(w_landed[s], turn * 16 + 16)
                act(w_hi[:, s % SLOTS, :], raw[:, s, :], ACT.Copy, hi_ready)

            def rms(n):
                e.wait_ge(ms_done, n)
                act(rms_t[:, :], bank[2][:, 0:BT], ACT.Sqrt, ms_out, scale=1.0 / D, bias=eps[:, 0:1])

            def spread(dst, src, done):
                act(dst.rearrange("p (g f) -> p g f", f=HD),
                    src.rearrange("p a g -> p g a").broadcast_to([P, 2 * BT, HD]), ACT.Copy, done)

            def next_high(turn, s):
                e.wait_ge(job_done, turn * RAW + (s + 1))
                high(turn + (s + 2) // RAW, (s + 2) % RAW)

            e.dma_start(prm[:, :], par).then_inc(par_landed, 16)
            e.wait_ge(par_landed, 16)
            e.wait_ge(eps_ready, 3)
            high(0, 0)
            for k in range(KT):
                e.wait_ge(x_landed[k], 16)
                act(a_hi[:, k, :], x[:, k, :], ACT.Identity, ahi_ready, scale=par_col("pre_mix_g", k))
                act(sc[:, k, :], x[:, k, :], ACT.Square, sq_ready)
            high(0, 1)
            e.wait_ge(on["drv_in"], 1)
            act(drv[:, TMP + 2:TMP + 4], drv[:, TMP:TMP + 2], ACT.Exp, on["drv_exp"])
            rms(1)

            for n in range(J_OUT):
                next_high(n // RAW, n % RAW)
                if n in (2, 4):
                    i = (n - 2) // 2
                    e.wait_ge(job_out, 2 * i + 2)
                    act(sc[:, 10 + i, :], u[:, CG0 + 2 * i, :], ACT.Tanh, on["gate_tanh"], scale=0.5)

            def y_hi(tile, src, after, reached, scale=1.0):
                e.wait_ge(after, reached)
                act(b_hi[:, tile, :], src, ACT.Copy, bhi_ready, scale=scale)

            for i in range(2):
                y_hi(2 + i, sc[:, i, :], on["sc_y"], i + 1)
            e.dma_start(alibi, const_in[:, CHUNK_CONSTS:NCONST]).then_inc(on["alibi_landed"], 16)
            for i in range(2):
                e.wait_ge(on["conf_d"], i + 1)
                act(sc[:, 4 + i, :], sc[:, 10 + i, :], ACT.Square, on["conf_sq"])
            for n in range(2):
                e.wait_ge(on["v_tr"], n + 1)
                act(vtok[:, :, n * P:(n + 1) * P], bank[6][:, :].rearrange("p (b f) -> p b f", b=BT), ACT.Copy,
                    on["v_tok"])

            def lru_gates(i):
                e.wait_ge(on["lru_mm"], i + 1)
                act(sc[:, i, :], bank[0][:, :], ACT.Tanh, on["lru_tr"], bias=drv[:, LBA + i:LBA + i + 1], scale=0.5)
                act(sc[:, 2 + i, :], bank[1][:, :], ACT.Tanh, on["lru_tr"], bias=drv[:, LBX + i:LBX + i + 1], scale=0.5)

            def lru_decay(i):
                e.wait_ge(on["lru_tr"], 2 * i + 1)
                act(sc[:, 8 + i, :], sc[:, i, :], ACT.Exp, on["lru_a"], bias=drv[:, SP4 + i:SP4 + i + 1],
                    scale=drv[:, SP4 + i:SP4 + i + 1])
                e.wait_ge(on["lru_a"], i + 1)
                act(sc[:, i, :], sc[:, i, :], ACT.Tanh, on["lru_t1"], bias=drv[:, SP2 + i:SP2 + i + 1],
                    scale=drv[:, SP2 + i:SP2 + i + 1])

            def other_mixers(stage):
                if stage == 1:
                    e.wait_ge(on["conf_var"], 1)
                    act(cn_t[:, :, :].rearrange("p i g -> p (i g)"), bank[2][:, 0:4 * BT], ACT.Sqrt, on["conf_ve"],
                        scale=1.0 / 64, bias=eps[:, 1:2])
                elif stage == 3:
                    for i in range(2):
                        act(gelu[i], u[:, LG0 + i, :], ACT.Square, on["lru_x2"])
                elif stage == 5:
                    for i in range(2):
                        e.wait_ge(on["conf_n"], i + 1)
                        act(sc[:, 4 + i, :], sc[:, 10 + i, :], ACT.Tanh, on["conf_t"], scale=0.5)
                elif stage == 6:
                    lru_gates(0)
                elif stage == 7:
                    for i in range(2):
                        y_hi(i, sc[:, 10 + i, :], on["conf_y"], i + 1, scale=0.5)
                    lru_decay(0)
                elif stage == 8:
                    lru_gates(1)
                    lru_decay(1)
                elif stage == 9:
                    for i in range(2):
                        e.wait_ge(on["lru_t1"], i + 1)
                        act(sc[:, 6 + i, :], sc[:, i, :], ACT.Sqrt, on["lru_root"])
                    for i in range(2):
                        e.wait_ge(on["lru_in"], i + 1)
                        act(gelu[i], gelu[i], ACT.Tanh, on["lru_th"], scale=math.sqrt(2.0 / math.pi))
                elif stage == 15:
                    for i in range(2):
                        y_hi(6 + i, sc[:, 10 + i, :], on["lru_y"], i + 1, scale=0.25)

            for n, (pair, qt, hh) in enumerate(HEADS):
                keys = (qt + 1) * P
                e.wait_ge(on["s_max"], n + 1)
                if n >= 2:
                    e.wait_ge(on["p_tr"], n - 1)
                act(u[:, 2 + n % 2, 0:keys], u[:, n % 2, 0:keys], ACT.Exp, on["p_exp"], bias=stat[:, n:n + 1],
                    accum_out=stat[:, 16 + n:17 + n])
                other_mixers(n)
                e.wait_ge(on["p_tr"], n + 1)
                if n >= 2:
                    e.wait_ge(on["pv_done"], n - 1)
                act(u[:, V0 + n % 2, 0:keys], bank[5 + n % 2][:, 0:keys], ACT.Copy, on["p_tok"])
                if qt == BT - 1 and hh == 1:
                    e.wait_ge(on["pv_done"], n + 1)
                    act(b_hi[:, 4 + pair, :], bank[7][:, :], ACT.Copy, bhi_ready)

            for n in range(KT):
                next_high((J_OUT + n) // RAW, n % RAW)
                act(sq[:, n, :], bank[n % 2][:, :], ACT.Square, sq_ready)
                act(z[:, n, :], bank[n % 2][:, :], ACT.Copy, job_out)
            rms(2)
            for k in range(KT):
                e.wait_ge(x_ready, k + 1)
                act(a_hi[:, k, :], x[:, k, :], ACT.Identity, ahi_ready, scale=par_col("pre_mlp_g", k))
                act(sq[:, k, :], x[:, k, :], ACT.Square, sq_ready)

            def mlp(grp, last):
                job = grp * (2 * KT)
                for t in range(KT):
                    next_high(grp * (2 * KT // RAW) + (J_MLP + t) // RAW, t % RAW)
                    e.wait_ge(job_out, job + (J_MLP + t + 1))
                    e.wait_ge(blo_ready, grp * KT + (KT + t - 1))
                    act(h_tmp[:, 2 + t % 2, :], h_tmp[:, t % 2, :], ACT.Square, on["hq_ready"])
                    e.wait_ge(on["hq_ready"], grp * KT + (t + 1))
                    act(b_hi[:, t, :], h_tmp[:, 2 + t % 2, :], ACT.Copy, bhi_ready)
                for t in range(KT):
                    next_high(grp * (2 * KT // RAW) + (J_MLP + KT + t) // RAW, t % RAW)
                    if last:
                        e.wait_ge(job_out, job + (J_MLP + KT + t + 1))
                        act(sq[:, t, :], m_acc[:, t, :], ACT.Square, sq_ready)

            rms(3)
            with e.Fori(0, FG - 1) as grp:
                mlp(grp, False)
            mlp(FG - 1, True)

            e.dma_start(w_lor[:, :, :], w_lora).then_inc(lora_landed, 16)
            rms(4)
            for k in range(KT):
                e.wait_ge(x_ready, KT + k + 1)
                act(sq[:, k, :], x[:, k, :], ACT.Square, sq_ready)
                e.dma_start(x_spill[k], x[:, k, :]).then_inc(spilled[k], 16)
            rms(5)

            def mix_hi(dst, n, t):
                e.wait_ge(on["mix_ready"], n * KT + t + 1)
                act(dst[:, t, :], mix[:, t % 2, :], ACT.Copy, ahi_ready if dst is a_hi else bhi_ready)

            for t in range(KT):
                mix_hi(a_hi, 0, t)
            for n, (first, store, following) in enumerate(((J_RK, rk_k, b_hi), (J_RR, rk_r, a_hi), (J_RV, rk_v, b_hi))):
                for t in range(KT):
                    next_high((first + t) // RAW, t % RAW)
                    act(store[:, t, :], bank[t % 2][:, :], ACT.Copy, job_out)
                    if n == 2 and t == KT // 2:
                        e.wait_ge(on["lora_k"], 2 * KT)
                        act(lora[0:64, :], bank[2][0:64, :], ACT.Tanh, on["lora_out"])
                        act(lora[64:128, :], bank[3][64:128, :], ACT.Copy, on["lora_out"])
                    early = ((0, 1), (2,), (3,), (4,), (5,), (6,), (7,), ())
                    late = ((), (), (), (), (0, 1, 2), (3, 4, 5), (6, 7), ())
                    for ahead in (late if n == 2 else early)[t]:
                        mix_hi(following, n + 1, ahead)
            for t in range(KT):
                next_high((J_RG + t) // RAW, t % RAW)
                if t >= 2:
                    e.wait_ge(job_out, J_RG + t - 1)
                else:
                    e.wait_ge(blo_ready, 56)
                act(mix[:, t % 2, :], bank[t % 2][:, :], ACT.Tanh, on["g_tanh"], scale=0.5)
                if t >= 2:
                    e.wait_ge(on["kq_done"], t - 1)
                c = RW + t * 8 + RW_KK
                act(key_sq[:, t % 2, :], rk_k[:, t, :], ACT.Square, on["kq_ready"], scale=drv[:, c:c + 1])
            e.wait_ge(on["kq_done"], KT)
            act(kn_t[:, :, :].rearrange("p i g -> p (i g)"), bank[4][:, 0:64], ACT.Sqrt, on["kn_root"])

            e.wait_ge(on["kn_ready"], 1)
            e.wait_ge(job_out, J_RO)

            def prepare(t, before):
                s, tile = t[1] % 2, bass.ds(index(t), 1)
                if t[1]:
                    e.wait_ge(on["gram_out"], count(t, NG + 2, 0))
                e.dma_start(w_up[:, :], lora_up[tile].rearrange("a p m -> p (a m)")).then_inc(on["up_landed"], 16)
                act(cp[:, :], drv[:, RW:RW + 64].rearrange("p (k c) -> p k c", k=KT)[:, tile, :].rearrange(
                    "p a c -> p (a c)"), ACT.Copy, on["cp_ready"])
                spread(wide[:, :], kn_t[:, tile, :], on["kn_wide"])
                e.wait_ge(on["cp_ready"], count(t, 1, 1))
                act(kk, rk_k[:, tile, :].rearrange("p a t -> p (a t)"), ACT.Identity, on["kk_ready"],
                    scale=cp[:, RW_KK:RW_KK + 1])
                e.wait_ge(on["up_done"], count(t, 1, 1))
                act(thx[:, :, 1:129], bank[0][:, :].rearrange("p (b t) -> p b t", b=BT), ACT.Tanh, on["th_ready"],
                    bias=cp[:, RW_W0:RW_W0 + 1], scale=0.5)
                act(ta[:, :], bank[1][:, :], ACT.Tanh, on["th_ready"], bias=cp[:, RW_A0:RW_A0 + 1], scale=0.5)
                if before:
                    squares(before)
                e.wait_ge(on["kn_done"], count(t, 1, 1))
                act(wide[:, :], rk_v[:, tile, :].rearrange("p a t -> p (a t)"), ACT.Copy, on["vf_ready"])
                e.wait_ge(on["cs_ready"], count(t, 1, 1))
                act(exi[:, :, :], thx[:, :, :], ACT.Exp, on["ex_ready"], scale=-DECAY)
                e.wait_ge(on["ex_ready"], count(t, 2, 1))
                act(ex[:, :, :], thx[:, :, :], ACT.Exp, on["ex_ready"], scale=DECAY)

                def transposed(n, dst):
                    e.wait_ge(on["tr_done"], count(t, 3, n + 1))
                    act(dst[:, :, :], bank[(0, 2, 0)[n]][:, :].rearrange("p (b f) -> p b f", b=BT), ACT.Copy,
                        on["tr_out"])

                transposed(0, v_ts[s])
                if before:
                    deviation(before)
                e.wait_ge(on["f_ready"], count(t, 1, 1))
                for hh in range(2):
                    rows = slice(64 * hh, 64 * hh + 64)
                    act(be_h[rows, hh, :, :], be[rows, :, :], ACT.Copy, on["halves_ready"])
                    act(ka_h[rows, hh, :, :], ka[rows, :, :], ACT.Copy, on["halves_ready"])
                transposed(1, be_ts[s])
                transposed(2, ka_ts[s])
                if before:
                    affine(before)

            def output(t):
                e.wait_ge(on["y_part"], count(t, BT, BT))
                act(ys[:, :], bank[7][:, :], ACT.Copy, on["y_out"])

            def squares(t):
                tile = bass.ds(index(t), 1)
                e.wait_ge(on["yd_ready"], count(t, 1, 1))
                act(t2[:, :], ys[:, :], ACT.Square, on["yq_ready"])
                act(cp_end[:, :], drv[:, RW:RW + 64].rearrange("p (k c) -> p k c", k=KT)[:, tile, :].rearrange(
                    "p a c -> p (a c)"), ACT.Copy, on["end_ready"])

            def deviation(t):
                e.wait_ge(on["vn_done"], count(t, 1, 1))
                act(gn_t[:, :], bank[7][:, 0:NG], ACT.Sqrt, on["vn_out"], scale=1.0 / HD, bias=eps[:, 2:3])

            def affine(t):
                e.wait_ge(on["end_ready"], count(t, 1, 1))
                e.wait_ge(on["gn_mul"], count(t, 1, 1))
                act(ys[:, :], ys[:, :], ACT.Identity, on["gn_aff"], scale=cp_end[:, RW_GW:RW_GW + 1],
                    bias=cp_end[:, RW_GB:RW_GB + 1])

            def both(t, before, following):
                if following:
                    prepare(following, before)
                else:
                    squares(before)
                    deviation(before)
                    affine(before)
                if before:
                    e.wait_ge(on["gated"], count(before, 1, 1))
                output(t)

            prepare((0, 0), None)
            both((0, 0), None, (0, 1))
            with e.Fori(0, KT // 2 - 1) as i:
                both((i, 1), (i, 0), (i, 2))
                both((i, 2), (i, 1), (i, 3))
            both((0, KT - 1), (0, KT - 2), None)
            squares((0, KT - 1))

            def gated_hi(t):
                e.wait_ge(on["gated"], t + 1)
                act(b_hi[:, t, :], rk_k[:, t, :], ACT.Copy, bhi_ready)

            e.dma_start(x_back[:, :, :], x_spill.rearrange("k p t -> p k t")).then_inc(on["x_returned"], 16)
            gated_hi(0)
            gated_hi(1)
            deviation((0, KT - 1))
            gated_hi(2)
            affine((0, KT - 1))
            for t in range(3, KT):
                gated_hi(t)

            for n in range(KT - 2):
                next_high((J_RO + n) // RAW, n % RAW)

        @block.vector
        def _(e):
            v = Steps(e, v_steps)
            tt, ts, stt = e.tensor_tensor, e.tensor_scalar, e.scalar_tensor_tensor

            v(e.memset(zpad[:, :, 0:CONF_K - 1], 0.0))
            v(e.memset(xpad[:, :, 0:LRU_K - 1], 0.0))
            v(e.memset(cpad[:, :, 0:SC_K - 1], 0.0))
            e.wait_ge(par_landed, 16)
            lam = prm[:, PCOL["lam"]:PCOL["lam"] + 2]
            nl, ml, ee, s1, s2, pp = (drv[:, TMP + 2 * n:TMP + 2 * n + 2] for n in (5, 0, 1, 2, 3, 4))
            v(ts(nl, lam, -1.0, None, ALU.mult))
            tt(ml, nl, lam, ALU.min).then_inc(on["drv_in"], 1)
            v(ts(drv[:, CW:CW + 62], prm[:, PCOL["conf_w"]:PCOL["conf_w"] + 62], 0.5, None, ALU.mult))
            v(ts(drv[:, LBA:LBA + 4], prm[:, PCOL["lru_ba"]:PCOL["lru_ba"] + 4], 0.5, None, ALU.mult))
            v(e.tensor_copy(drv[:, RW:RW + 64], prm[:, PCOL["rw"]:PCOL["rw"] + 64]))
            rw = drv[:, RW:RW + 64].rearrange("p (k c) -> p k c", k=KT)
            v(ts(rw[:, :, RW_W0:RW_A0 + 1], rw[:, :, RW_W0:RW_A0 + 1], 0.5, None, ALU.mult))
            v(ts(rw[:, :, RW_OMK:RW_OMK + 1], rw[:, :, RW_KA:RW_KA + 1], -0.5, 1.0, ALU.mult, ALU.add))
            v(ts(rw[:, :, RW_KA:RW_KA + 1], rw[:, :, RW_KA:RW_KA + 1], 0.5, None, ALU.mult))
            for k in range(KT):
                e.wait_ge(ahi_ready, k + 1)
                stt(a_lo[:, k, :], x[:, k, :], par_col("pre_mix_g", k), a_hi[:, k, :].bitcast(F32), ALU.mult,
                    ALU.subtract).then_inc(alo_ready, 1)
            e.wait_ge(on["drv_exp"], 1)
            v(ts(s1, ee, 2.0, None, ALU.add))
            v(e.reciprocal(s1, s1))
            v(tt(s1, s1, ee, ALU.mult))
            v(tt(s2, s1, s1, ALU.mult))
            v(ts(pp, s2, 1.0 / 17, None, ALU.mult))
            for odd in (15, 13, 11, 9, 7, 5, 3):
                v(stt(pp, pp, 1.0 / odd, s2, ALU.add, ALU.mult))
            v(stt(pp, pp, 1.0, s1, ALU.add, ALU.mult))
            v(ts(nl, nl, 0.0, None, ALU.max))
            v(ts(nl, nl, 2.0, None, ALU.mult))
            v(stt(drv[:, SP2:SP2 + 2], pp, 4.0, nl, ALU.mult, ALU.add))
            ts(drv[:, SP4:SP4 + 2], drv[:, SP2:SP2 + 2], -2.0, None, ALU.mult).then_inc(on["drv_ready"], 1)

            def spread(dst, src, width, done):
                groups = T // width
                e.tensor_copy(dst.rearrange("p (g f) -> p g f", f=width),
                              src.rearrange("p (g f) -> p g f", f=1).broadcast_to([P, groups, width])).then_inc(done, 1)

            def inverse_rms(n):
                e.wait_ge(ms_out, n)
                v(e.reciprocal(rms_t[:, :], rms_t[:, :]))
                spread(wide[:, :], rms_t[:, :], P, wide_ready)
                e.wait_ge(row_done, n)
                e.tensor_copy(row[:, :], bank[2][:, :]).then_inc(row_ready, 1)
                e.wait_ge(row_ready, n)

            inverse_rms(1)

            def tap(n):
                t, i = n // 2, n % 2
                w = drv[:, CW + i * CONF_K + t:CW + i * CONF_K + t + 1]
                src, acc = zpad[:, i, t:t + T], sc[:, 8 + i, :]
                if t == 0:
                    v(ts(acc, src, w, par_col("conf_b", i), ALU.mult, ALU.add))
                else:
                    v(stt(acc, src, w, acc, ALU.mult, ALU.add))

            taps = 0
            for n in range(J_OUT):
                e.wait_ge(job_done, n + 1)
                dst = u[:, n, :]
                if n in (LX0, LX1):
                    dst = xpad[:, n - LX0, LRU_K - 1:]
                if n in (Q0, Q1):
                    stt(dst, bank[n % 2][:, :], HD ** -0.5, row[:, :], ALU.mult, ALU.mult).then_inc(job_out, 1)
                else:
                    tt(dst, bank[n % 2][:, :], row[:, :], ALU.mult).then_inc(job_out, 1)
                if n in (3, 5):
                    i = (n - 3) // 2
                    e.wait_ge(on["gate_tanh"], i + 1)
                    v(stt(zpad[:, i, CONF_K - 1:], sc[:, 10 + i, :], 1.0, u[:, CV0 + 2 * i, :], ALU.add, ALU.mult))
                if n > 5:
                    for _ in range(5 if n < J_OUT - 1 else 2 * CONF_K):
                        if taps < 2 * CONF_K:
                            tap(taps)
                            taps += 1
            e.wait_ge(job_out, J_OUT)

            for i in range(2):
                v(tt(cpad[:, i, SC_K - 1:], u[:, SC0 + 2 * i, :], u[:, SX0 + 2 * i, :], ALU.mult))
                for t in range(SC_K):
                    w = par_col("sconv_w", i * SC_K + t)
                    if t == 0:
                        v(ts(sc[:, i, :], cpad[:, i, 0:T], w, None, ALU.mult))
                    else:
                        v(stt(sc[:, i, :], cpad[:, i, t:t + T], w, sc[:, i, :], ALU.mult, ALU.add))
                tt(sc[:, i, :], sc[:, i, :], u[:, SB0 + i, :], ALU.mult).then_inc(on["sc_y"], 1)

            def y_lo(tile, src, nth, scale=None):
                e.wait_ge(bhi_ready, nth)
                hi = b_hi[:, tile, :].bitcast(F32)
                if scale is None:
                    tt(b_lo[:, tile, :], src, hi, ALU.subtract).then_inc(blo_ready, 1)
                else:
                    stt(b_lo[:, tile, :], src, scale, hi, ALU.mult, ALU.subtract).then_inc(blo_ready, 1)

            for i in range(2):
                e.wait_ge(on["conf_mean"], i + 1)
                tt(sc[:, 10 + i, :], sc[:, 8 + i, :], bank[i][:, :], ALU.subtract).then_inc(on["conf_d"], 1)

            def lru_conv(i):
                xc = u[:, LX0 + i, :]
                for t in range(LRU_K):
                    w, src = par_col("lru_w", i * LRU_K + t), xpad[:, i, t:t + T]
                    if t == 0:
                        v(ts(xc, src, w, par_col("lru_b", i), ALU.mult, ALU.add))
                    elif t < LRU_K - 1:
                        v(stt(xc, src, w, xc, ALU.mult, ALU.add))
                    else:
                        stt(xc, src, w, xc, ALU.mult, ALU.add).then_inc(on["lru_xc"], 1)

            def lru_scan_in(i):
                ti, root, a = (sc[:, n + i, :] for n in (2, 6, 8))
                e.wait_ge(on["lru_root"], i + 1)
                v(stt(ti, ti, 1.0, u[:, LX0 + i, :], ALU.add, ALU.mult))
                v(stt(root, a, 1.0, root, ALU.add, ALU.mult))
                v(tt(ti, ti, root, ALU.mult))

            def other_mixers(stage):
                if stage == 0:
                    for i in range(2):
                        y_lo(2 + i, sc[:, i, :], i + 1)
                elif stage in (1, 3):
                    lru_conv(stage // 2)
                elif stage == 2:
                    e.wait_ge(on["conf_ve"], 1)
                    v(e.reciprocal(cn_t[:, :, :], cn_t[:, :, :]))
                    for i in range(2):
                        spread(sc[:, 6 + i, :], cn_t[:, i, :], HD, on["conf_rs"])
                elif stage == 4:
                    for i in range(2):
                        e.wait_ge(on["conf_row"], i + 1)
                        v(tt(sc[:, 10 + i, :], sc[:, 10 + i, :], bank[i][:, :], ALU.mult))
                        ts(sc[:, 10 + i, :], sc[:, 10 + i, :], par_col("gn_g", i), par_col("gn_b", i), ALU.mult,
                           ALU.add).then_inc(on["conf_n"], 1)
                elif stage == 5:
                    for i in range(2):
                        e.wait_ge(on["lru_x2"], i + 1)
                        v(ts(gelu[i], gelu[i], 0.044715, 1.0, ALU.mult, ALU.add))
                        tt(gelu[i], gelu[i], u[:, LG0 + i, :], ALU.mult).then_inc(on["lru_in"], 1)
                elif stage == 6:
                    for i in range(2):
                        e.wait_ge(on["conf_t"], i + 1)
                        stt(sc[:, 10 + i, :], sc[:, 4 + i, :], 1.0, sc[:, 10 + i, :], ALU.add, ALU.mult)\
                            .then_inc(on["conf_y"], 1)
                elif stage == 7:
                    for i in range(2):
                        y_lo(i, sc[:, 10 + i, :], 3 + i, 0.5)
                elif stage in (10, 12):
                    lru_scan_in(stage // 2 - 5)
                elif stage in (11, 13):
                    i = stage // 2 - 5
                    v(e.tensor_tensor_scan(sc[:, 10 + i, :], sc[:, 8 + i, :], sc[:, 2 + i, :], 0.0, ALU.mult, ALU.add))
                elif stage == 14:
                    for i in range(2):
                        root, hh = sc[:, 6 + i, :], sc[:, 10 + i, :]
                        e.wait_ge(on["lru_th"], i + 1)
                        v(stt(root, gelu[i], 1.0, u[:, LG0 + i, :], ALU.add, ALU.mult))
                        tt(hh, hh, root, ALU.mult).then_inc(on["lru_y"], 1)
                elif stage == 15:
                    for i in range(2):
                        y_lo(6 + i, sc[:, 10 + i, :], 6 + i, 0.25)

            e.wait_ge(on["alibi_landed"], 16)
            for n, (pair, qt, hh) in enumerate(HEADS):
                keys = (qt + 1) * P
                s = u[:, n % 2, 0:keys]
                e.wait_ge(on["qk_done"], n + 1)
                if n >= 2:
                    e.wait_ge(on["p_exp"], n - 1)
                slope = 2.0 ** (-8.0 * (2 * pair + hh + 1) / ATT_HEADS)
                stt(s, alibi[:, 384 - qt * P:384 - qt * P + keys], slope, bank[3 + n % 2][:, 0:keys], ALU.mult,
                    ALU.add).then_inc(on["s_out"], 1)
                e.wait_ge(on["s_out"], n + 1)
                e.tensor_reduce(stat[:, n:n + 1], s, AX_X, ALU.max, negate=True).then_inc(on["s_max"], 1)
                other_mixers(n)
                e.wait_ge(on["p_exp"], n + 1)
                v(e.reciprocal(stat[:, 16 + n:17 + n], stat[:, 16 + n:17 + n]))
                ts(u[:, 2 + n % 2, 0:keys], u[:, 2 + n % 2, 0:keys], stat[:, 16 + n:17 + n], None,
                   ALU.mult).then_inc(on["p_ready"], 1)
                if qt == BT - 1 and hh == 1:
                    y_lo(4 + pair, bank[7][:, :], (5, 8)[pair])

            e.wait_ge(job_done, J_OUT + 1)
            v(e.memset(m_acc[:, :, :], 0.0))

            def add_normed(src, gain, norm, first, after):
                inverse_rms(norm)
                for k in range(KT):
                    if k % 2:
                        e.wait_ge(on["mul_ready"], (norm // 2 - 1) * (KT // 2) + k // 2 + 1)
                    else:
                        v(tt(src[:, k, :], src[:, k, :], row[:, :], ALU.mult))
                    stt(x[:, k, :], src[:, k, :], par_col(gain, k), x[:, k, :], ALU.mult, ALU.add).then_inc(x_ready, 1)
                    if k:
                        after(k - 1)
                after(KT - 1)

            def mlp_in_lo(k):
                e.wait_ge(ahi_ready, KT + k + 1)
                stt(a_lo[:, k, :], x[:, k, :], par_col("pre_mlp_g", k), a_hi[:, k, :].bitcast(F32), ALU.mult,
                    ALU.subtract).then_inc(alo_ready, 1)

            add_normed(z, "post_mix_g", 2, 0, mlp_in_lo)
            inverse_rms(3)

            def mlp_out_lo(grp, t):
                e.wait_ge(bhi_ready, grp * KT + (KT + t + 1))
                tt(b_lo[:, t, :], h_tmp[:, 2 + t % 2, :], b_hi[:, t, :].bitcast(F32), ALU.subtract)\
                    .then_inc(blo_ready, 1)

            with e.Fori(0, FG) as grp:
                for t in range(KT):
                    e.wait_ge(job_done, grp * (2 * KT) + (J_MLP + t + 1))
                    stt(h_tmp[:, t % 2, :], bank[t % 2][:, :], 0.0, row[:, :], ALU.max, ALU.mult)\
                        .then_inc(job_out, 1)
                    if t:
                        mlp_out_lo(grp, t - 1)
                mlp_out_lo(grp, KT - 1)
                for t in range(KT):
                    e.wait_ge(job_done, grp * (2 * KT) + (J_MLP + KT + t + 1))
                    tt(m_acc[:, t, :], m_acc[:, t, :], bank[t % 2][:, :], ALU.add).then_inc(job_out, 1)
            e.wait_ge(job_out, J_RK)

            add_normed(m_acc, "post_mlp_g", 4, KT, lambda k: None)
            inverse_rms(5)
            e.wait_ge(x_ready, 2 * KT)


            def h_tile(k):
                v(ts(dx[:, k, 0:1], x[:, k, 0:1], par_col("l0_norm", k), row[:, 0:1], ALU.mult, ALU.mult))
                v(ts(dx[:, k, 0:1], dx[:, k, 0:1], -1.0, None, ALU.mult))
                e.wait_ge(spilled[k], 16)
                stt(h[:, k, :], x[:, k, :], par_col("l0_norm", k), row[:, :], ALU.mult, ALU.mult)\
                    .then_inc(on["h_ready"], 1)

            def mix_lo(n, hi, lo, base, t):
                e.wait_ge(ahi_ready if hi is a_hi else bhi_ready, base + t + 1)
                tt(lo[:, t, :], mix[:, t % 2, :], hi[:, t, :].bitcast(F32), ALU.subtract)\
                    .then_inc(alo_ready if hi is a_hi else blo_ready, 1)

            def mixes(n, which, hi, lo, base):
                if n == 0:
                    h_tile(0)
                for t in range(KT):
                    if n == 0:
                        if t < KT - 1:
                            h_tile(t + 1)
                        e.wait_ge(on["dx_ready"], t + 1)
                    if t >= 2:
                        e.wait_ge(alo_ready if hi is a_hi else blo_ready, base + t - 1)
                    stt(mix[:, t % 2, :], dx[:, t, :], par_col("mu", which * KT + t), h[:, t, :], ALU.mult,
                        ALU.add).then_inc(on["mix_ready"], 1)
                    if t:
                        mix_lo(n, hi, lo, base, t - 1)
                mix_lo(n, hi, lo, base, KT - 1)

            mixes(0, 2, a_hi, a_lo, 2 * KT)
            e.wait_ge(alo_ready, 3 * KT)
            mixes(1, 0, b_hi, b_lo, KT + FG * KT)
            e.wait_ge(blo_ready, KT + FG * KT + KT)
            e.wait_ge(job_done, J_RR)
            mixes(2, 3, a_hi, a_lo, 3 * KT)
            e.wait_ge(alo_ready, 4 * KT)
            for t in range(KT):
                for s, which in ((0, 1), (1, 4)):
                    if t:
                        e.wait_ge(on["lora_k"], 2 * t - 1 + s)
                    stt(mix[:, s, :], dx[:, t, :], par_col("mu", which * KT + t), h[:, t, :], ALU.mult,
                        ALU.add).then_inc(on["xw_ready"], 1)
            e.wait_ge(job_done, J_RV)
            e.wait_ge(on["lora_k"], 2 * KT)
            mixes(3, 5, b_hi, b_lo, KT + FG * KT + KT)
            e.wait_ge(blo_ready, 56)
            for t in range(KT):
                e.wait_ge(on["g_tanh"], t + 1)
                stt(rk_g[:, t, :], mix[:, t % 2, :], 1.0, bank[t % 2][:, :], ALU.add, ALU.mult).then_inc(job_out, 1)
            e.wait_ge(job_out, J_RO)
            e.wait_ge(on["kn_root"], 1)
            flat_kn = kn_t[:, :, :].rearrange("p i g -> p (i g)")
            v(ts(flat_kn, flat_kn, 1e-12, None, ALU.max))
            e.reciprocal(flat_kn, flat_kn).then_inc(on["kn_ready"], 1)

            v(e.memset(be_h[:, :, :, :], 0.0))
            e.memset(ka_h[:, :, :, :], 0.0).then_inc(on["halves_ready"], 1)

            def blocks(a):
                return a.rearrange("p (b t) -> p b t", b=BT)

            def flat(store, t):
                return store[:, bass.ds(index(t), 1), :].rearrange("p a t -> p (a t)")

            def decays(t):
                v(e.memset(thx[:, :, 0:1], -1.0))
                e.wait_ge(on["th_ready"], count(t, 2, 1))
                v(ts(thx[:, :, :], thx[:, :, :], 1.0, None, ALU.add))
                v(e.tensor_tensor_scan(cs[:, :, :].rearrange("p b t -> p (b t)"), const("reset"),
                                       thx[:, :, :].rearrange("p b t -> p (b t)"), 0.0, ALU.mult, ALU.add))
                tt(thx[:, :, :], cs[:, :, :], cs[:, :, 64:65].broadcast_to([P, BT, 129]), ALU.subtract)\
                    .then_inc(on["cs_ready"], 1)

            def keys(t):
                e.wait_ge(on["th_ready"], count(t, 2, 2))
                v(ts(t1[:, :], ta[:, :], cp[:, RW_KA:RW_KA + 1], cp[:, RW_OMK:RW_OMK + 1], ALU.mult, ALU.add))
                v(tt(kmod, t1[:, :], flat(rk_k, t), ALU.mult))
                v(ts(ta[:, :], ta[:, :], 0.5, 0.5, ALU.mult, ALU.add))
                stt(t1[:, :], flat(rk_r, t), cp[:, RW_RK:RW_RK + 1], kmod, ALU.mult, ALU.mult)\
                    .then_inc(on["cut_ready"], 1)

            def kappa_rho(t):
                s = t[1] % 2
                e.wait_ge(on["ex_ready"], count(t, 2, 2))
                v(tt(ars[s][:, :, 1, :], blocks(flat(rk_r, t)), ex[:, :, 1:129], ALU.mult))
                v(tt(fade[:, s, 0:BT - 1], ex[:, 0:BT - 1, 128], exi[:, 1:BT, 0], ALU.mult))

            def alpha_beta(t):
                e.wait_ge(on["kn_done"], count(t, 1, 1))
                v(tt(kk, kk, bank[2][:, :], ALU.mult))
                stt(ars[t[1] % 2][:, :, 0, :], blocks(kk), -1.0, ex[:, :, 0:128], ALU.mult, ALU.mult)\
                    .then_inc(on["alpha_ready"], 1)

            def bonus(t):
                e.wait_ge(on["bk_done"], count(t, 1, 1))
                tt(flat(rk_v, t), flat(rk_v, t), bank[1][:, :], ALU.mult).then_inc(on["bonus_ready"], 1)

            def gram(t, n):
                s, src = t[1] % 2, bank[(n + 1) % 3]
                e.wait_ge(on["gram_done"], count(t, NG + 2, n + 1))
                if n < NG:
                    tt(grams[s][:, n % 2 * BT + n // 2, :, :].rearrange("p (a c) t -> p a (c t)", a=2),
                       src[:, :].rearrange("p (a c) -> p a c", a=2),
                       const("gram").rearrange("p (a c) -> p a c", a=1).broadcast_to([P, 2, 2 * P]),
                       ALU.mult).then_inc(on["gram_out"], 1)
                else:
                    part = slice((n - NG) * BT, (n - NG) * BT + BT)
                    tt(a_full[s][:, part, :], blocks(src[:, :]), over_blocks(const("lower")), ALU.mult)\
                        .then_inc(on["gram_out"], 1)

            def pairs(t, part):
                tta = grams[t[1] % 2][:, :, 0, :]
                if part == 0:
                    e.wait_ge(on["gram_out"], count(t, NG + 2, NG))
                    tt(tta, tta, over_problems(const("pairT")), ALU.mult).then_inc(on["tt_part"], 1)
                    return
                e.wait_ge(on["tt_part"], count(t, 1, 1))
                tt(tta, tta, over_problems(const("ident")), ALU.add).then_inc(on["tt_init"], 1)

            def last_q(t):
                for hh in range(2):
                    e.wait_ge(on["q_done"], count(t, 2 * LEVELS, 2 * LEVELS - 2 + hh + 1))
                    e.tensor_copy(q_full[LOW, BT * hh:BT * hh + BT, HIGH], blocks(bank[BANKS_AT[-1][hh]][:, :])[LOW, :, HIGH])\
                        .then_inc(on["q_out"], 1)

            def last_t(t):
                q0, q1, t0, n0 = BANKS_AT[-1]
                for hh in range(2):
                    part = slice(BT * hh, BT * hh + BT)
                    e.wait_ge(on["tt_done"], count(t, 2 * LEVELS, 2 * LEVELS - 2 + hh + 1))
                    e.tensor_copy(grams[t[1] % 2][LOW, part, 0, HIGH], blocks(bank[(t0, q0)[hh]][:, :])[LOW, :, HIGH])\
                        .then_inc(on["tt_out"], 1)

            def level_q(t, lv):
                for hh in range(2):
                    e.wait_ge(on["q_done"], count(t, 2 * LEVELS, 2 * lv + hh + 1))
                    tt(q_full[:, BT * hh:BT * hh + BT, :], blocks(bank[BANKS_AT[lv][hh]][:, :]),
                       over_blocks(const("level", lv)), ALU.mult).then_inc(on["q_out"], 1)

            def level_t(t, lv):
                q0, q1, t0, n0 = BANKS_AT[lv]
                for hh in range(2):
                    part = slice(BT * hh, BT * hh + BT)
                    tta = grams[t[1] % 2][:, part, 0, :]
                    e.wait_ge(on["tt_done"], count(t, 2 * LEVELS, 2 * lv + hh + 1))
                    tt(tta, tta, blocks(bank[(t0, q0)[hh]][:, :]), ALU.add).then_inc(on["tt_out"], 1)
                    e.wait_ge(on["tn_done"], count(t, 2 * LEVELS - 2, 2 * lv + hh + 1))
                    tt(t_full[:, part, :], t_full[:, part, :], blocks(bank[(n0, q1)[hh]][:, :]), ALU.add)\
                        .then_inc(on["tn_out"], 1)

            def state(t, b, following):
                if b == 0:
                    e.memset(s_t[:, :], 0.0).then_inc(on["st_out"], 1)
                e.wait_ge(on["r_done"], count(t, BT, b + 1))
                e.tensor_copy(r_s[:, :], bank[3][:, 0:P]).then_inc(on["r_out"], 1)
                if following and b == BT - 1:
                    pairs(following, 1)
                if following and GRAMS_AT[b] < NG + 2:
                    gram(following, GRAMS_AT[b])
                e.wait_ge(on["u_done"], count(t, BT, b + 1))
                e.tensor_copy(u_s[:, :], bank[5][:, 0:P]).then_inc(on["u_out"], 1)
                if following:
                    for n in range(GRAMS_AT[b] + 1, GRAMS_AT[b + 1])[:1]:
                        gram(following, n)
                if b < BT - 1:
                    e.wait_ge(on["st_done"], count(t, BT - 1, b + 1))
                    v(tt(s_new[:, :], s_t[:, :], bank[4][:, 0:P], ALU.add))
                    stt(s_t[:, :], s_new[:, :], fade[:, t[1] % 2, b:b + 1], const("blk"), ALU.mult, ALU.mult)\
                        .then_inc(on["st_out"], 1)
                if following:
                    for n in range(GRAMS_AT[b] + 2, GRAMS_AT[b + 1]):
                        gram(following, n)
                if following and b == BT - 2:
                    pairs(following, 0)

            def centre(t):
                e.wait_ge(on["ym_done"], count(t, 1, 1))
                tt(ys[:, :], ys[:, :], bank[7][:, :], ALU.subtract).then_inc(on["yd_ready"], 1)

            def inverse_deviation(t):
                e.wait_ge(on["vn_out"], count(t, 1, 1))
                v(e.reciprocal(gn_t[:, :], gn_t[:, :]))
                spread(t2[:, :], gn_t[:, :], HD, on["gn_wide"])

            def normed(t):
                e.wait_ge(on["gn_row"], count(t, 1, 1))
                tt(ys[:, :], ys[:, :], bank[7][:, :], ALU.mult).then_inc(on["gn_mul"], 1)

            def gate(t):
                e.wait_ge(on["gn_aff"], count(t, 1, 1))
                v(tt(ys[:, :], ys[:, :], flat(rk_v, t), ALU.add))
                stt(flat(rk_k, t), ys[:, :], 0.5, flat(rk_g, t), ALU.mult, ALU.mult).then_inc(on["gated"], 1)

            def both(t, before, following):
                for lv in range(LEVELS - 1):
                    level_q(t, lv)
                    if lv == 0 and before:
                        centre(before)
                    if following:
                        if lv == 0:
                            decays(following)
                        elif lv == 1:
                            keys(following)
                            kappa_rho(following)
                        elif lv == 2:
                            alpha_beta(following)
                        elif lv == 3:
                            bonus(following)
                    if before and lv == 3:
                        inverse_deviation(before)
                    elif before and lv == 4:
                        normed(before)
                    level_t(t, lv)
                last_q(t)
                if before:
                    gate(before)
                if following:
                    gram(following, 0)
                    gram(following, 1)
                last_t(t)
                for b in range(BT):
                    state(t, b, following)

            for part in (decays, keys, kappa_rho, alpha_beta, bonus):
                part((0, 0))
            for n in range(NG + 2):
                gram((0, 0), n)
            pairs((0, 0), 0)
            pairs((0, 0), 1)
            both((0, 0), None, (0, 1))
            with e.Fori(0, KT // 2 - 1) as i:
                v.loop(i, 2 * STEPS_V)
                both((i, 1), (i, 0), (i, 2))
                both((i, 2), (i, 1), (i, 3))
            v.end(KT // 2 - 1)
            both((0, KT - 1), (0, KT - 2), None)
            centre((0, KT - 1))

            def gated_lo(t):
                e.wait_ge(bhi_ready, KT + FG * KT + 2 * KT + t + 1)
                tt(b_lo[:, t, :], rk_k[:, t, :], b_hi[:, t, :].bitcast(F32), ALU.subtract).then_inc(blo_ready, 1)

            gated_lo(0)
            gated_lo(1)
            inverse_deviation((0, KT - 1))
            gated_lo(2)
            normed((0, KT - 1))
            gate((0, KT - 1))
            for t in range(3, KT):
                gated_lo(t)

            e.wait_ge(on["x_returned"], 16)
            for t in range(KT):
                e.wait_ge(job_done, J_RO + t + 1)
                tt(o_buf[:, t, :], x_back[:, t, :], bank[t % 2][:, :], ALU.add).then_inc(job_out, 1)

        @block.tensor
        def _(e):
            mm = e.matmul

            def job(j, s, hi, lo, ready=None, base=0, free=True):
                e.wait_ge(lo_ready, j + 1)
                if free:
                    e.wait_ge(job_out, j - 1)
                for k in range(KT):
                    if ready is not None:
                        e.wait_ge(ready, base + (k + 1))
                    wh, wl = w_hi[:, s, k * P:(k + 1) * P], w_lo[:, s, k * P:(k + 1) * P]
                    mm(bank[s][:, :], wh, hi[:, k, :], start=(k == 0), stop=False)
                    mm(bank[s][:, :], wh, lo[:, k, :], start=False, stop=False)
                    last = mm(bank[s][:, :], wl, hi[:, k, :], start=False, stop=(k == KT - 1))
                last.then_inc(job_done, 1)

            def jobs(first, count, hi, lo):
                with e.Fori(0, count // SLOTS) as i:
                    for s in range(SLOTS):
                        job(i * SLOTS + (first + s), s, hi, lo)

            def turned(n, src, done):
                for b in range(BT):
                    ins = e.transpose(bank[n][:, b * P:(b + 1) * P], src[:, b * P:(b + 1) * P], const("ident"))
                ins.then_inc(done, 1)

            def head_sums(n, col, src, done):
                for b in range(BT):
                    ins = mm(bank[n][:, col + 2 * b:col + 2 * b + 2], src[:, b * P:(b + 1) * P],
                             const("blk").rearrange("p (h f) -> p h f", h=2)[:, :, 0], start=True, stop=True,
                             skip_group_check=True)
                if done is not None:
                    ins.then_inc(done, 1)

            def spread_out(nth):
                e.wait_ge(wide_ready, nth + 1)
                turned(2, wide[:, :], row_done)

            def square_sum(k, nth, src, last=True):
                e.wait_ge(sq_ready, nth * KT + k + 1)
                for b in range(BT):
                    ins = mm(bank[2][:, b:b + 1], src[:, k, b * P:(b + 1) * P], const("ones"),
                             start=(k == 0 and b == 0), stop=(k == KT - 1), skip_group_check=True)
                if k == KT - 1:
                    ins.then_inc(ms_done, 1)
                    if last:
                        spread_out(nth)

            job(0, 0, a_hi, a_lo, alo_ready, 0, free=False)
            e.wait_ge(const_landed, 16)
            for k in range(KT):
                square_sum(k, 0, sc, last=False)
            job(1, 1, a_hi, a_lo, free=False)
            spread_out(0)
            jobs(2, J_OUT - 2, a_hi, a_lo)

            e.wait_ge(bd_landed, 16)
            e.wait_ge(job_out, J_OUT)
            e.wait_ge(on["sc_y"], 1)
            for i in range(2):
                mm(bank[i][:, :], const("mean"), sc[:, 8 + i, :], start=True, stop=True).then_inc(on["conf_mean"], 1)
            e.wait_ge(on["sc_y"], 2)
            for n in range(2):
                if n:
                    e.wait_ge(on["v_tok"], n)
                for b in range(BT):
                    ins = e.transpose(bank[6][:, b * P:(b + 1) * P], u[:, V0 + n, b * P:(b + 1) * P], const("ident"))
                ins.then_inc(on["v_tr"], 1)
            e.wait_ge(on["v_tok"], 2)

            def other_mixers(stage):
                if stage == 0:
                    for i in range(2):
                        e.wait_ge(on["conf_sq"], i + 1)
                        head_sums(2, 2 * BT * i, sc[:, 4 + i, :], on["conf_var"] if i else None)
                elif stage == 3:
                    for i in range(2):
                        e.wait_ge(on["conf_rs"], i + 1)
                        turned(i, sc[:, 6 + i, :], on["conf_row"])
                elif stage in (5, 7):
                    i = stage // 2 - 2
                    e.wait_ge(on["lru_xc"], i + 1)
                    e.wait_ge(on["conf_n"], 2)
                    if i:
                        e.wait_ge(on["lru_tr"], 2 * i)
                    mm(bank[0][:, :], bd[:, i, :], u[:, LX0 + i, :], start=True, stop=True)
                    mm(bank[1][:, :], bd[:, 2 + i, :], u[:, LX0 + i, :], start=True, stop=True)\
                        .then_inc(on["lru_mm"], 1)

            def scores(n):
                pair, qt, hh = HEADS[n]
                rows = slice(64 * hh, 64 * hh + 64)
                if n >= 2:
                    e.wait_ge(on["s_out"], n - 1)
                mm(bank[3 + n % 2][:, 0:(qt + 1) * P], u[rows, Q0 + pair, qt * P:(qt + 1) * P],
                   u[rows, K0 + pair, 0:(qt + 1) * P], start=True, stop=True).then_inc(on["qk_done"], 1)

            scores(0)
            for n, (pair, qt, hh) in enumerate(HEADS):
                if n + 1 < len(HEADS):
                    scores(n + 1)
                other_mixers(n)
                e.wait_ge(on["p_ready"], n + 1)
                if n >= 2:
                    e.wait_ge(on["p_tok"], n - 1)
                for b in range(qt + 1):
                    ins = e.transpose(bank[5 + n % 2][:, b * P:(b + 1) * P], u[:, 2 + n % 2, b * P:(b + 1) * P],
                                      const("ident"))
                ins.then_inc(on["p_tr"], 1)
                e.wait_ge(on["p_tok"], n + 1)
                if pair == 1 and qt == 0:
                    e.wait_ge(blo_ready, 5)
                head = 2 * pair + hh
                for b in range(qt + 1):
                    ins = mm(bank[7][64 * hh:64 * hh + 64, qt * P:(qt + 1) * P],
                             vtok[:, b, head * HD:(head + 1) * HD], u[:, V0 + n % 2, b * P:(b + 1) * P],
                             start=(b == 0), stop=(b == qt))
                ins.then_inc(on["pv_done"], 1)

            def jobs_with_norm(first, hi, lo, nth):
                for t in range(KT):
                    job(first + t, t % SLOTS, hi, lo)
                    if t:
                        square_sum(t - 1, nth, sq)
                square_sum(KT - 1, nth, sq)

            e.wait_ge(job_out, J_OUT)
            e.wait_ge(blo_ready, KT)
            jobs_with_norm(J_OUT, b_hi, b_lo, 1)

            e.wait_ge(job_out, J_MLP)
            job(J_MLP, 0, a_hi, a_lo, alo_ready, KT)
            for k in range(KT):
                square_sum(k, 2, sq, last=False)
            job(J_MLP + 1, 1, a_hi, a_lo)
            spread_out(2)
            jobs(J_MLP + 2, KT - 2, a_hi, a_lo)

            def down(grp, norm):
                first = grp * (2 * KT) + (J_MLP + KT)
                for t in range(KT):
                    if t == 0:
                        job(first + t, 0, b_hi, b_lo, blo_ready, grp * KT + KT)
                    else:
                        job(first + t, t % SLOTS, b_hi, b_lo)
                    if norm and t:
                        square_sum(t - 1, 3, sq)
                if norm:
                    square_sum(KT - 1, 3, sq)

            down(0, False)
            with e.Fori(1, FG - 1) as grp:
                for t in range(KT):
                    job(grp * (2 * KT) + (J_MLP + t), t % SLOTS, a_hi, a_lo)
                down(grp, False)
            jobs(J_MLP + (FG - 1) * 2 * KT, KT, a_hi, a_lo)
            down(FG - 1, True)

            e.wait_ge(job_out, J_RK)
            for k in range(KT):
                square_sum(k, 4, sq)
            for t in range(SLOTS):
                if t == 0:
                    job(J_RK, 0, a_hi, a_lo, alo_ready, 2 * KT)
                else:
                    job(J_RK + t, t, a_hi, a_lo)
            jobs(J_RK + 2, KT - 2, a_hi, a_lo)
            e.wait_ge(blo_ready, KT + FG * KT + KT)
            jobs(J_RR, KT, b_hi, b_lo)
            e.wait_ge(lora_landed, 16)
            e.wait_ge(alo_ready, 4 * KT)
            for k in range(KT):
                if k % 2 == 0:
                    job(J_RV + k // 2, k // 2 % SLOTS, a_hi, a_lo)
                for s in range(2):
                    e.wait_ge(on["xw_ready"], 2 * k + s + 1)
                    mm(bank[2 + s][64 * s:64 * s + 64, :], w_lor[:, k, 64 * s:64 * s + 64], mix[:, s, :], start=(k == 0),
                       stop=(k == KT - 1)).then_inc(on["lora_k"], 1)
            jobs(J_RV + KT // 2, KT // 2, a_hi, a_lo)
            e.wait_ge(blo_ready, KT + FG * KT + 2 * KT)
            e.wait_ge(job_out, J_RG)
            for t in range(KT):
                job(J_RG + t, t % SLOTS, b_hi, b_lo)
                if t:
                    e.wait_ge(on["kq_ready"], t)
                    head_sums(4, 2 * BT * (t - 1), key_sq[:, (t - 1) % 2, :], on["kq_done"])
            e.wait_ge(on["kq_ready"], KT)
            head_sums(4, 2 * BT * (KT - 1), key_sq[:, (KT - 1) % 2, :], on["kq_done"])

            e.wait_ge(job_out, J_RO)
            e.wait_ge(on["lora_out"], 2)

            def up(t):
                if t[1]:
                    e.wait_ge(on["gram_out"], count(t, NG + 2, 0))
                e.wait_ge(on["up_landed"], count(t, 16, 16))
                mm(bank[0][:, :], w_up[0:64, :], lora[0:64, :], start=True, stop=True)
                mm(bank[1][:, :], w_up[64:128, :], lora[64:128, :], start=True, stop=True).then_inc(on["up_done"], 1)

            def key_norms(t):
                e.wait_ge(on["kn_wide"], count(t, 1, 1))
                turned(2, wide[:, :], on["kn_done"])

            def values(t):
                e.wait_ge(on["vf_ready"], count(t, 1, 1))
                e.wait_ge(on["th_ready"], count(t, 2, 2))
                turned(0, wide[:, :], on["tr_done"])
                e.wait_ge(on["cut_ready"], count(t, 1, 1))
                mm(bank[1][:, :], const("blk"), t1[:, :], start=True, stop=True).then_inc(on["bk_done"], 1)

            def beta(t):
                e.wait_ge(on["f_ready"], count(t, 1, 1))
                turned(2, be[:, :, :].rearrange("p b t -> p (b t)"), on["tr_done"])

            def kappa(t):
                e.wait_ge(on["tr_out"], count(t, 3, 1))
                turned(0, ka[:, :, :].rearrange("p b t -> p (b t)"), on["tr_done"])

            def gram(t, n):
                ar, dst = ars[t[1] % 2], bank[(n + 1) % 3]
                if n == 0:
                    e.wait_ge(on["halves_ready"], count(t, 4, 5))
                    e.wait_ge(on["bonus_ready"], count(t, 1, 1))
                elif n < 3:
                    e.wait_ge(on["tr_out"], count(t, 3, n + 1))
                else:
                    e.wait_ge(on["gram_out"], count(t, NG + 2, n - 2))
                if n < NG:
                    b, hh = n // 2, n % 2
                    right = ar[:, b, :, :].rearrange("p c t -> p (c t)")
                    mm(dst[:, 0:2 * P], be_h[:, hh, b, :], right, start=True, stop=True)
                    ins = mm(dst[:, 2 * P:4 * P], ka_h[:, hh, b, :], right, start=True, stop=True)
                else:
                    for b in range(BT):
                        ins = mm(dst[:, b * P:(b + 1) * P], ar[:, b, 0, :], be_h[:, n - NG, b, :], start=True,
                                 stop=True)
                ins.then_inc(on["gram_done"], 1)

            def products(n, left, right, done):
                for g in range(left.shape[1]):
                    ins = mm(bank[n][:, g * P:(g + 1) * P], left[:, g, :], right[:, g, :], start=True,
                             stop=True)
                ins.then_inc(done, 1)

            def level_q(t, lv):
                for hh in range(2):
                    part = slice(BT * hh, BT * hh + BT)
                    if lv == 0:
                        e.wait_ge(on["tt_init"], count(t, 1, 1))
                    else:
                        e.wait_ge(on["tt_out"], count(t, 2 * LEVELS, 2 * lv - 2 + hh + 1))
                    products(BANKS_AT[lv][hh], a_full[t[1] % 2][:, part, :], grams[t[1] % 2][:, part, 0, :],
                             on["q_done"])

            def level_t(t, lv):
                q0, q1, t0, n0 = BANKS_AT[lv]
                if lv == 0:
                    e.wait_ge(on["tn_init"], count(t, 1, 1))
                for hh in range(2):
                    part = slice(BT * hh, BT * hh + BT)
                    if lv:
                        e.wait_ge(on["tn_out"], count(t, 2 * LEVELS - 2, 2 * lv - 2 + hh + 1))
                    e.wait_ge(on["q_out"], count(t, 2 * LEVELS, 2 * lv + hh + 1))
                    products((t0, q0)[hh], t_full[:, part, :], q_full[:, part, :], on["tt_done"])
                    if lv and hh == 0:
                        e.wait_ge(on["tn_out"], count(t, 2 * LEVELS - 2, 2 * lv))
                    products((n0, q1)[hh], q_full[:, part, :], t_full[:, part, :], on["tn_done"])

            def last_products(n, left, right, rows, hh, done):
                for b in range(BT):
                    dst = bank[n][:, b * P + 64:(b + 1) * P]
                    g = BT * hh + b
                    if b == 0:
                        mm(dst, left[rows, g, :], right[rows, g, HIGH], start=True, stop=True)
                    else:
                        ins = mm(dst[LOW, :], left[rows, g, LOW], right[rows, g, HIGH], start=True, stop=True)
                ins.then_inc(done, 1)

            def last_q(t):
                for hh in range(2):
                    e.wait_ge(on["tt_out"], count(t, 2 * LEVELS, 2 * LEVELS - 4 + hh + 1))
                    last_products(BANKS_AT[-1][hh], a_full[t[1] % 2], grams[t[1] % 2][:, :, 0, :], HIGH, hh, on["q_done"])

            def last_t(t):
                e.wait_ge(on["tn_out"], count(t, 2 * LEVELS - 2, 2 * LEVELS - 2))
                q0, q1, t0, n0 = BANKS_AT[-1]
                for hh in range(2):
                    e.wait_ge(on["q_out"], count(t, 2 * LEVELS, 2 * LEVELS - 2 + hh + 1))
                    last_products((t0, q0)[hh], t_full, q_full, LOW, hh, on["tt_done"])

            def state(t, b, following):
                s, part = t[1] % 2, slice(b * P, (b + 1) * P)
                g, ar, v_t = grams[s], ars[s], v_ts[s]
                e.wait_ge(on["st_out"], count(t, BT, b + 1))
                mm(bank[3][:, 0:P], ar[:, b, 0, :], s_t[:, :], start=True, stop=False, skip_group_check=True)
                for hh in range(2):
                    cols = slice(64 * hh, 64 * hh + 64)
                    ins = mm(bank[3][:, cols], g[:, BT * hh + b, 2, :], v_t[:, b, cols], start=False, stop=(hh == 1),
                             skip_group_check=True)
                ins.then_inc(on["r_done"], 1)
                if following and GRAMS_AT[b] < NG + 2:
                    gram(following, GRAMS_AT[b])
                e.wait_ge(on["r_out"], count(t, BT, b + 1))
                for hh in range(2):
                    cols = slice(64 * hh, 64 * hh + 64)
                    ins = mm(bank[5][:, cols], g[:, BT * hh + b, 0, :], r_s[:, cols], start=True, stop=True)
                ins.then_inc(on["u_done"], 1)
                if following:
                    for n in range(GRAMS_AT[b] + 1, GRAMS_AT[b + 1])[:1]:
                        gram(following, n)
                mm(bank[7][:, part], s_t[:, :], ar[:, b, 1, :], start=True, stop=False, skip_group_check=True)
                for hh in range(2):
                    cols = slice(64 * hh, 64 * hh + 64)
                    mm(bank[7][cols, part], v_t[:, b, cols], g[:, BT * hh + b, 3, :], start=False, stop=False,
                       skip_group_check=True)
                if b < BT - 1:
                    mm(bank[4][:, 0:P], ka_ts[s][:, b, :], v_t[:, b, :], start=True, stop=False)
                e.wait_ge(on["u_out"], count(t, BT, b + 1))
                if b < BT - 1:
                    mm(bank[4][:, 0:P], be_ts[s][:, b, :], u_s[:, :], start=False, stop=True).then_inc(on["st_done"], 1)
                for hh in range(2):
                    cols = slice(64 * hh, 64 * hh + 64)
                    ins = mm(bank[7][cols, part], u_s[:, cols], g[:, BT * hh + b, 1, :], start=False,
                             stop=(hh == 1), skip_group_check=True)
                ins.then_inc(on["y_part"], 1)
                if following:
                    for n in range(GRAMS_AT[b] + 2, GRAMS_AT[b + 1]):
                        gram(following, n)

            def centre(t):
                e.wait_ge(on["y_out"], count(t, 1, 1))
                mm(bank[7][:, :], const("mean"), ys[:, :], start=True, stop=True).then_inc(on["ym_done"], 1)

            def variance(t):
                e.wait_ge(on["yq_ready"], count(t, 1, 1))
                head_sums(7, 0, t2[:, :], on["vn_done"])

            def deviations(t):
                e.wait_ge(on["gn_wide"], count(t, 1, 1))
                turned(7, t2[:, :], on["gn_row"])

            def both(t, before, following):
                for lv in range(LEVELS - 1):
                    level_q(t, lv)
                    if lv == 0 and before:
                        centre(before)
                    if following:
                        if lv == 0:
                            up(following)
                        elif lv == 1:
                            key_norms(following)
                        elif lv == 2:
                            values(following)
                        elif lv == 3:
                            beta(following)
                        elif lv == 4:
                            kappa(following)
                    if lv == 2 and before:
                        variance(before)
                    elif lv == 4 and before:
                        deviations(before)
                    level_t(t, lv)
                last_q(t)
                if following:
                    gram(following, 0)
                    gram(following, 1)
                last_t(t)
                e.wait_ge(on["tt_out"], count(t, 2 * LEVELS, 2 * LEVELS))
                if before:
                    e.wait_ge(on["gn_mul"], count(before, 1, 1))
                for b in range(BT):
                    state(t, b, following)

            for part in (up, key_norms, values, beta, kappa):
                part((0, 0))
            for n in range(NG + 2):
                gram((0, 0), n)
            both((0, 0), None, (0, 1))
            with e.Fori(0, KT // 2 - 1) as i:
                both((i, 1), (i, 0), (i, 2))
                both((i, 2), (i, 1), (i, 3))
            both((0, KT - 1), (0, KT - 2), None)
            centre((0, KT - 1))
            variance((0, KT - 1))
            deviations((0, KT - 1))
            job(J_RO, 0, b_hi, b_lo, blo_ready, KT + FG * KT + 2 * KT)
            job(J_RO + 1, 1, b_hi, b_lo)
            jobs(J_RO + 2, KT - 2, b_hi, b_lo)


_OUT = "out_0_dram"


def kernel(**inputs):
    import concourse.bacc as bacc
    from concourse.bass_utils import run_bass_kernel_spmd

    def arr(name):
        return np.asarray(inputs[name])

    def blocks_of(w):
        k, n = w.shape
        return w.reshape(k // P, P, n // P, P).transpose(2, 1, 0, 3).reshape(n // P, P, k)

    w1, w2 = blocks_of(arr("mlp_w1")[0]), arr("mlp_w2")[0]
    rw_in = arr("l0_w_in_2")
    jobs = [blocks_of(arr("w_in")[0])[W_IN_ORDER], blocks_of(arr("w_out")[0])]
    for g in range(FG):
        jobs += [w1[g * KT:(g + 1) * KT], blocks_of(w2[g * D:(g + 1) * D])]
    for c in (1, 0, 2, 3):
        jobs.append(blocks_of(rw_in[:, c * D:(c + 1) * D]))
    jobs.append(blocks_of(arr("l0_w_out_2")))
    wall = np.concatenate(jobs)

    w_lora = rw_in[:, 4 * D:4 * D + P].reshape(KT, P, P).transpose(1, 0, 2)
    lora_up = np.concatenate([arr("l0_w_up_2"), arr("l0_a_up_2")]).reshape(P, KT, P).transpose(1, 0, 2)
    bd = np.zeros((4, P, P), np.float32)
    for n, name in enumerate(("lru_wa", "lru_wx")):
        for b in range(4):
            at = slice(64 * (b % 2), 64 * (b % 2) + 64)
            bd[2 * n + b // 2, at, at] = arr(name)[0, b]

    def cols(v):
        return v.reshape(-1, P).T

    def taps(w):
        return w.reshape(w.shape[0], 2, P).transpose(2, 1, 0).reshape(P, -1)

    rw = np.stack([cols(arr(n).reshape(-1)) for n in (
        "l0_w0_2", "l0_a0_2", "l0_k_k_2", "l0_k_a_2", "l0_r_k_2", "l0_gn_w_2", "l0_gn_b_2", "l0_k_a_2")], 2)
    parts = {
        "pre_mix_g": cols(arr("pre_mix_g")), "post_mix_g": cols(arr("post_mix_g")),
        "pre_mlp_g": cols(arr("pre_mlp_g")), "post_mlp_g": cols(arr("post_mlp_g")),
        "l0_norm": cols(arr("l0_norm_2")), "mu": cols(arr("l0_mu_2")), "conf_w": taps(arr("conf_dw_w")[0]),
        "conf_b": cols(arr("conf_dw_b")), "gn_g": cols(arr("conf_gn_g")), "gn_b": cols(arr("conf_gn_b")),
        "sconv_w": taps(arr("sconv_w")[0]), "lru_w": taps(arr("lru_conv_w")[0]), "lru_b": cols(arr("lru_conv_b")),
        "lru_ba": cols(arr("lru_ba")), "lru_bx": cols(arr("lru_bx")), "lam": cols(arr("lru_lam")),
        "rw": rw.reshape(P, 64),
    }
    arrays = {
        "xT": arr("x").reshape(T, D).T.reshape(KT, P, T), "wall": wall, "w_lora": w_lora, "lora_up": lora_up,
        "lru_bd": bd, "par": np.concatenate([parts[n] for n, _ in PARAMS], 1), "const_in": constants(),
    }
    nc = bacc.Bacc("TRN2", target_bir_lowering=False, num_devices=1)
    args, fed = {}, {}
    for name, a in arrays.items():
        a = np.ascontiguousarray(a)
        fed[f"in_{name}"] = a
        args[name] = nc.dram_tensor(f"in_{name}", a.shape, F32, kind="ExternalInput").ap()
    args["x_spill"] = nc.dram_tensor("x_spill", (KT, P, T), F32, kind="Internal").ap()
    args["out"] = nc.dram_tensor(_OUT, (KT, P, T), F32, kind="ExternalOutput").ap()
    build_program(nc, **args)
    r = run_bass_kernel_spmd(nc, [fed], core_ids=[0])
    return np.ascontiguousarray(r.results[0][_OUT].reshape(D, T).T).reshape(1, T, D)
```
